# Optimizing a Trainium2 kernel written in Bass

```python
import math
import jax, jax.numpy as jnp
from jax import lax
import numpy as np

D_MODEL = 1024
BATCH = 1
SEQ = 256
DEPTH = 2

CHUNK = 64
Q_BLOCK = 128
HEAD_DIM = 64
ROPE_THETA = 10000.0
EPS = 1e-6
MAX_POS_OFFSET = 4096
A_HEADS = 8
A_KV_LORA = 256
IDX_HEADS = 4
IDX_DIM = 64
TOPK_MAX = 256
B_HEADS = 8
C_HEADS = 8
C_V_DIM = 128
A_WIDTH = A_HEADS * HEAD_DIM
B_WIDTH = B_HEADS * HEAD_DIM
C_QK_WIDTH = C_HEADS * HEAD_DIM
C_WIDTH = C_HEADS * C_V_DIM
N_BRANCH = 3
IN_SIZES = (A_WIDTH, A_KV_LORA, IDX_HEADS * IDX_DIM, IDX_DIM, IDX_HEADS,
            B_WIDTH, B_WIDTH, B_WIDTH,
            C_QK_WIDTH, C_QK_WIDTH, C_WIDTH, C_WIDTH,
            N_BRANCH * D_MODEL)
N_IN = sum(IN_SIZES)
N_EXPERTS = 64
TOP_K = 8
N_GROUPS = 8
TOPK_GROUPS = 4
EXPERT_DIM = 256
SHARED_DIM = 256
ROUTED_SCALE = 2.5
MOE_BLOCK = 128
N_ADA = 6

kernel_name = "chunk_causal_hybrid_dsa_stickbreak_retention_moe"

def rms_norm(x, g):
    xf = x.astype(jnp.float32)
    y = xf * lax.rsqrt(jnp.mean(xf * xf, axis=-1, keepdims=True) + EPS)
    return (y * g.astype(jnp.float32)).astype(x.dtype)

def rope(x, positions):
    half = x.shape[-1] // 2
    inv_freq = ROPE_THETA ** (-jnp.arange(half, dtype=jnp.float32) / half)
    ang = positions.astype(jnp.float32)[:, :, None, None] * inv_freq
    cos, sin = jnp.cos(ang), jnp.sin(ang)
    xf = x.astype(jnp.float32)
    x1, x2 = xf[..., :half], xf[..., half:]
    return jnp.concatenate([x1 * cos - x2 * sin, x2 * cos + x1 * sin], axis=-1).astype(x.dtype)

def dsa_mixer(q, c_kv, iq, ik, iw, g_kv, w_uk, w_uv, positions):
    b, s, h, d = q.shape
    topk = min(TOPK_MAX, s // 4)
    c_kv = rms_norm(c_kv, g_kv)
    k = rope((c_kv @ w_uk)[:, :, None, :], positions)[:, :, 0]
    v = c_kv @ w_uv
    q = rope(q, positions)
    iq = rope(iq, positions).astype(jnp.float32)
    ik = rope(ik[:, :, None, :], positions)[:, :, 0].astype(jnp.float32)
    iw = iw.astype(jnp.float32) * IDX_HEADS ** -0.5
    key_chunk = jnp.arange(s) // CHUNK

    def block(i):
        t0 = i * Q_BLOCK
        qb = lax.dynamic_slice_in_dim(q, t0, Q_BLOCK, axis=1)
        iqb = lax.dynamic_slice_in_dim(iq, t0, Q_BLOCK, axis=1)
        iwb = lax.dynamic_slice_in_dim(iw, t0, Q_BLOCK, axis=1)
        q_chunk = (t0 + jnp.arange(Q_BLOCK)) // CHUNK
        admissible = key_chunk[None, :] <= q_chunk[:, None]
        logits = jnp.einsum('bthd,bsd->bths', iqb, ik) * IDX_DIM ** -0.5
        score = jnp.einsum('bth,bths->bts', iwb, jax.nn.relu(logits))
        score = jnp.where(admissible[None], score, -jnp.inf)
        _, idx = lax.top_k(score, topk)
        valid = key_chunk[idx] <= q_chunk[None, :, None]
        k_sel = jax.vmap(lambda kb, ib: kb[ib])(k, idx)
        v_sel = jax.vmap(lambda vb, ib: vb[ib])(v, idx)
        sc = jnp.einsum('bthd,btkd->bhtk', qb, k_sel).astype(jnp.float32) * d ** -0.5
        sc = jnp.where(valid[:, None], sc, -jnp.inf)
        p = jax.nn.softmax(sc, axis=-1).astype(v.dtype)
        return jnp.einsum('bhtk,btkd->bthd', p, v_sel)

    out = lax.map(block, jnp.arange(s // Q_BLOCK))
    return jnp.moveaxis(out, 0, 1).reshape(b, s, h * d)

def stick_breaking_mixer(q, k, v):
    b, s, h, d = q.shape
    key_pos = jnp.arange(s)

    def block(i):
        t0 = i * Q_BLOCK
        qb = lax.dynamic_slice_in_dim(q, t0, Q_BLOCK, axis=1)
        z = jnp.einsum('bthd,bshd->bhts', qb, k).astype(jnp.float32) * d ** -0.5
        causal = key_pos[None, :] < (t0 + jnp.arange(Q_BLOCK))[:, None]
        log_beta = jax.nn.log_sigmoid(z)
        log_not = jnp.where(causal, jax.nn.log_sigmoid(-z), 0.0)
        tail = lax.cumsum(log_not, axis=3, reverse=True) - log_not
        a = jnp.where(causal, jnp.exp(log_beta + tail), 0.0)
        return jnp.einsum('bhts,bshd->bthd', a.astype(v.dtype), v)

    out = lax.map(block, jnp.arange(s // Q_BLOCK))
    return jnp.moveaxis(out, 0, 1).reshape(b, s, h * d)

def head_group_norm(o, g):
    b, s, h, dv = o.shape
    of = o.astype(jnp.float32)
    mu = jnp.mean(of, axis=-1, keepdims=True)
    var = jnp.mean(jnp.square(of - mu), axis=-1, keepdims=True)
    y = ((of - mu) * lax.rsqrt(var + EPS)).reshape(b, s, h * dv)
    return y * g.astype(jnp.float32)

def retention_mixer(q, k, v, gate, g_ret, positions):
    b, s, h, dk = q.shape
    dv = v.shape[-1]
    n = s // CHUNK
    log_g = jnp.log(1.0 - 2.0 ** (-5.0 - jnp.arange(h, dtype=jnp.float32)))
    q = rope(q, positions)
    k = rope(k, positions) * dk ** -0.5
    qc = q.reshape(b, n, CHUNK, h, dk)
    kc = k.reshape(b, n, CHUNK, h, dk)
    vc = v.reshape(b, n, CHUNK, h, dv)
    pos = jnp.arange(CHUNK, dtype=jnp.float32)
    decay_in = jnp.exp(log_g[:, None, None] * jnp.abs(pos[:, None] - pos[None, :]))
    sc = jnp.einsum('bnahd,bnchd->bnhac', qc, kc) * decay_in
    intra = jnp.einsum('bnhac,bnche->bnahe', sc, vc)
    zeta = jnp.exp(log_g[:, None] * (CHUNK - 1 - pos))
    kv = jnp.einsum('bnchd,hc,bnche->bnhde', kc, zeta, vc)
    g_chunk = jnp.exp(log_g * CHUNK)[None, :, None, None]

    def step(state, kv_i):
        return state * g_chunk + kv_i, state

    _, prev = lax.scan(step, jnp.zeros_like(kv[:, 0]), jnp.moveaxis(kv, 1, 0))
    prev = jnp.moveaxis(prev, 0, 1)
    xi = jnp.exp(log_g[:, None] * (pos + 1.0))
    cross = jnp.einsum('bnahd,bnhde,ha->bnahe', qc, prev, xi)
    o = (intra + cross).reshape(b, s, h, dv)
    o = head_group_norm(o, g_ret).astype(gate.dtype)
    return jax.nn.silu(gate.reshape(b, s, h * dv)) * o

def mixing_sublayer(h, positions, w_in, g_kv, w_uk, w_uv, g_ret, w_o_a, w_o_b, w_o_c, w_out):
    b, s, d_model = h.shape
    split_points = [int(p) for p in np.cumsum(IN_SIZES)[:-1]]
    z = h @ w_in
    (qa, ckv, iq, ik, iw, qb, kb, vb, qc, kc, vc, gc, gates) = jnp.split(z, split_points, axis=-1)
    ya = dsa_mixer(qa.reshape(b, s, A_HEADS, HEAD_DIM), ckv,
                   iq.reshape(b, s, IDX_HEADS, IDX_DIM), ik, iw, g_kv, w_uk, w_uv, positions) @ w_o_a
    yb = stick_breaking_mixer(qb.reshape(b, s, B_HEADS, HEAD_DIM), kb.reshape(b, s, B_HEADS, HEAD_DIM),
                              vb.reshape(b, s, B_HEADS, HEAD_DIM)) @ w_o_b
    yc = retention_mixer(qc.reshape(b, s, C_HEADS, HEAD_DIM), kc.reshape(b, s, C_HEADS, HEAD_DIM),
                         vc.reshape(b, s, C_HEADS, C_V_DIM), gc.reshape(b, s, C_HEADS, C_V_DIM),
                         g_ret, positions) @ w_o_c
    g = jax.nn.sigmoid(gates.astype(jnp.float32)).astype(h.dtype).reshape(b, s, N_BRANCH, d_model)
    merged = g[:, :, 0] * ya + g[:, :, 1] * yb + g[:, :, 2] * yc
    return merged @ w_out

def moe_sublayer(h, w_router, router_bias, w1, w3, w2, ws1, ws3, ws2):
    b, s, d_model = h.shape
    x = h.reshape(-1, d_model)
    t = x.shape[0]
    scores = jax.nn.sigmoid((x @ w_router).astype(jnp.float32))
    sel = scores + router_bias.astype(jnp.float32)
    grp_score = lax.top_k(sel.reshape(t, N_GROUPS, N_EXPERTS // N_GROUPS), 2)[0].sum(-1)
    _, top_groups = lax.top_k(grp_score, TOPK_GROUPS)
    gmask = jnp.any(top_groups[:, :, None] == jnp.arange(N_GROUPS)[None, None, :], axis=1)
    sel = jnp.where(jnp.repeat(gmask, N_EXPERTS // N_GROUPS, axis=1), sel, -jnp.inf)
    _, eidx = lax.top_k(sel, TOP_K)
    wts = jnp.take_along_axis(scores, eidx, axis=1)
    wts = wts / jnp.sum(wts, axis=-1, keepdims=True) * ROUTED_SCALE
    n_assign = t * TOP_K
    flat_e = eidx.reshape(-1)
    flat_tok = jnp.repeat(jnp.arange(t, dtype=jnp.int32), TOP_K)
    order = jnp.argsort(flat_e)
    se, stok, sw = flat_e[order], flat_tok[order], wts.reshape(-1)[order]
    counts = jnp.zeros((N_EXPERTS,), jnp.int32).at[flat_e].add(1)
    starts = jnp.cumsum(counts) - counts
    padded = (counts + MOE_BLOCK - 1) // MOE_BLOCK * MOE_BLOCK
    pad_ends = jnp.cumsum(padded)
    pad_starts = pad_ends - padded
    dest = pad_starts[se] + (jnp.arange(n_assign, dtype=jnp.int32) - starts[se])
    n_blocks = (n_assign + N_EXPERTS * (MOE_BLOCK - 1) + MOE_BLOCK - 1) // MOE_BLOCK
    n_rows = n_blocks * MOE_BLOCK
    row_tok = jnp.full((n_rows,), t, jnp.int32).at[dest].set(stok)
    row_w = jnp.zeros((n_rows,), jnp.float32).at[dest].set(sw)
    block_e = jnp.minimum(jnp.searchsorted(pad_ends, jnp.arange(n_blocks) * MOE_BLOCK, side='right'),
                          N_EXPERTS - 1)
    x_pad = jnp.concatenate([x, jnp.zeros((1, d_model), x.dtype)], axis=0)

    def run_block(args):
        tok, wt, e = args
        xb = x_pad[tok]
        hid = jax.nn.silu(xb @ w1[e]) * (xb @ w3[e])
        return (hid @ w2[e]) * wt[:, None].astype(x.dtype)

    out = lax.map(run_block, (row_tok.reshape(n_blocks, MOE_BLOCK), row_w.reshape(n_blocks, MOE_BLOCK), block_e))
    routed = jax.ops.segment_sum(out.reshape(n_rows, d_model), row_tok, num_segments=t + 1)[:t]
    shared = (jax.nn.silu(x @ ws1) * (x @ ws3)) @ ws2
    return (routed + shared).reshape(b, s, d_model)

def setup_inputs(seed: int = 0) -> dict:
    key = jax.random.key(seed)
    ks = jax.random.split(key, 32)
    f32 = jnp.float32
    nrm = lambda k, shape, fan_in: jax.random.normal(k, shape, f32) * fan_in ** -0.5
    gain = lambda k, shape: 1.0 + 0.05 * jax.random.normal(k, shape, f32)
    offsets = jax.random.randint(ks[2], (BATCH, 1), 0, MAX_POS_OFFSET, dtype=jnp.int32)
    return {
        "x": jax.random.normal(ks[0], (BATCH, SEQ, D_MODEL), f32),
        "c": jax.random.normal(ks[1], (BATCH, D_MODEL), f32),
        "positions": offsets + jnp.arange(SEQ, dtype=jnp.int32)[None, :],
        "ada_w": nrm(ks[3], (DEPTH, D_MODEL, N_ADA * D_MODEL), D_MODEL) * 0.5,
        "ada_b": 0.02 * jax.random.normal(ks[4], (DEPTH, N_ADA * D_MODEL), f32),
        "g_pre_mix": gain(ks[5], (DEPTH, D_MODEL)),
        "g_post_mix": gain(ks[6], (DEPTH, D_MODEL)),
        "g_pre_ffn": gain(ks[7], (DEPTH, D_MODEL)),
        "g_post_ffn": gain(ks[8], (DEPTH, D_MODEL)),
        "w_in": nrm(ks[9], (DEPTH, D_MODEL, N_IN), D_MODEL),
        "g_kv": gain(ks[10], (DEPTH, A_KV_LORA)),
        "w_uk": nrm(ks[11], (DEPTH, A_KV_LORA, HEAD_DIM), A_KV_LORA),
        "w_uv": nrm(ks[12], (DEPTH, A_KV_LORA, HEAD_DIM), A_KV_LORA),
        "g_ret": gain(ks[13], (DEPTH, C_WIDTH)),
        "w_o_a": nrm(ks[14], (DEPTH, A_WIDTH, D_MODEL), A_WIDTH),
        "w_o_b": nrm(ks[15], (DEPTH, B_WIDTH, D_MODEL), B_WIDTH),
        "w_o_c": nrm(ks[16], (DEPTH, C_WIDTH, D_MODEL), C_WIDTH),
        "w_out": nrm(ks[17], (DEPTH, D_MODEL, D_MODEL), D_MODEL),
        "w_router": nrm(ks[18], (DEPTH, D_MODEL, N_EXPERTS), D_MODEL),
        "router_bias": 0.01 * jax.random.normal(ks[19], (DEPTH, N_EXPERTS), f32),
        "w1": nrm(ks[20], (DEPTH, N_EXPERTS, D_MODEL, EXPERT_DIM), D_MODEL),
        "w3": nrm(ks[21], (DEPTH, N_EXPERTS, D_MODEL, EXPERT_DIM), D_MODEL),
        "w2": nrm(ks[22], (DEPTH, N_EXPERTS, EXPERT_DIM, D_MODEL), EXPERT_DIM),
        "ws1": nrm(ks[23], (DEPTH, D_MODEL, SHARED_DIM), D_MODEL),
        "ws3": nrm(ks[24], (DEPTH, D_MODEL, SHARED_DIM), D_MODEL),
        "ws2": nrm(ks[25], (DEPTH, SHARED_DIM, D_MODEL), SHARED_DIM),
    }

def reference(x, c, positions, ada_w, ada_b, g_pre_mix, g_post_mix, g_pre_ffn, g_post_ffn,
              w_in, g_kv, w_uk, w_uv, g_ret, w_o_a, w_o_b, w_o_c, w_out,
              w_router, router_bias, w1, w3, w2, ws1, ws3, ws2):
    for l in range(DEPTH):
        mod = (jax.nn.silu(c) @ ada_w[l] + ada_b[l])[:, None, :]
        sh1, sc1, gt1, sh2, sc2, gt2 = jnp.split(mod, N_ADA, axis=-1)
        h = rms_norm(x, g_pre_mix[l]) * (1.0 + sc1) + sh1
        y = mixing_sublayer(h, positions, w_in[l], g_kv[l], w_uk[l], w_uv[l], g_ret[l],
                            w_o_a[l], w_o_b[l], w_o_c[l], w_out[l])
        x = x + gt1 * rms_norm(y, g_post_mix[l])
        h = rms_norm(x, g_pre_ffn[l]) * (1.0 + sc2) + sh2
        y = moe_sublayer(h, w_router[l], router_bias[l], w1[l], w3[l], w2[l], ws1[l], ws3[l], ws2[l])
        x = x + gt2 * rms_norm(y, g_post_ffn[l])
    return x


_drawn_inputs = setup_inputs


def setup_inputs(seed=0):
    import zlib

    import numpy as np

    out = dict(_drawn_inputs(seed))
    spreads = {}
    factors = {}
    for name, (base, spread) in spreads.items():
        noise = np.random.default_rng([zlib.crc32(name.encode()), seed]).standard_normal(out[name].shape)
        drawn = base * np.exp(spread * noise) if base else spread * noise
        out[name] = __import__('jax').numpy.asarray(drawn.astype(out[name].dtype))
    for name, factor in factors.items():
        out[name] = (out[name] * factor).astype(out[name].dtype)
    return out
```

```python
from contextlib import ExitStack

import concourse.bass as bass
import numpy as np
from concourse import mybir

F32 = mybir.dt.float32
I32 = mybir.dt.int32
ALU = mybir.AluOpType
ACT = mybir.ActivationFunctionType
AX = mybir.AxisListType.X

P = 128
D = 1024
SEQ = 256
DEPTH = 2
TT = SEQ // P
KD = D // P
EPS = 1e-6
HD = 64
NH = 8
KVL = 256
IDXH = 4
TOPK = 64
CHUNK = 64
CV = 128
NE = 64
NG = 8
EG = NE // NG
TOPG = 4
ED = 256
ROUTED_SCALE = 2.5
BIG = 1e30
GONE = -3e38
GONE_T = -2e38
TRI = SEQ + P

IN = dict(qa=0, ckv=512, iq=768, ik=1024, iw=1088, qb=1092, kb=1604, vb=2116, qc=2628, kc=3140, vc=3652,
          gc=4676, gates=5700)

NS = 3
CHUNKS = ([("ada", n) for n in range(12)]
          + [("in", IN["ckv"], 256), ("in", IN["iq"], 324), ("in", IN["qa"], 512), ("in", IN["qb"], 512),
             ("in", IN["kb"], 512), ("in", IN["vb"], 512), ("in", IN["qc"], 512), ("in", IN["kc"], 512),
             ("in", IN["vc"], 512), ("in", IN["vc"] + 512, 512), ("in", IN["gc"], 512), ("in", IN["gc"] + 512, 512)]
          + [("in", IN["gates"] + 512 * n, 512) for n in range(6)]
          + [("oab", 0), ("oc", 0), ("oab", 1), ("oc", 1), ("out", 0), ("out", 1)])
NCH = len(CHUNKS)
assert NCH % NS == 0

NB = 8
PAIRS = NH // 2


def plan_units():
    u = []
    for g in range(7):
        if g < 6:
            u += [("ada", 2 * g), ("ada", 2 * g + 1)]
        if g >= 1:
            n = 2 * (g - 1)
            u += [("gt", n), ("gt", n + 1)] if n in (4, 10) else [("mod", n)]
    u += [("xT", m) for m in range(4)]
    u += [("ckv",), ("iq",), ("ik",), ("iw",), ("qa", 0), ("qa", 1), ("ckvT",), ("kv",)]
    u += [("lg", i, h) for i in range(TT) for h in range(IDXH)]
    u += [("qb", 0), ("qb", 1), ("kb", 0), ("kb", 1), ("vb", 0), ("vb", 1)]
    u += [("qc", 0), ("qc", 1), ("kc", 0), ("kc", 1)]
    for n in range(NH + 2):
        if n < NH:
            u += [("z", n)]
        if 1 <= n < NH + 1:
            u += [("cum", n - 1)]
        if n >= 3 and n % 2 == 1:
            u += [("ob", (n - 3) // 2)]
        if n < 4:
            u += [("vc", n)]
        elif n < 8:
            u += [("gc", n - 4)]
    for n in range(2 * NH + 3):
        if n < 2 * NH:
            u += [("sc", n)]
        if 2 <= n < 2 * NH + 2:
            u += [("pT", n - 2)]
        if n >= 4 and n % 2 == 0:
            u += [("oa", (n - 4) // 2)]
        if n < 12:
            u += [("gate", n)]
    for n in range(NH + 1):
        if n < NH:
            u += [("ret", n)]
        if n >= 1:
            u += [("oc", n - 1)]
    u += [("ocT", m) for m in range(4)]
    for j in range(KD):
        u += [("yab", j), ("yc", j)]
    u += [("y", h, i) for h in range(2) for i in range(TT)]
    u += [("hT", m) for m in range(4)]
    u += [("rt",)]
    return u


UNITS = plan_units()
UNIT = {name: n for n, name in enumerate(UNITS)}
NU = len(UNITS)
USES = [len(range(b, NU, NB)) for b in range(NB)]
NEX = NE + 1
NW = 4

TOTAL = dict(
    bank_full=NU, chunk_used=len(CHUNKS), layer_done=1, params=16 * 13, decay=32,
    ada_copied=12, mod_done=8, ms_ready=6, rsq_raw=6, rms_ready=2, xn_ready=4, hT_ready=8,
    ckv_copied=1, ckv_scaled=1, ckvT_ready=1, vA_ready=1, rope_mul=9, roped=9, iw_ready=1, relu_ready=8, lg_used=8,
    sel_ready=2, qkb_ready=4, vb_ready=2, vc_ready=4, gc_ready=4, gate_ready=12,
    zs_ready=8, ln_ready=8, zb_ready=8, sp_ready=8, w_ready=8, a_ready=8, ob_ready=4,
    sm_ready=16, p_ready=16, rinv_ready=16, pn_ready=16, pTs_ready=16, oa_ready=8,
    rw_ready=8, osb_ready=8, ocn_ready=2, ocg_ready=2, ocT_ready=4,
    tab_ready=8, tc_ready=8, mT_ready=8, y_ready=4, dx_ready=4, x_ready=4,
    scores_ready=1, gates_ready=1,
    h_ready=2 * NEX, silu_ready=2 * NEX, hid_ready=2 * NEX, eT_ready=NEX, eTs_ready=NEX, w2_used=NEX, w13_used=NEX,
    yacc_ready=1, y2_ready=4,
    vector_chain=272, scalar_chain=127, gpsimd_chain=8,
)


def mixer_constants():
    half = HD // 2
    inv = np.float32(10000.0) ** (-np.arange(half, dtype=np.float32) / np.float32(half))
    p = np.arange(P)
    col = np.zeros((P, 4), np.float32)
    col[:, 0] = inv.astype(np.float32)[p % half]
    col[:, 1] = np.where(p % HD < half, -1.0, 1.0)
    ident = np.eye(P, dtype=np.float32)
    later = (p[:, None] >= p[None, :]).astype(np.float32)
    t = np.arange(SEQ)
    key0, key1 = p[:, None], p[:, None] + P
    causal = np.concatenate([key0 < t[None, :], key1 < t[None, P:]], 1)
    causal_neg = np.where(causal, 0.0, -BIG)
    adm = np.zeros((P, TT, SEQ), np.float32)
    for i in range(TT):
        adm[:, i, :] = np.where(t[None, :] // CHUNK <= (p[:, None] + i * P) // CHUNK, 0.0, -BIG)
    dec = np.zeros((P, NH, TRI), np.float64)
    for h in range(NH):
        lg = np.log(1.0 - 2.0 ** (-5.0 - h))
        for keys, q, c0 in ((p, t, 0), (p + P, t[P:], SEQ)):
            k, a = keys[:, None], q[None, :]
            inner = np.exp(lg * np.abs(k - a))
            cross = np.exp(lg * ((a % CHUNK + 1) + CHUNK * (a // CHUNK - k // CHUNK - 1) + (CHUNK - 1 - k % CHUNK)))
            w = np.where(k // CHUNK == a // CHUNK, inner, np.where(k // CHUNK < a // CHUNK, cross, 0.0))
            dec[:, h, c0:c0 + len(q)] = w * HD ** -0.5
    fixed = np.concatenate([ident, later, col, causal, causal_neg, adm.reshape(P, -1)], 1).astype(np.float32)
    return np.ascontiguousarray(fixed), np.ascontiguousarray(dec.reshape(P, -1).astype(np.float32))


def build(nc, x, c, positions, ada_w, ada_b, g_pre_mix, g_post_mix, g_pre_ffn, g_post_ffn, w_in, g_kv, w_uk, w_uv,
          g_ret, w_o_a, w_o_b, w_o_c, w_out, w_router, router_bias, w1, w3, w2, ws1, ws3, ws2, fixed, decay, out,
          depth=DEPTH, dbg=None):
    ctx = ExitStack()
    with ctx:
        def sb(name, shape, dt=F32):
            return ctx.enter_context(nc.sbuf_tensor(name, shape, dt))

        def sem(name):
            return ctx.enter_context(nc.semaphore(name))

        M = sb("M", [P, 24576])
        wring = M[:, 0:NS * 4096].rearrange("p (s k n) -> p s k n", s=NS, k=KD)
        gT = M[:, 12288:18432].rearrange("p (b t) -> p b t", b=24)
        dec = M[:, 18432:21504].rearrange("p (h t) -> p h t", h=NH)
        qcT = M[:, 21504:22528].rearrange("p (b t) -> p b t", b=4)
        kcT = M[:, 22528:23552].rearrange("p (b t) -> p b t", b=4)
        vb_s = M[:, 23552:24576].rearrange("p (i n) -> p i n", i=TT)
        w13 = M[:, 0:NW * 4096].rearrange("p (s j k n) -> p s j k n", s=NW, j=2, k=KD)
        w2s = M[:, 16384:24576].rearrange("p (s j n) -> p s j n", s=NW, j=2)
        x_sb = sb("x_sb", [P, TT, D])
        hT = sb("hT", [P, KD, SEQ])
        rows = sb("rows", [P, TT, D])
        fix = sb("fix", [P, 260 + 2 * TRI + TT * SEQ])
        ident, later = fix[:, 0:128], fix[:, 128:256]
        invf, rsign = fix[:, 256:257], fix[:, 257:258]
        cm01, cmneg = fix[:, 260:260 + TRI], fix[:, 260 + TRI:260 + 2 * TRI]
        adm = fix[:, 260 + 2 * TRI:].rearrange("p (i t) -> p i t", i=TT)
        ones = sb("ones", [P, P])
        zeros = sb("zeros", [1, P])
        ones32 = sb("ones32", [P, P])
        cosT = sb("cosT", [P, SEQ])
        sinT = sb("sinT", [P, SEQ])
        c_col = sb("c_col", [P, KD])
        c_rep = sb("c_rep", [P, KD, 32])
        gtg = sb("gtg", [P, 2, D])
        modc = sb("modc", [P, 4, KD])
        gpre = sb("gpre", [P, 2, KD])
        adabc = sb("adabc", [P, 4, KD])
        gkv_c = sb("gkv_c", [P, 2])
        gret_c = sb("gret_c", [P, KD])
        rbias = sb("rbias", [P, NE])
        wuk = sb("wuk", [P, 2, HD])
        wuv = sb("wuv", [P, 2, HD])
        wrt = sb("wrt", [P, KD, NE])
        ms, rs0, rs, rt1 = (sb(f"norm_{n}", [P, 16]) for n in ("ms", "raw", "r", "t"))
        part = sb("part", [P, 4])
        qbT = sb("qbT", [P, 4, SEQ])
        kbT = sb("kbT", [P, 4, SEQ])
        qaT = sb("qaT", [P, 4, SEQ])
        vc_s = sb("vc_s", [P, TT, D])
        gcs = sb("gcs", [P, TT, D])
        oaT = sb("oaT", [P, 4, SEQ])
        obT = sb("obT", [P, 4, SEQ])
        iqT = sb("iqT", [P, 2, SEQ])
        ikT = sb("ikT", [P, SEQ])
        kT = sb("kT", [P, SEQ])
        vA = sb("vA", [P, TT, HD])
        iw_s = sb("iw_s", [P, TT, IDXH])
        ckv_s = sb("ckv_s", [P, TT, KVL])
        ckvT = sb("ckvT", [P, 2, SEQ])
        selb = sb("selb", [P, TT, SEQ])
        top8 = sb("top8", [P, 8])
        nmx = sb("nmx", [P, 3])
        rsum = sb("rsum", [P, 3])
        rinv = sb("rinv", [P, 3])
        bst = sb("bst", [P, 2 * NH, 6])
        mv = sb("mv", [P, 2 * NH, 2])
        scr = sb("scr", [P, 3072])
        rsc = sb("rsc", [P, TT, NE])
        rsel = sb("rsel", [P, TT, NE])
        rwk = sb("rwk", [P, TT, NE])
        gsc = sb("gsc", [P, NG])
        g8 = sb("g8", [P, NG, 8])
        gate = sb("gate", [P, TT, NEX])
        adaS = vc_s[:, :, :].rearrange("p i (a n) -> p (i a) n", a=2)
        gpost = gcs
        gtb = [b[0:1, :, :].rearrange("p a n -> p (a n)") for b in (qbT, kbT)]
        rp = scr[:, 0:2048].rearrange("p (b a n) -> p b a n", b=2, a=2)
        lr = scr[:, 2048:3072].rearrange("p (b t) -> p b t", b=4)
        zs = scr[:, 0:768].rearrange("p (b n) -> p b n", b=2)
        ln = scr[:, 768:1536].rearrange("p (b n) -> p b n", b=2)
        aw = scr[:, 1536:3072].rearrange("p (b n) -> p b n", b=4)
        sm = scr[:, 0:768].rearrange("p (b n) -> p b n", b=3)
        pTs = scr[:, 768:1792].rearrange("p (b n) -> p b n", b=4)
        rw = scr[:, 0:768].rearrange("p (b n) -> p b n", b=2)
        tab = scr[:, 0:1024].rearrange("p (b a n) -> p b a n", b=2, a=2)
        tc = scr[:, 1024:1536].rearrange("p (b n) -> p b n", b=2)
        dx = scr[:, 0:2048].rearrange("p (b n) -> p b n", b=2)
        junk = scr[:, 2048:3072]
        esl = scr[:, 0:512].rearrange("p (b n) -> p b n", b=2)
        hid = scr[:, 512:1536].rearrange("p (b i n) -> p b i n", b=2, i=TT)
        eTs = scr[:, 1536:2048].rearrange("p (j t) -> p j t", j=2)

        def ocT(k):
            return (qcT, kcT)[k // 4][:, k % 4, :]

        def mT(j):
            return (qbT, kbT)[j // 4][:, j % 4, :]

        psums = [ctx.enter_context(nc.psum_tensor(f"bank{b}", [P, 512], F32)) for b in range(8)]

        S = {name: sem(name) for name in TOTAL}
        slot_full = [sem(f"slot_full{n}") for n in range(NS)]
        w13_full = [sem(f"w13_full{n}") for n in range(NW)]
        w2_full = [sem(f"w2_full{n}") for n in range(NW)]
        bank_free = [sem(f"bank_free{n}") for n in range(NB)]
        fixed_loaded, x_loaded, pos_loaded, angles, sincos, csig, setup, out_stored = (
            sem(n) for n in ("fixed_loaded", "x_loaded", "pos_loaded", "angles", "sincos", "csig", "setup", "out_stored"))
        setup_chain = sem("setup_chain")
        waits_apart = sem("waits_apart")

        def at(l, name, n):
            return S[name], l * TOTAL[name] + n

        def full(l, unit):
            return S["bank_full"], l * NU + UNIT[unit] + 1

        def bank(unit):
            return psums[UNIT[unit] % NB]

        def freed(unit):
            return bank_free[UNIT[unit] % NB]

        def flat(b):
            return b.rearrange("p a n -> p (a n)")

        def apart(eng):
            eng.sem_inc(waits_apart, 1)

        class Chain:

            def __init__(self, eng, name):
                self.eng, self.name, self.n = eng, name, 0

            def link(self, l, ins):
                self.n += 1
                ins.then_inc(S[self.name], 1)
                self.eng.wait_ge(S[self.name], l * TOTAL[self.name] + self.n)

        block = ctx.enter_context(nc.Block())

        @block.sync
        def _(sp):
            sp.dma_start(fix[:, :], fixed).then_inc(fixed_loaded, 16)
            for i in range(TT):
                sp.dma_start(x_sb[:, i, :], x[0, i * P:(i + 1) * P, :]).then_inc(x_loaded, 16)
            sp.dma_start(c_col[:, :], c[0, :].rearrange("(p k) -> p k", k=KD)).then_inc(x_loaded, 16)

            def chunk(l, n):
                slot = n % NS
                if n < NS:
                    sp.wait_ge(S["w13_used"], l * NEX + NW)
                else:
                    sp.wait_ge(*at(l, "chunk_used", n - NS + 1))
                apart(sp)
                kind = CHUNKS[n]
                w = wring[:, slot]
                if kind[0] == "ada":
                    sp.dma_start(w, ada_w[l, :, 512 * kind[1]:512 * kind[1] + 512].rearrange("(p k) n -> p k n", k=KD))\
                      .then_inc(slot_full[slot], 32)
                elif kind[0] == "in":
                    sp.dma_start(w[:, :, 0:kind[2]],
                                 w_in[l, :, kind[1]:kind[1] + kind[2]].rearrange("(p k) n -> p k n", k=KD))\
                      .then_inc(slot_full[slot], 32)
                elif kind[0] == "oab":
                    for b, src in enumerate((w_o_a, w_o_b)):
                        sp.dma_start(w[:, 4 * b:4 * b + 4, :],
                                     src[l, :, 512 * kind[1]:512 * kind[1] + 512].rearrange("(k p) n -> p k n", p=P))\
                          .then_inc(slot_full[slot], 16)
                elif kind[0] == "oc":
                    sp.dma_start(w, w_o_c[l, :, 512 * kind[1]:512 * kind[1] + 512].rearrange("(p k) n -> p k n", k=KD))\
                      .then_inc(slot_full[slot], 32)
                else:
                    sp.dma_start(w, w_out[l, :, 512 * kind[1]:512 * kind[1] + 512].rearrange("(k p) n -> p k n", p=P))\
                      .then_inc(slot_full[slot], 32)

            def expert(l, q, slot, a1, a3, a2):
                sp.wait_ge(S["w13_used"], q + 1)
                apart(sp)
                sp.dma_start(w13[:, slot, 0], a1.rearrange("(p k) n -> p k n", k=KD)).then_inc(w13_full[slot], 16)
                sp.dma_start(w13[:, slot, 1], a3.rearrange("(p k) n -> p k n", k=KD)).then_inc(w13_full[slot], 16)
                sp.wait_ge(S["w2_used"], q + 1)
                apart(sp)
                sp.dma_start(w2s[:, slot], a2.rearrange("(p j) n -> p j n", j=2)).then_inc(w2_full[slot], 16)

            with sp.Fori(0, depth) as l:
                for n in range(NCH):
                    chunk(l, n)
                sp.wait_ge(*full(l, ("y", 0, 0)))
                apart(sp)
                sp.wait_ge(*at(l, "chunk_used", NCH))
                apart(sp)
                with sp.Fori(0, NE // NW) as r:
                    for slot in range(NW):
                        e = r * NW + slot
                        expert(l, l * NEX + e, slot, w1[l, e, :, :], w3[l, e, :, :], w2[l, e, :, :])
                expert(l, l * NEX + NE, 0, ws1[l, :, :], ws3[l, :, :], ws2[l, :, :])
            sp.wait_ge(S["layer_done"], depth + 1)
            for i in range(TT):
                sp.dma_start(out[0, i * P:(i + 1) * P, :], x_sb[:, i, :]).then_inc(out_stored, 16)
            sp.wait_ge(out_stored, 16 * TT)

        @block.gpsimd
        def _(pool):
            chain = Chain(pool, "gpsimd_chain")
            pos_i = obT[:, 0, :].bitcast(I32)
            pool.dma_start(pos_i, positions.to_broadcast([P, SEQ])).then_inc(pos_loaded, 16)
            pool.memset(ones[:, :], 1.0)
            pool.memset(ones32[:, :], 1.0 / 32)
            pool.memset(zeros[:, :], 0.0)
            pool.memset(gate[:, :, NE:NEX], 1.0).then_inc(setup, 1)

            with pool.Fori(0, depth) as l:
                pool.wait_ge(S["layer_done"], l + 1)
                col = lambda v: v.rearrange("(p k) -> p k", k=KD)
                row = lambda v: v.rearrange("(a n) -> a n", a=1)
                pool.dma_start(gpre[:, 0, :], col(g_pre_mix[l, :])).then_inc(S["params"], 16)
                pool.dma_start(gpre[:, 1, :], col(g_pre_ffn[l, :])).then_inc(S["params"], 16)
                pool.dma_start(adabc[:, 0:2, :], ada_b[l, 0:2 * D].rearrange("(v p k) -> p v k", v=2, k=KD))\
                    .then_inc(S["params"], 16)
                pool.dma_start(adabc[:, 2:4, :], ada_b[l, 3 * D:5 * D].rearrange("(v p k) -> p v k", v=2, k=KD))\
                    .then_inc(S["params"], 16)
                pool.dma_start(gtb[0], row(ada_b[l, 2 * D:3 * D])).then_inc(S["params"], 16)
                pool.dma_start(gtb[1], row(ada_b[l, 5 * D:6 * D])).then_inc(S["params"], 16)
                pool.dma_start(gpost[:, 0, :], row(g_post_mix[l, :]).to_broadcast([P, D])).then_inc(S["params"], 16)
                pool.dma_start(gpost[:, 1, :], row(g_post_ffn[l, :]).to_broadcast([P, D])).then_inc(S["params"], 16)
                pool.dma_start(gret_c[:, :], col(g_ret[l, :])).then_inc(S["params"], 16)
                pool.dma_start(rbias[:, :], row(router_bias[l, :]).to_broadcast([P, NE])).then_inc(S["params"], 16)
                pool.dma_start(wuk[:, :, :], w_uk[l, :, :].rearrange("(b p) n -> p b n", p=P)).then_inc(S["params"], 16)
                pool.dma_start(wuv[:, :, :], w_uv[l, :, :].rearrange("(b p) n -> p b n", p=P)).then_inc(S["params"], 16)
                pool.dma_start(wrt[:, :, :], w_router[l, :, :].rearrange("(p k) n -> p k n", k=KD))\
                    .then_inc(S["params"], 16)
                with nc.allow_non_contiguous_dma(reason="two columns"):
                    pool.dma_start(gkv_c[:, :], g_kv[l, :].rearrange("(b p) -> p b", p=P)).then_inc(S["decay"], 16)
                pool.dma_start(flat(dec), decay).then_inc(S["decay"], 16)

                for n, (dst, blocks) in enumerate(((iqT, 2), (ikT, 1), (qaT[:, 0:2], 2), (qaT[:, 2:4], 2), (kT, 1),
                                                   (qcT[:, 0:2], 2), (qcT[:, 2:4], 2), (kcT[:, 0:2], 2),
                                                   (kcT[:, 2:4], 2))):
                    pool.wait_ge(*at(l, "rope_mul", n + 1))
                    to = dst[:, :] if blocks == 1 else flat(dst[:, :, :])
                    w = blocks * SEQ
                    pool.tensor_tensor(to, rp[:, n % 2, 0, 0:w], rp[:, n % 2, 1, 0:w], ALU.add)\
                        .then_inc(S["roped"], 1)

                for h in range(NH):
                    pool.wait_ge(*at(l, "zs_ready", h + 1))
                    if h >= 4:
                        pool.wait_ge(*full(l, ("ob", (h - 4) // 2)))
                    pool.tensor_tensor(aw[:, h % 4, :], zs[:, h % 2, :], cmneg, ALU.add).then_inc(S["zb_ready"], 1)

                for n in range(2 * NH):
                    w = P * (n // NH + 1)
                    pool.wait_ge(*at(l, "rinv_ready", n + 1))
                    apart(pool)
                    pool.tensor_scalar(sm[:, n % 3, 0:w], sm[:, n % 3, 0:w], rinv[:, n % 3:n % 3 + 1], None, ALU.mult)\
                        .then_inc(S["pn_ready"], 1)

                for i in range(TT):
                    pool.wait_ge(*at(l, "ocn_ready", i + 1))
                    pool.wait_ge(*at(l, "gc_ready", 4))
                    pool.tensor_tensor(rows[:, i, :], rows[:, i, :], gcs[:, i, :], ALU.mult).then_inc(S["ocg_ready"], 1)

                for j in range(KD):
                    pool.wait_ge(*at(l, "tab_ready", j + 1))
                    chain.link(l, pool.tensor_tensor(mT(j), tab[:, j % 2, 0, :], tab[:, j % 2, 1, :], ALU.add))
                    pool.wait_ge(*at(l, "tc_ready", j + 1))
                    pool.tensor_tensor(mT(j), mT(j), tc[:, j % 2, :], ALU.add).then_inc(S["mT_ready"], 1)

                for n in range(2 * TT):
                    pool.wait_ge(*at(l, "dx_ready", n + 1))
                    i = n % TT
                    pool.tensor_tensor(x_sb[:, i, :], x_sb[:, i, :], dx[:, i, :], ALU.add).then_inc(S["x_ready"], 1)
            assert chain.n == TOTAL["gpsimd_chain"], chain.n

        @block.scalar
        def _(act):
            chain = Chain(act, "scalar_chain")
            act.wait_ge(angles, 1)
            act.activation(sinT[:, :], sinT[:, :], ACT.Sin)
            act.activation(cosT[:, :], cosT[:, :], ACT.Sin).then_inc(sincos, 1)
            act.wait_ge(x_loaded, 48)
            act.activation(c_col[:, :], c_col[:, :], ACT.Silu).then_inc(csig, 1)

            def rsqrt(l, n, w):
                act.wait_ge(*at(l, "ms_ready", n + 1))
                chain.link(l, act.activation(rs0[:, 0:w], ms[:, 0:w], ACT.Ln))
                act.activation(rs0[:, 0:w], rs0[:, 0:w], ACT.Exp, scale=-0.5).then_inc(S["rsq_raw"], 1)

            def normed_rows(l, n):
                act.wait_ge(*at(l, "rms_ready", n + 1))
                for i in range(TT):
                    act.activation(rows[:, i, :], x_sb[:, i, :], ACT.Copy, scale=rs[:, i:i + 1])\
                       .then_inc(S["xn_ready"], 1)

            def copy_out(l, unit, dst, src, name, func=ACT.Copy, scale=1.0):
                act.wait_ge(*full(l, unit))
                act.activation(dst, src, func, scale=scale).then_inc(S[name], 1)

            with act.Fori(0, depth) as l:
                for n in range(12):
                    act.wait_ge(*full(l, ("ada", n)))
                    chain.link(l, act.activation(adaS[:, n % 4, :], bank(("ada", n))[:, :], ACT.Copy))
                    act.sem_inc(S["ada_copied"], 1)
                    act.sem_inc(freed(("ada", n)), 1)
                rsqrt(l, 0, TT)
                normed_rows(l, 0)

                def take(unit, dst, src, name, func=ACT.Copy, scale=1.0):
                    act.wait_ge(*full(l, unit))
                    chain.link(l, act.activation(dst, src, func, scale=scale))
                    act.sem_inc(S[name], 1)
                    act.sem_inc(freed(unit), 1)

                two = lambda b: b[:, :].rearrange("p (a n) -> p a n", a=2)
                take(("ckv",), ckv_s[:, :, :], two(bank(("ckv",))), "ckv_copied")
                take(("iw",), iw_s[:, :, :], bank(("iw",))[:, 0:2 * IDXH].rearrange("p (i h) -> p i h", i=TT), "iw_ready")
                rsqrt(l, 1, TT)
                n = 0
                for i in range(TT):
                    w = P * (i + 1)
                    for h in range(IDXH):
                        if n >= 4:
                            act.wait_ge(*at(l, "lg_used", n - 3))
                        take(("lg", i, h), lr[:, n % 4, 0:w], bank(("lg", i, h))[:, 0:w], "relu_ready",
                             ACT.Relu, HD ** -0.5 * IDXH ** -0.5)
                        n += 1
                for name, dst in (("qb", qbT), ("kb", kbT)):
                    for m in range(2):
                        take((name, m), flat(dst[:, 2 * m:2 * m + 2, :]), bank((name, m))[:, :], "qkb_ready")
                for i in range(TT):
                    take(("vb", i), vb_s[:, i, :], bank(("vb", i))[:, :], "vb_ready")
                act.wait_ge(*at(l, "roped", 9))
                for n in range(NH + 2):
                    if n < NH:
                        z, e = zs[:, n % 2, :], ln[:, n % 2, :]
                        if n >= 2:
                            act.wait_ge(*full(l, ("cum", n - 2)))
                            act.wait_ge(*at(l, "zb_ready", n - 1))
                        take(("z", n), z, bank(("z", n))[:, 0:TRI], "zs_ready", ACT.Copy, HD ** -0.5)
                        chain.link(l, act.activation(e, z, ACT.Abs))
                        chain.link(l, act.activation(e, e, ACT.Exp, scale=-1.0))
                        act.activation(e, e, ACT.Ln, bias=1.0).then_inc(S["ln_ready"], 1)
                    if 1 <= n < NH + 1:
                        act.wait_ge(*at(l, "w_ready", n))
                        act.activation(aw[:, (n - 1) % 4, :], aw[:, (n - 1) % 4, :], ACT.Exp).then_inc(S["a_ready"], 1)
                    if n >= 3 and n % 2 == 1:
                        m = (n - 3) // 2
                        take(("ob", m), obT[:, m, :], bank(("ob", m))[:, 0:SEQ], "ob_ready")
                    if n < 4:
                        take(("vc", n), vc_s[:, n % 2, 512 * (n // 2):512 * (n // 2) + 512], bank(("vc", n))[:, :],
                             "vc_ready")
                    elif n < 8:
                        m = n - 4
                        take(("gc", m), gcs[:, m % 2, 512 * (m // 2):512 * (m // 2) + 512], bank(("gc", m))[:, :],
                             "gc_ready", ACT.Silu)
                for n in range(2 * NH + 3):
                    if n < 2 * NH:
                        w = P * (n // NH + 1)
                        act.wait_ge(*at(l, "sm_ready", n + 1))
                        act.activation(sm[:, n % 3, 0:w], sm[:, n % 3, 0:w], ACT.Exp, bias=nmx[:, n % 3:n % 3 + 1],
                                       accum_out=rsum[:, n % 3:n % 3 + 1]).then_inc(S["p_ready"], 1)
                    if 2 <= n < 2 * NH + 2:
                        m = n - 2
                        w = P * (m // NH + 1)
                        take(("pT", m), pTs[:, m % 4, 0:w], bank(("pT", m))[:, 0:w], "pTs_ready")
                    if n >= 4 and n % 2 == 0:
                        m = (n - 4) // 2
                        i, hb = m // PAIRS, m % PAIRS
                        take(("oa", m), oaT[:, hb, i * P:(i + 1) * P], bank(("oa", m))[:, 0:P], "oa_ready")
                    if n < 12:
                        take(("gate", n), flat(gT[:, 2 * n:2 * n + 2, :]), bank(("gate", n))[:, :], "gate_ready",
                             ACT.Sigmoid)
                for h in range(NH):
                    take(("oc", h), rows[:, :, h * CV:(h + 1) * CV],
                         bank(("oc", h))[:, 0:2 * CV].rearrange("p (i n) -> p i n", i=TT), "osb_ready")
                rsqrt(l, 2, 2 * NH)
                for m in range(4):
                    act.wait_ge(*full(l, ("ocT", m)))
                    for kk in range(2):
                        k = 2 * m + kk
                        chain.link(l, act.activation(ocT(k), bank(("ocT", m))[:, kk * SEQ:(kk + 1) * SEQ], ACT.Copy,
                                                     scale=gret_c[:, k:k + 1]))
                    act.sem_inc(S["ocT_ready"], 1)
                    act.sem_inc(freed(("ocT", m)), 1)
                for hf in range(2):
                    for i in range(TT):
                        take(("y", hf, i), rows[:, i, hf * 512:hf * 512 + 512], bank(("y", hf, i))[:, :], "y_ready")
                rsqrt(l, 3, TT)
                rsqrt(l, 4, TT)
                normed_rows(l, 1)
                take(("rt",), rsc[:, :, :], bank(("rt",))[:, 0:TT * NE].rearrange("p (i e) -> p i e", i=TT),
                     "scores_ready", ACT.Sigmoid)

                def silu(q, i):
                    act.wait_ge(S["h_ready"], q * TT + i + 1)
                    act.activation(esl[:, i, :], psums[i][:, 0:ED], ACT.Silu).then_inc(S["silu_ready"], 1)

                def hidden_T(q):
                    act.wait_ge(S["eT_ready"], q + 1)
                    act.activation(flat(eTs[:, :, :]), psums[2][:, :], ACT.Copy).then_inc(S["eTs_ready"], 1)

                q0 = l * NEX
                silu(q0, 0)
                silu(q0, 1)
                with act.Fori(0, NE // NW) as r:
                    for s in range(NW):
                        q = q0 + (r * NW + s)
                        silu(q + 1, 0)
                        hidden_T(q)
                        silu(q + 1, 1)
                hidden_T(q0 + NE)
                act.wait_ge(*at(l, "yacc_ready", 1))
                for i in range(TT):
                    for hf in range(2):
                        act.activation(rows[:, i, hf * 512:hf * 512 + 512], psums[4 + 2 * i + hf][:, :], ACT.Copy)\
                           .then_inc(S["y2_ready"], 1)
                rsqrt(l, 5, TT)
            assert chain.n == TOTAL["scalar_chain"], chain.n

        @block.vector
        def _(dve):
            chain = Chain(dve, "vector_chain")
            for b in range(NB):
                dve.sem_inc(bank_free[b], 1)
            dve.sem_inc(S["layer_done"], 1)
            dve.sem_inc(S["w13_used"], NW)
            dve.sem_inc(S["w2_used"], NW)
            dve.sem_inc(S["hid_ready"], TT)
            dve.sem_inc(S["eTs_ready"], 1)

            steps = [0]

            def once(ins):
                steps[0] += 1
                ins.then_inc(setup_chain, 1)
                dve.wait_ge(setup_chain, steps[0])

            dve.wait_ge(fixed_loaded, 16)
            dve.wait_ge(pos_loaded, 16)
            pos_f, ang, turns = (obT[:, n, :] for n in (1, 2, 3))
            once(dve.tensor_copy(pos_f, obT[:, 0, :].bitcast(I32)))
            once(dve.tensor_scalar(ang, pos_f, invf, None, ALU.mult))
            near = 1.5 * 2 ** 23
            c1 = 6.28125
            c2 = float(np.float32(2 * np.pi - c1))
            c2 = float(np.frombuffer((np.frombuffer(np.float32(c2).tobytes(), np.uint32) & 0xFFFFF000).tobytes(),
                                     np.float32)[0])
            c3 = float(np.float32(2 * np.pi - c1 - c2))
            for dst, quarter in ((sinT, 0.0), (cosT, 0.25)):
                once(dve.tensor_scalar(turns, ang, 1 / (2 * np.pi), quarter, ALU.mult, ALU.add))
                once(dve.tensor_scalar(turns, turns, near, near, ALU.add, ALU.subtract))
                once(dve.scalar_tensor_tensor(out=dst[:, :], in0=turns, scalar=-c1, in1=ang, op0=ALU.mult, op1=ALU.add))
                once(dve.scalar_tensor_tensor(out=dst[:, :], in0=turns, scalar=-c2, in1=dst[:, :], op0=ALU.mult,
                                              op1=ALU.add))
                once(dve.scalar_tensor_tensor(out=dst[:, :], in0=turns, scalar=-c3, in1=dst[:, :], op0=ALU.mult,
                                              op1=ALU.add))
                if quarter:
                    once(dve.tensor_scalar(dst[:, :], dst[:, :], np.pi / 2, None, ALU.add))
                pi = float(np.nextafter(np.float32(np.pi), np.float32(0)))
                once(dve.tensor_scalar(dst[:, :], dst[:, :], -pi, pi, ALU.max, ALU.min))
            dve.sem_inc(angles, 1)
            dve.wait_ge(setup, 1)
            dve.wait_ge(csig, 1)
            for k in range(KD):
                once(dve.tensor_scalar(c_rep[:, k, :], ones[:, 0:32], c_col[:, k:k + 1], None, ALU.mult))
            dve.wait_ge(sincos, 1)
            once(dve.tensor_scalar(sinT[:, :], sinT[:, :], rsign, None, ALU.mult))
            dve.sem_inc(setup, 1)

            with dve.Fori(0, depth) as l:
                link = lambda ins: chain.link(l, ins)

                def refine(n, w):
                    dve.wait_ge(*at(l, "rsq_raw", n + 1))
                    link(dve.tensor_tensor(rt1[:, 0:w], ms[:, 0:w], rs0[:, 0:w], ALU.mult))
                    link(dve.tensor_tensor(rt1[:, 0:w], rt1[:, 0:w], rs0[:, 0:w], ALU.mult))
                    link(dve.tensor_scalar(rt1[:, 0:w], rt1[:, 0:w], -0.5, 1.5, ALU.mult, ALU.add))
                    link(dve.tensor_tensor(rs[:, 0:w], rs0[:, 0:w], rt1[:, 0:w], ALU.mult))

                def mean_square(src, w, to):
                    link(dve.tensor_tensor_reduce(junk[:, 0:w], src, src, 1.0, 0.0, ALU.mult, ALU.add,
                                                  part[:, to:to + 1]))

                def to_ms(w):
                    link(dve.tensor_scalar(ms[:, 0:TT], part[:, 0:TT], 1.0 / w, EPS, ALU.mult, ALU.add))
                    dve.sem_inc(S["ms_ready"], 1)

                def prenorm(n, root, units):
                    for i in range(TT):
                        mean_square(x_sb[:, i, :], D, i)
                    to_ms(D)
                    refine(root, TT)
                    dve.sem_inc(S["rms_ready"], 1)
                    for m in range(4):
                        unit = (units, m)
                        dve.wait_ge(*full(l, unit))
                        for kk in range(2):
                            k = 2 * m + kk
                            link(dve.tensor_scalar(hT[:, k, :], bank(unit)[:, kk * SEQ:(kk + 1) * SEQ],
                                                   modc[:, 2 * n + 1, k:k + 1], modc[:, 2 * n, k:k + 1],
                                                   ALU.mult, ALU.add))
                        dve.sem_inc(S["hT_ready"], 1)
                        dve.sem_inc(freed(unit), 1)

                def rope(n, unit, blocks):
                    b = bank(unit)
                    dve.wait_ge(*full(l, unit))
                    if n >= 2:
                        dve.wait_ge(*at(l, "roped", n - 1))
                    for q in range(4):
                        o = 32 * (q ^ 1)
                        for a in range(blocks):
                            dve.tensor_tensor(rp[32 * q:32 * q + 32, n % 2, 0, a * SEQ:(a + 1) * SEQ],
                                              b[o:o + 32, a * SEQ:(a + 1) * SEQ], sinT[32 * q:32 * q + 32, :],
                                              ALU.mult)
                    for a in range(blocks):
                        ins = dve.tensor_tensor(rp[:, n % 2, 1, a * SEQ:(a + 1) * SEQ], b[:, a * SEQ:(a + 1) * SEQ],
                                                cosT[:, :], ALU.mult)
                    link(ins)
                    dve.sem_inc(S["rope_mul"], 1)
                    if unit != ("kv",):
                        dve.sem_inc(freed(unit), 1)

                dve.wait_ge(*at(l, "params", 13 * 16))
                for n in (0, 2, 4, 5, 6, 8, 10, 11):
                    if n in (4, 5, 10, 11):
                        g, hf = n // 6, n % 2
                        dve.wait_ge(*full(l, ("gt", n)))
                        link(dve.tensor_tensor(gtg[:, g, hf * 512:hf * 512 + 512], bank(("gt", n))[:, :],
                                               gpost[:, g, hf * 512:hf * 512 + 512], ALU.mult))
                        dve.sem_inc(freed(("gt", n)), 1)
                    else:
                        v = {0: 0, 2: 1, 6: 2, 8: 3}[n]
                        dve.wait_ge(*full(l, ("mod", n)))
                        link(dve.tensor_tensor(modc[:, v, :], bank(("mod", n))[:, 0:KD], adabc[:, v, :], ALU.add))
                        dve.sem_inc(freed(("mod", n)), 1)
                        if v % 2:
                            link(dve.scalar_tensor_tensor(out=modc[:, v, :], in0=modc[:, v, :], scalar=1.0,
                                                          in1=gpre[:, v // 2, :], op0=ALU.add, op1=ALU.mult))
                dve.wait_ge(x_loaded, 48)
                prenorm(0, 0, "xT")

                dve.wait_ge(*at(l, "ckv_copied", 1))
                for i in range(TT):
                    mean_square(ckv_s[:, i, :], KVL, i)
                to_ms(KVL)
                refine(1, TT)
                for i in range(TT):
                    link(dve.tensor_scalar(ckv_s[:, i, :], ckv_s[:, i, :], rs[:, i:i + 1], None, ALU.mult))
                dve.sem_inc(S["ckv_scaled"], 1)
                rope(0, ("iq",), 2)
                rope(1, ("ik",), 1)
                rope(2, ("qa", 0), 2)
                rope(3, ("qa", 1), 2)
                dve.wait_ge(*at(l, "decay", 32))
                dve.wait_ge(*full(l, ("ckvT",)))
                for b in range(2):
                    link(dve.tensor_scalar(ckvT[:, b, :], bank(("ckvT",))[:, b * SEQ:(b + 1) * SEQ], gkv_c[:, b:b + 1],
                                           None, ALU.mult))
                dve.sem_inc(S["ckvT_ready"], 1)
                dve.sem_inc(freed(("ckvT",)), 1)
                rope(4, ("kv",), 1)
                link(dve.tensor_copy(vA[:, :, :], bank(("kv",))[:, SEQ:SEQ + TT * HD].rearrange("p (i n) -> p i n", i=TT)))
                dve.sem_inc(S["vA_ready"], 1)
                dve.sem_inc(freed(("kv",)), 1)

                dve.wait_ge(*at(l, "iw_ready", 1))
                n = 0
                for i in range(TT):
                    w = P * (i + 1)
                    score = selb[:, i, 0:w]
                    for h in range(IDXH):
                        dve.wait_ge(*at(l, "relu_ready", n + 1))
                        link(dve.scalar_tensor_tensor(out=score, in0=lr[:, n % 4, 0:w],
                                                      scalar=iw_s[:, i, h:h + 1],
                                                      in1=adm[:, i, 0:w] if h == 0 else score,
                                                      op0=ALU.mult, op1=ALU.add))
                        dve.sem_inc(S["lg_used"], 1)
                        n += 1
                    for _ in range(TOPK // 8):
                        apart(dve)
                        link(dve.max(top8[:, :], score))
                        apart(dve)
                        link(dve.match_replace(score, top8[:, :], score, GONE))
                    link(dve.tensor_scalar(score, score, GONE_T, -1.0, ALU.is_le, ALU.add))
                    link(dve.tensor_scalar(score, score, BIG, None, ALU.mult))
                    dve.sem_inc(S["sel_ready"], 1)
                for n, (name, m) in enumerate((("qc", 0), ("qc", 1), ("kc", 0), ("kc", 1))):
                    rope(5 + n, (name, m), 2)

                for n in range(NH + 1):
                    if n < NH:
                        dve.wait_ge(*at(l, "ln_ready", n + 1))
                        z, e = zs[:, n % 2, :], ln[:, n % 2, :]
                        link(dve.scalar_tensor_tensor(out=e, in0=z, scalar=0.0, in1=e, op0=ALU.max, op1=ALU.add))
                        dve.tensor_tensor(e, e, cm01, ALU.mult).then_inc(S["sp_ready"], 1)
                    if n >= 1:
                        h = n - 1
                        dve.wait_ge(*full(l, ("cum", h)))
                        dve.wait_ge(*at(l, "zb_ready", h + 1))
                        link(dve.scalar_tensor_tensor(out=aw[:, h % 4, :], in0=bank(("cum", h))[:, 0:TRI], scalar=-1.0,
                                                      in1=aw[:, h % 4, :], op0=ALU.mult, op1=ALU.add))
                        dve.sem_inc(S["w_ready"], 1)
                        dve.sem_inc(freed(("cum", h)), 1)

                dve.wait_ge(*full(l, ("ob", PAIRS - 1)))
                for n in range(2 * NH + 1):
                    if n < 2 * NH:
                        i = n // NH
                        w = P * (i + 1)
                        dve.wait_ge(*full(l, ("sc", n)))
                        if n >= 3:
                            dve.wait_ge(*full(l, ("pT", n - 3)))
                        link(dve.scalar_tensor_tensor(out=sm[:, n % 3, 0:w], in0=bank(("sc", n))[:, 0:w],
                                                      scalar=HD ** -0.5, in1=selb[:, i, 0:w], op0=ALU.mult,
                                                      op1=ALU.add))
                        dve.sem_inc(freed(("sc", n)), 1)
                        dve.tensor_reduce(nmx[:, n % 3:n % 3 + 1], sm[:, n % 3, 0:w], AX, ALU.max, negate=True)\
                           .then_inc(S["sm_ready"], 1)
                    if n >= 1:
                        m = (n - 1) % 3
                        dve.wait_ge(*at(l, "p_ready", n))
                        dve.reciprocal(rinv[:, m:m + 1], rsum[:, m:m + 1]).then_inc(S["rinv_ready"], 1)

                dve.wait_ge(*full(l, ("oa", 2 * PAIRS - 1)))
                for n in range(NH + 1):
                    if n < NH:
                        dve.wait_ge(*full(l, ("ret", n)))
                        link(dve.tensor_tensor(rw[:, n % 2, :], bank(("ret", n))[:, 0:TRI], dec[:, n, :], ALU.mult))
                        dve.sem_inc(S["rw_ready"], 1)
                        dve.sem_inc(freed(("ret", n)), 1)
                    if n >= 1:
                        h = n - 1
                        dve.wait_ge(*at(l, "osb_ready", n))
                        for i in range(TT):
                            link(dve.bn_stats(bst[:, i * NH + h, :], rows[:, i, h * CV:(h + 1) * CV]))
                for m in range(TT * NH):
                    apart(dve)
                    link(dve.bn_aggr(mv[:, m, :], bst[:, m, :]))
                link(dve.tensor_scalar(ms[:, 0:TT * NH], mv[:, :, 1], EPS, None, ALU.add))
                dve.sem_inc(S["ms_ready"], 1)
                refine(2, TT * NH)
                for i in range(TT):
                    for h in range(NH):
                        m = i * NH + h
                        link(dve.tensor_scalar(rows[:, i, h * CV:(h + 1) * CV], rows[:, i, h * CV:(h + 1) * CV],
                                               mv[:, m, 0:1], rs[:, m:m + 1], ALU.subtract, ALU.mult))
                    dve.sem_inc(S["ocn_ready"], 1)

                dve.wait_ge(*at(l, "gate_ready", 12))
                for j in range(KD):
                    if j >= 2:
                        dve.wait_ge(*at(l, "mT_ready", j - 1))
                    dve.wait_ge(*full(l, ("yab", j)))
                    link(dve.tensor_tensor(tab[:, j % 2], bank(("yab", j))[:, :].rearrange("p (a n) -> p a n", a=2),
                                           gT[:, j:j + 9:8, :], ALU.mult))
                    dve.sem_inc(S["tab_ready"], 1)
                    dve.sem_inc(freed(("yab", j)), 1)
                    dve.wait_ge(*full(l, ("yc", j)))
                    link(dve.tensor_tensor(tc[:, j % 2, :], bank(("yc", j))[:, 0:SEQ], gT[:, 16 + j, :], ALU.mult))
                    dve.sem_inc(S["tc_ready"], 1)
                    dve.sem_inc(freed(("yc", j)), 1)

                def postnorm(n, root, name):
                    dve.wait_ge(*at(l, name, 4))
                    for i in range(TT):
                        mean_square(rows[:, i, :], D, i)
                    to_ms(D)
                    refine(root, TT)
                    for i in range(TT):
                        dve.scalar_tensor_tensor(out=dx[:, i, :], in0=rows[:, i, :], scalar=rs[:, i:i + 1],
                                                 in1=gtg[:, n, :], op0=ALU.mult, op1=ALU.mult)\
                           .then_inc(S["dx_ready"], 1)
                    dve.wait_ge(*at(l, "x_ready", TT * (n + 1)))

                postnorm(0, 3, "y_ready")
                prenorm(1, 4, "hT")

                dve.wait_ge(*at(l, "scores_ready", 1))
                for i in range(TT):
                    sel = rsel[:, i, :]
                    link(dve.tensor_tensor(sel, rsc[:, i, :], rbias[:, :], ALU.add))
                    for g in range(NG):
                        apart(dve)
                        link(dve.max(g8[:, g, :], rsel[:, i, g * EG:(g + 1) * EG]))
                    link(dve.tensor_tensor(gsc[:, :], g8[:, :, 0], g8[:, :, 1], ALU.add))
                    apart(dve)
                    link(dve.max(top8[:, :], gsc[:, :]))
                    link(dve.memset(top8[:, TOPG:8], 2 * GONE_T / 3))
                    apart(dve)
                    link(dve.match_replace(gsc[:, :], top8[:, :], gsc[:, :], GONE))
                    link(dve.tensor_scalar(gsc[:, :], gsc[:, :], GONE_T, -1.0, ALU.is_le, ALU.add))
                    link(dve.tensor_scalar(gsc[:, :], gsc[:, :], BIG, None, ALU.mult))
                    link(dve.tensor_tensor(sel.rearrange("p (g e) -> p g e", g=NG),
                                           sel.rearrange("p (g e) -> p g e", g=NG),
                                           gsc[:, :].unsqueeze(2).to_broadcast([P, NG, EG]), ALU.add))
                    apart(dve)
                    link(dve.max(top8[:, :], sel))
                    apart(dve)
                    link(dve.match_replace(sel, top8[:, :], sel, GONE))
                    link(dve.tensor_scalar(sel, sel, GONE_T, None, ALU.is_le))
                    link(dve.tensor_tensor_reduce(rwk[:, i, :], sel, rsc[:, i, :], 1.0, 0.0, ALU.mult, ALU.add,
                                                  part[:, i:i + 1]))
                    link(dve.reciprocal(part[:, 2 + i:3 + i], part[:, i:i + 1]))
                    link(dve.tensor_scalar(gate[:, i, 0:NE], rwk[:, i, :], part[:, 2 + i:3 + i], ROUTED_SCALE,
                                           ALU.mult, ALU.mult))

                def hidden(q, e, buf, i):
                    dve.wait_ge(S["silu_ready"], q * TT + i + 1)
                    dve.scalar_tensor_tensor(out=hid[:, buf, i, :], in0=esl[:, i, :], scalar=gate[:, i, bass.ds(e, 1)],
                                             in1=psums[i][:, ED:2 * ED], op0=ALU.mult, op1=ALU.mult)\
                       .then_inc(S["hid_ready"], 1)

                q0 = l * NEX
                for i in range(TT):
                    hidden(q0, 0, 0, i)
                with dve.Fori(0, NE // NW) as r:
                    for s in range(NW):
                        e = r * NW + s + 1
                        for i in range(TT):
                            hidden(q0 + e, e, (s + 1) % 2, i)
                postnorm(1, 5, "y2_ready")
                dve.sem_inc(S["layer_done"], 1)
            assert chain.n == TOTAL["vector_chain"], chain.n

        @block.tensor
        def _(pe):
            mm = pe.matmul
            pe.wait_ge(setup, 2)
            pe.wait_ge(fixed_loaded, 16)

            with pe.Fori(0, depth) as l:
                order = [0]
                used = [0]

                def take(*unit):
                    u = order[0]
                    assert UNITS[u] == unit, (UNITS[u], unit)
                    order[0] += 1
                    pe.wait_ge(bank_free[u % NB], l * USES[u % NB] + u // NB + 1)
                    return psums[u % NB]

                def chunk_in(n):
                    pe.wait_ge(slot_full[n % NS], l * (NCH // NS * 32) + 32 * (n // NS + 1))
                    return wring[:, n % NS]

                def chunk_out(ins):
                    used[0] += 1
                    pe.sem_inc(S["chunk_used"], 1)

                def ada(n):
                    b = take("ada", n)
                    w = chunk_in(n)
                    for k in range(KD):
                        j = k % 4
                        ins = mm(b[32 * j:32 * j + 32, :], c_rep[:, k, :], w[:, k, :], start=(k < 4), stop=(k >= 4),
                                 tile_position=(0, 32 * j))
                    ins.then_inc(S["bank_full"], 1)
                    pe.wait_ge(S["bank_full"], l * NU + order[0])
                    pe.sem_inc(S["chunk_used"], 1)

                def mod_columns(n):
                    b = take("mod", n)
                    for hf in range(2):
                        pe.wait_ge(*at(l, "ada_copied", n + hf + 1))
                        for k in range(KD):
                            ins = mm(b[64 * hf:64 * hf + 64, k:k + 1], adaS[:, (n + hf) % 4, k:512:KD], ones32[:, 0:1],
                                     start=True, stop=True)
                    ins.then_inc(S["bank_full"], 1)

                def gate_rows(n):
                    b = take("gt", n)
                    pe.wait_ge(*at(l, "ada_copied", n + 1))
                    pe.wait_ge(*at(l, "params", 13 * 16))
                    mm(b[:, :], ones32[:, :], adaS[:, n % 4, :], start=True, stop=False)
                    mm(b[:, :], ones[0:1, :], gtb[n // 6][:, 512 * (n % 2):512 * (n % 2) + 512], start=False, stop=True)\
                        .then_inc(S["bank_full"], 1)

                for g in range(7):
                    if g < 6:
                        ada(2 * g)
                        ada(2 * g + 1)
                    if g >= 1:
                        n = 2 * (g - 1)
                        if n in (4, 10):
                            gate_rows(n)
                            gate_rows(n + 1)
                        else:
                            mod_columns(n)

                def transposes(unit, i_ready):
                    for m in range(4):
                        b = take(unit, m)
                        if m == 0:
                            for name, count in i_ready:
                                pe.wait_ge(*at(l, name, count))
                        for kk in range(2):
                            for i in range(TT):
                                ins = pe.transpose(b[:, kk * SEQ + i * P:kk * SEQ + (i + 1) * P],
                                                   rows[:, i, 2 * m + kk:D:KD], ident)
                        ins.then_inc(S["bank_full"], 1)

                transposes("xT", [("xn_ready", 2)])
                pe.wait_ge(*at(l, "hT_ready", 4))

                def project_T(unit, w, cols, blocks, at_col=0):
                    b = take(*unit)
                    for a in range(blocks):
                        for k in range(KD):
                            ins = mm(b[:, at_col + a * SEQ:at_col + (a + 1) * SEQ], w[:, k, cols + a * P:cols + (a + 1) * P],
                                     hT[:, k, :], start=(k == 0), stop=(k == KD - 1))
                    ins.then_inc(S["bank_full"], 1)

                def project(b, at_col, w, cols, width, i):
                    for k in range(KD):
                        ins = mm(b[:, at_col:at_col + width], hT[:, k, i * P:(i + 1) * P], w[:, k, cols:cols + width],
                                 start=(k == 0), stop=(k == KD - 1))
                    return ins

                def chunk_done():
                    pe.wait_ge(S["bank_full"], l * NU + order[0])
                    pe.sem_inc(S["chunk_used"], 1)

                c = 12
                w = chunk_in(c)
                b = take("ckv")
                for i in range(TT):
                    ins = project(b, i * KVL, w, 0, KVL, i)
                ins.then_inc(S["bank_full"], 1)
                chunk_done()
                c += 1
                w = chunk_in(c)
                project_T(("iq",), w, 0, 2)
                b = take("ik")
                for hf in range(2):
                    for k in range(KD):
                        ins = mm(b[64 * hf:64 * hf + 64, 0:SEQ], w[:, k, 256:320], hT[:, k, :], start=(k == 0),
                                 stop=(k == KD - 1))
                ins.then_inc(S["bank_full"], 1)
                b = take("iw")
                for i in range(TT):
                    ins = project(b, i * IDXH, w, 320, IDXH, i)
                ins.then_inc(S["bank_full"], 1)
                chunk_done()
                c += 1
                w = chunk_in(c)
                project_T(("qa", 0), w, 0, 2)
                project_T(("qa", 1), w, 256, 2)
                chunk_done()
                c += 1
                b = take("ckvT")
                pe.wait_ge(*at(l, "ckv_scaled", 1))
                for a in range(2):
                    for i in range(TT):
                        ins = pe.transpose(b[:, a * SEQ + i * P:a * SEQ + (i + 1) * P], ckv_s[:, i, a * P:(a + 1) * P],
                                           ident)
                ins.then_inc(S["bank_full"], 1)
                b = take("kv")
                pe.wait_ge(*at(l, "ckvT_ready", 1))
                for hf in range(2):
                    for a in range(2):
                        mm(b[64 * hf:64 * hf + 64, 0:SEQ], wuk[:, a, :], ckvT[:, a, :], start=(a == 0), stop=(a == 1))
                for i in range(TT):
                    for a in range(2):
                        ins = mm(b[:, SEQ + i * HD:SEQ + (i + 1) * HD], ckvT[:, a, i * P:(i + 1) * P], wuv[:, a, :],
                                 start=(a == 0), stop=(a == 1))
                ins.then_inc(S["bank_full"], 1)
                pe.wait_ge(*at(l, "roped", 2))
                for i in range(TT):
                    for h in range(IDXH):
                        b = take("lg", i, h)
                        r = slice(64 * (h % 2), 64 * (h % 2) + 64)
                        mm(b[:, 0:P * (i + 1)], iqT[r, h // 2, i * P:(i + 1) * P], ikT[r, 0:P * (i + 1)], start=True,
                           stop=True).then_inc(S["bank_full"], 1)
                for name in ("qb", "kb"):
                    w = chunk_in(c)
                    project_T((name, 0), w, 0, 2)
                    project_T((name, 1), w, 256, 2)
                    chunk_done()
                    c += 1
                w = chunk_in(c)
                for i in range(TT):
                    b = take("vb", i)
                    project(b, 0, w, 0, 512, i).then_inc(S["bank_full"], 1)
                chunk_done()
                c += 1
                for name in ("qc", "kc"):
                    w = chunk_in(c)
                    project_T((name, 0), w, 0, 2)
                    project_T((name, 1), w, 256, 2)
                    chunk_done()
                    c += 1

                def head_rows(h):
                    return slice(64 * (h % 2), 64 * (h % 2) + 64)

                def key_query(b, kk, qq, h):
                    r, hb = head_rows(h), h // 2
                    mm(b[:, 0:SEQ], kk[r, hb, 0:P], qq[r, hb, :], start=True, stop=True)
                    return mm(b[:, SEQ:TRI], kk[r, hb, P:SEQ], qq[r, hb, P:SEQ], start=True, stop=True)

                pe.wait_ge(*at(l, "qkb_ready", 4))
                for n in range(NH + 2):
                    if n < NH:
                        b = take("z", n)
                        key_query(b, kbT, qbT, n).then_inc(S["bank_full"], 1)
                    if 1 <= n < NH + 1:
                        h = n - 1
                        b = take("cum", h)
                        pe.wait_ge(*at(l, "sp_ready", h + 1))
                        e = ln[:, h % 2, :]
                        mm(b[:, 0:SEQ], later, e[:, 0:SEQ], start=True, stop=False)
                        mm(b[:, P:SEQ], ones[:, :], e[:, SEQ:TRI], start=False, stop=True)
                        mm(b[:, SEQ:TRI], later, e[:, SEQ:TRI], start=True, stop=True).then_inc(S["bank_full"], 1)
                    if n >= 3 and n % 2 == 1:
                        m = (n - 3) // 2
                        b = take("ob", m)
                        if m == 0:
                            pe.wait_ge(*at(l, "vb_ready", 2))
                        for h in (2 * m, 2 * m + 1):
                            pe.wait_ge(*at(l, "a_ready", h + 1))
                            a = aw[:, h % 4, :]
                            r = head_rows(h)
                            mm(b[r, 0:SEQ], vb_s[:, 0, h * HD:(h + 1) * HD], a[:, 0:SEQ], start=True, stop=False)
                            ins = mm(b[r, P:SEQ], vb_s[:, 1, h * HD:(h + 1) * HD], a[:, SEQ:TRI], start=False, stop=True)
                        ins.then_inc(S["bank_full"], 1)
                    if n < 4:
                        if n % 2 == 0:
                            w = chunk_in(c)
                        b = take("vc", n)
                        project(b, 0, w, 0, 512, n % 2).then_inc(S["bank_full"], 1)
                    elif n < 8:
                        if n % 2 == 0:
                            w = chunk_in(c)
                        b = take("gc", n - 4)
                        project(b, 0, w, 0, 512, n % 2).then_inc(S["bank_full"], 1)
                    if n < 8 and n % 2:
                        chunk_done()
                        c += 1

                for n in range(2 * NH + 3):
                    if n < 2 * NH:
                        i, h = n // NH, n % NH
                        b = take("sc", n)
                        if n == 0:
                            pe.wait_ge(*at(l, "roped", 5))
                        r = head_rows(h)
                        mm(b[:, 0:P * (i + 1)], qaT[r, h // 2, i * P:(i + 1) * P], kT[r, 0:P * (i + 1)], start=True,
                           stop=True).then_inc(S["bank_full"], 1)
                    if 2 <= n < 2 * NH + 2:
                        m = n - 2
                        b = take("pT", m)
                        pe.wait_ge(*at(l, "pn_ready", m + 1))
                        for a in range(m // NH + 1):
                            ins = pe.transpose(b[:, a * P:(a + 1) * P], sm[:, m % 3, a * P:(a + 1) * P], ident)
                        ins.then_inc(S["bank_full"], 1)
                    if n >= 4 and n % 2 == 0:
                        o = (n - 4) // 2
                        i = o // PAIRS
                        b = take("oa", o)
                        if o == 0:
                            pe.wait_ge(*at(l, "vA_ready", 1))
                        for m in (2 * o, 2 * o + 1):
                            pe.wait_ge(*at(l, "pTs_ready", m + 1))
                            for a in range(i + 1):
                                ins = mm(b[head_rows(m), 0:P], vA[:, a, :], pTs[:, m % 4, a * P:(a + 1) * P],
                                         start=(a == 0), stop=(a == i))
                        ins.then_inc(S["bank_full"], 1)
                    if n < 12:
                        if n % 2 == 0:
                            w = chunk_in(c)
                        project_T(("gate", n), w, 256 * (n % 2), 2)
                        if n % 2:
                            chunk_done()
                            c += 1

                pe.wait_ge(*at(l, "roped", 9))
                pe.wait_ge(*at(l, "vc_ready", 4))
                for n in range(NH + 1):
                    if n < NH:
                        b = take("ret", n)
                        key_query(b, kcT, qcT, n).then_inc(S["bank_full"], 1)
                    if n >= 1:
                        h = n - 1
                        b = take("oc", h)
                        pe.wait_ge(*at(l, "rw_ready", h + 1))
                        s = rw[:, h % 2, :]
                        v0, v1 = (vc_s[:, i, h * CV:(h + 1) * CV] for i in range(TT))
                        mm(b[:, 0:CV], s[:, 0:P], v0, start=True, stop=True)
                        mm(b[:, CV:2 * CV], s[:, P:SEQ], v0, start=True, stop=False)
                        mm(b[:, CV:2 * CV], s[:, SEQ:TRI], v1, start=False, stop=True).then_inc(S["bank_full"], 1)
                transposes("ocT", [("ocg_ready", 2)])
                pe.wait_ge(*at(l, "ocT_ready", 4))
                pe.wait_ge(*at(l, "oa_ready", 8))
                pe.wait_ge(*at(l, "ob_ready", 4))

                for j in range(KD):
                    if j % 4 == 0:
                        wab, wc = chunk_in(c), chunk_in(c + 1)
                    cols = slice(P * (j % 4), P * (j % 4) + P)
                    b = take("yab", j)
                    for a, src in enumerate((oaT, obT)):
                        for k in range(4):
                            ins = mm(b[:, a * SEQ:(a + 1) * SEQ], wab[:, 4 * a + k, cols], src[:, k, :], start=(k == 0),
                                     stop=(k == 3))
                    ins.then_inc(S["bank_full"], 1)
                    b = take("yc", j)
                    for k in range(KD):
                        ins = mm(b[:, 0:SEQ], wc[:, k, cols], ocT(k), start=(k == 0), stop=(k == KD - 1))
                    ins.then_inc(S["bank_full"], 1)
                    if j % 4 == 3:
                        chunk_done()
                        chunk_done()
                        c += 2
                pe.wait_ge(*at(l, "mT_ready", 8))
                for hf in range(2):
                    w = chunk_in(c)
                    for i in range(TT):
                        b = take("y", hf, i)
                        for j in range(KD):
                            ins = mm(b[:, :], mT(j)[:, i * P:(i + 1) * P], w[:, j, :], start=(j == 0), stop=(j == KD - 1))
                        ins.then_inc(S["bank_full"], 1)
                    chunk_done()
                    c += 1
                assert c == NCH
                transposes("hT", [("xn_ready", 4)])
                pe.wait_ge(*at(l, "hT_ready", 8))
                b = take("rt")
                for i in range(TT):
                    for k in range(KD):
                        ins = mm(b[:, i * NE:(i + 1) * NE], hT[:, k, i * P:(i + 1) * P], wrt[:, k, :], start=(k == 0),
                                 stop=(k == KD - 1))
                ins.then_inc(S["bank_full"], 1)
                assert order[0] == NU

                for b in range(NB):
                    pe.wait_ge(bank_free[b], l * USES[b] + USES[b] + 1)
                q0 = l * NEX

                def up(q, slot, turn, i):
                    if i == 0:
                        pe.wait_ge(w13_full[slot], turn * 32)
                    pe.wait_ge(S["hid_ready"], q * TT + i + 1)
                    for k in range(KD):
                        ins = mm(psums[i][:, :].rearrange("p (j n) -> p j n", j=2), hT[:, k, i * P:(i + 1) * P],
                                 w13[:, slot, :, k, :], start=(k == 0), stop=(k == KD - 1))
                    ins.then_inc(S["h_ready"], 1)
                    if i == 1:
                        pe.wait_ge(S["h_ready"], (q + 1) * TT)
                        pe.sem_inc(S["w13_used"], 1)

                def turn_hidden(q, buf):
                    pe.wait_ge(S["hid_ready"], (q + 1) * TT + TT)
                    pe.wait_ge(S["eTs_ready"], q + 1)
                    for j in range(2):
                        for i in range(TT):
                            ins = pe.transpose(psums[2][:, j * SEQ + i * P:j * SEQ + (i + 1) * P],
                                               hid[:, buf, i, j:ED:2], ident)
                    ins.then_inc(S["eT_ready"], 1)

                def down(q, slot, turn, last):
                    pe.wait_ge(w2_full[slot], turn * 16)
                    pe.wait_ge(S["eTs_ready"], q + 2)
                    for i in range(TT):
                        for hf in range(2):
                            for j in range(2):
                                ins = mm(psums[4 + 2 * i + hf][:, :], eTs[:, j, i * P:(i + 1) * P],
                                         w2s[:, slot, j, hf * 512:hf * 512 + 512], start=False, stop=(last and j == 1),
                                         skip_group_check=True)
                    ins.then_inc(S["w2_used"], 1)

                for n in range(4):
                    mm(psums[4 + n][:, :], zeros[0:1, 0:P], ones32[0:1, 0:1].to_broadcast([1, 512]), start=True, stop=False, skip_group_check=True)
                T0 = NE // NW
                up(q0, 0, l * (T0 + 1) + 1, 0)
                up(q0, 0, l * (T0 + 1) + 1, 1)
                with pe.Fori(0, NE // NW) as r:
                    for s in range(NW):
                        q = q0 + (r * NW + s)
                        t = (s + 1) % NW
                        this_turn = l * (T0 + (s == 0)) + r + 1
                        next_turn = l * (T0 + (t == 0)) + r + 1 + (t == 0)
                        up(q + 1, t, next_turn, 0)
                        turn_hidden(q, s % 2)
                        up(q + 1, t, next_turn, 1)
                        down(q, s, this_turn, False)
                turn_hidden(q0 + NE, 0)
                down(q0 + NE, 0, l * (T0 + 1) + T0 + 1, True)
                pe.wait_ge(S["w2_used"], q0 + NEX + NW)
                pe.sem_inc(S["yacc_ready"], 1)


_INS = ["x", "c", "positions", "ada_w", "ada_b", "g_pre_mix", "g_post_mix", "g_pre_ffn", "g_post_ffn", "w_in", "g_kv",
        "w_uk", "w_uv", "g_ret", "w_o_a", "w_o_b", "w_o_c", "w_out", "w_router", "router_bias", "w1", "w3", "w2",
        "ws1", "ws3", "ws2"]


def kernel(**inputs):
    import concourse.bacc as _bacc
    from concourse.bass_utils import run_bass_kernel_spmd as _run

    nc = _bacc.Bacc("TRN2", target_bir_lowering=False, num_devices=1)
    arrays = {name: np.ascontiguousarray(inputs[name]) for name in _INS}
    arrays["fixed"], arrays["decay"] = mixer_constants()
    args = {name: nc.dram_tensor(f"in_{name}", a.shape, mybir.dt.from_np(a.dtype), kind="ExternalInput").ap()
            for name, a in arrays.items()}
    args["out"] = nc.dram_tensor("out_0", (1, SEQ, D), F32, kind="ExternalOutput").ap()
    build(nc, **args)
    r = _run(nc, [{f"in_{name}": a for name, a in arrays.items()}], core_ids=[0])
    return r.results[0]["out_0"]
```

```python
from contextlib import ExitStack

import concourse.bass as bass
import numpy as np
from concourse import mybir

F32 = mybir.dt.float32
I32 = mybir.dt.int32
ALU = mybir.AluOpType
ACT = mybir.ActivationFunctionType
AX = mybir.AxisListType.X

P = 128
D = 1024
SEQ = 256
DEPTH = 2
TT = SEQ // P
KD = D // P
EPS = 1e-6
HD = 64
NH = 8
KVL = 256
IDXH = 4
TOPK = 64
CHUNK = 64
CV = 128
NE = 64
NG = 8
EG = NE // NG
TOPG = 4
ED = 256
ROUTED_SCALE = 2.5
BIG = 1e30
GONE = -3e38
GONE_T = -2e38
TRI = SEQ + P

IN = dict(qa=0, ckv=512, iq=768, ik=1024, iw=1088, qb=1092, kb=1604, vb=2116, qc=2628, kc=3140, vc=3652,
          gc=4676, gates=5700)

NS = 3
CHUNKS = ([("ada", n) for n in range(12)]
          + [("in", IN["ckv"], 256), ("in", IN["iq"], 324), ("in", IN["qa"], 512), ("in", IN["qb"], 512),
             ("in", IN["kb"], 512), ("in", IN["vb"], 512), ("in", IN["qc"], 512), ("in", IN["kc"], 512),
             ("in", IN["vc"], 512), ("in", IN["vc"] + 512, 512), ("in", IN["gc"], 512), ("in", IN["gc"] + 512, 512)]
          + [("in", IN["gates"] + 512 * n, 512) for n in range(6)]
          + [("oab", 0), ("oc", 0), ("oab", 1), ("oc", 1), ("out", 0), ("out", 1)])
NCH = len(CHUNKS)
assert NCH % NS == 0

NB = 8
PAIRS = NH // 2


def plan_units():
    u = []
    for g in range(7):
        if g < 6:
            u += [("ada", 2 * g), ("ada", 2 * g + 1)]
        if g >= 1:
            n = 2 * (g - 1)
            u += [("gt", n), ("gt", n + 1)] if n in (4, 10) else [("mod", n)]
    u += [("xT", m) for m in range(4)]
    u += [("ckv",), ("iq",), ("ik",), ("iw",), ("qa", 0), ("qa", 1), ("ckvT",), ("kv",)]
    u += [("lg", i, h) for i in range(TT) for h in range(IDXH)]
    u += [("qb", 0), ("qb", 1), ("kb", 0), ("kb", 1), ("vb", 0), ("vb", 1)]
    u += [("qc", 0), ("qc", 1), ("kc", 0), ("kc", 1)]
    for n in range(NH + 2):
        if n < NH:
            u += [("z", n)]
        if 1 <= n < NH + 1:
            u += [("cum", n - 1)]
        if n >= 3 and n % 2 == 1:
            u += [("ob", (n - 3) // 2)]
        if n < 4:
            u += [("vc", n)]
        elif n < 8:
            u += [("gc", n - 4)]
    for n in range(2 * NH + 3):
        if n < 2 * NH:
            u += [("sc", n)]
        if 2 <= n < 2 * NH + 2:
            u += [("pT", n - 2)]
        if n >= 4 and n % 2 == 0:
            u += [("oa", (n - 4) // 2)]
        if n < 12:
            u += [("gate", n)]
    for n in range(NH + 1):
        if n < NH:
            u += [("ret", n)]
        if n >= 1:
            u += [("oc", n - 1)]
    u += [("ocT", m) for m in range(4)]
    for j in range(KD):
        u += [("yab", j), ("yc", j)]
    u += [("y", h, i) for h in range(2) for i in range(TT)]
    u += [("hT", m) for m in range(4)]
    u += [("rt",), ("rank",), ("over",)]
    return u


UNITS = plan_units()
UNIT = {name: n for n, name in enumerate(UNITS)}
NU = len(UNITS)
USES = [len(range(b, NU, NB)) for b in range(NB)]
NEX = NE + 1
NW = 4
SLOTS = P // 2
NP = NE // 2
NT = NEX * TT
UNPICKED = 1000.0

TOTAL = dict(
    bank_full=NU, chunk_used=len(CHUNKS), layer_done=1, params=16 * 13, decay=32,
    ada_copied=12, mod_done=8, ms_ready=6, rsq_raw=6, rms_ready=2, xn_ready=4, hT_ready=8,
    ckv_copied=1, ckv_scaled=1, ckvT_ready=1, vA_ready=1, rope_mul=9, roped=9, iw_ready=1, relu_ready=8, lg_used=8,
    sel_ready=2, qkb_ready=4, vb_ready=2, vc_ready=4, gc_ready=4, gate_ready=12,
    zs_ready=8, ln_ready=8, zb_ready=8, sp_ready=8, w_ready=8, a_ready=8, ob_ready=4,
    sm_ready=16, p_ready=16, rinv_ready=16, pn_ready=16, pTs_ready=16, oa_ready=8,
    rw_ready=8, osb_ready=8, ocn_ready=2, ocg_ready=2, ocT_ready=4,
    tab_ready=8, tc_ready=8, mT_ready=8, y_ready=4, dx_ready=4, x_ready=4,
    scores_ready=1, mask_ready=1, over_ready=1, table_ready=1, split_ready=2,
    hot_built=NP, sel_built=NP, xg_full=NP, xg0_ready=NP, xg1_ready=NP, h_full=NP, silu_ready=NP, hid_ready=NP, turned=NP,
    eT_ready=NP, selT_ready=NP, o_full=NP, o0_ready=NP, o1_ready=NP, w13_used=NP + 1, w2_used=NP + 1,
    yacc_ready=2, y2_ready=4,
    vector_chain=294, scalar_chain=127, gpsimd_chain=8,
)


def mixer_constants():
    half = HD // 2
    inv = np.float32(10000.0) ** (-np.arange(half, dtype=np.float32) / np.float32(half))
    p = np.arange(P)
    col = np.zeros((P, 4), np.float32)
    col[:, 0] = inv.astype(np.float32)[p % half]
    col[:, 1] = np.where(p % HD < half, -1.0, 1.0)
    ident = np.eye(P, dtype=np.float32)
    later = (p[:, None] >= p[None, :]).astype(np.float32)
    t = np.arange(SEQ)
    key0, key1 = p[:, None], p[:, None] + P
    causal = np.concatenate([key0 < t[None, :], key1 < t[None, P:]], 1)
    earlier = (p[:, None] < p[None, :]).astype(np.float32)
    slots = np.broadcast_to(np.arange(SLOTS, dtype=np.float32), (P, SLOTS))
    causal_neg = np.where(causal, 0.0, -BIG)
    adm = np.zeros((P, TT, SEQ), np.float32)
    for i in range(TT):
        adm[:, i, :] = np.where(t[None, :] // CHUNK <= (p[:, None] + i * P) // CHUNK, 0.0, -BIG)
    dec = np.zeros((P, NH, TRI), np.float64)
    for h in range(NH):
        lg = np.log(1.0 - 2.0 ** (-5.0 - h))
        for keys, q, c0 in ((p, t, 0), (p + P, t[P:], SEQ)):
            k, a = keys[:, None], q[None, :]
            inner = np.exp(lg * np.abs(k - a))
            cross = np.exp(lg * ((a % CHUNK + 1) + CHUNK * (a // CHUNK - k // CHUNK - 1) + (CHUNK - 1 - k % CHUNK)))
            w = np.where(k // CHUNK == a // CHUNK, inner, np.where(k // CHUNK < a // CHUNK, cross, 0.0))
            dec[:, h, c0:c0 + len(q)] = w * HD ** -0.5
    fixed = np.concatenate([ident, later, col, causal, causal_neg, adm.reshape(P, -1), earlier, slots], 1).astype(np.float32)
    return np.ascontiguousarray(fixed), np.ascontiguousarray(dec.reshape(P, -1).astype(np.float32))


def build(nc, x, c, positions, ada_w, ada_b, g_pre_mix, g_post_mix, g_pre_ffn, g_post_ffn, w_in, g_kv, w_uk, w_uv,
          g_ret, w_o_a, w_o_b, w_o_c, w_out, w_router, router_bias, w1, w3, w2, ws1, ws3, ws2, fixed, decay, out,
          depth=DEPTH, dbg=None):
    ctx = ExitStack()
    with ctx:
        def sb(name, shape, dt=F32):
            return ctx.enter_context(nc.sbuf_tensor(name, shape, dt))

        def sem(name):
            return ctx.enter_context(nc.semaphore(name))

        M = sb("M", [P, 24576])
        wring = M[:, 0:NS * 4096].rearrange("p (s k n) -> p s k n", s=NS, k=KD)
        gT = M[:, 12288:18432].rearrange("p (b t) -> p b t", b=24)
        dec = M[:, 18432:21504].rearrange("p (h t) -> p h t", h=NH)
        qcT = M[:, 21504:22528].rearrange("p (b t) -> p b t", b=4)
        kcT = M[:, 22528:23552].rearrange("p (b t) -> p b t", b=4)
        vb_s = M[:, 23552:24576].rearrange("p (i n) -> p i n", i=TT)
        w13 = M[:, 0:NW * 4096].rearrange("p (s j k n) -> p s j k n", s=NW, j=2, k=KD)
        w2s = M[:, 16384:24576].rearrange("p (s j n) -> p s j n", s=NW, j=2)
        x_sb = sb("x_sb", [P, TT, D])
        hT = sb("hT", [P, KD, SEQ])
        rows = sb("rows", [P, TT, D])
        fix = sb("fix", [P, 260 + 2 * TRI + TT * SEQ + P + SLOTS])
        ident, later = fix[:, 0:128], fix[:, 128:256]
        invf, rsign = fix[:, 256:257], fix[:, 257:258]
        cm01, cmneg = fix[:, 260:260 + TRI], fix[:, 260 + TRI:260 + 2 * TRI]
        earlier = fix[:, 260 + 2 * TRI + TT * SEQ:][:, 0:P]
        slot_no = fix[:, 260 + 2 * TRI + TT * SEQ + P:]
        adm = fix[:, 260 + 2 * TRI:260 + 2 * TRI + TT * SEQ].rearrange("p (i t) -> p i t", i=TT)
        ones = sb("ones", [P, P])
        zeros = sb("zeros", [1, P])
        ones32 = sb("ones32", [P, P])
        cosT = sb("cosT", [P, SEQ])
        sinT = sb("sinT", [P, SEQ])
        c_col = sb("c_col", [P, KD])
        c_rep = sb("c_rep", [P, KD, 32])
        gtg = sb("gtg", [P, 2, D])
        modc = sb("modc", [P, 4, KD])
        gpre = sb("gpre", [P, 2, KD])
        adabc = sb("adabc", [P, 4, KD])
        gkv_c = sb("gkv_c", [P, 2])
        gret_c = sb("gret_c", [P, KD])
        rbias = sb("rbias", [P, NE])
        wuk = sb("wuk", [P, 2, HD])
        wuv = sb("wuv", [P, 2, HD])
        wrt = sb("wrt", [P, KD, NE])
        ms, rs0, rs, rt1 = (sb(f"norm_{n}", [P, 16]) for n in ("ms", "raw", "r", "t"))
        part = sb("part", [P, 4])
        qbT = sb("qbT", [P, 4, SEQ])
        kbT = sb("kbT", [P, 4, SEQ])
        qaT = sb("qaT", [P, 4, SEQ])
        vc_s = sb("vc_s", [P, TT, D])
        gcs = sb("gcs", [P, TT, D])
        oaT = sb("oaT", [P, 4, SEQ])
        obT = sb("obT", [P, 4, SEQ])
        iqT = sb("iqT", [P, 2, SEQ])
        ikT = sb("ikT", [P, SEQ])
        kT = sb("kT", [P, SEQ])
        vA = sb("vA", [P, TT, HD])
        iw_s = sb("iw_s", [P, TT, IDXH])
        ckv_s = sb("ckv_s", [P, TT, KVL])
        ckvT = sb("ckvT", [P, 2, SEQ])
        selb = sb("selb", [P, TT, SEQ])
        top8 = sb("top8", [P, 8])
        nmx = sb("nmx", [P, 3])
        rsum = sb("rsum", [P, 3])
        rinv = sb("rinv", [P, 3])
        bst = sb("bst", [P, 2 * NH, 6])
        mv = sb("mv", [P, 2 * NH, 2])
        scr = sb("scr", [P, 3072])
        rsc = sb("rsc", [P, TT, NE])
        rsel = sb("rsel", [P, TT, NE])
        rwk = sb("rwk", [P, TT, NE])
        gsc = sb("gsc", [P, NG])
        g8 = sb("g8", [P, NG, 8])
        gate = sb("gate", [P, TT, NE])
        gate_over = sb("gate_over", [P, TT, NEX])
        steps_done = sb("steps_done", [1, 1])
        def flat2(b):
            return b[:, :, :].rearrange("p a n -> p (a n)")

        adaS = vc_s[:, :, :].rearrange("p i (a n) -> p (i a) n", a=2)
        gpost = gcs
        gtb = [b[0:1, :, :].rearrange("p a n -> p (a n)") for b in (qbT, kbT)]
        rp = scr[:, 0:2048].rearrange("p (b a n) -> p b a n", b=2, a=2)
        lr = scr[:, 2048:3072].rearrange("p (b t) -> p b t", b=4)
        zs = scr[:, 0:768].rearrange("p (b n) -> p b n", b=2)
        ln = scr[:, 768:1536].rearrange("p (b n) -> p b n", b=2)
        aw = scr[:, 1536:3072].rearrange("p (b n) -> p b n", b=4)
        sm = scr[:, 0:768].rearrange("p (b n) -> p b n", b=3)
        pTs = scr[:, 768:1792].rearrange("p (b n) -> p b n", b=4)
        rw = scr[:, 0:768].rearrange("p (b n) -> p b n", b=2)
        tab = scr[:, 0:1024].rearrange("p (b a n) -> p b a n", b=2, a=2)
        tc = scr[:, 1024:1536].rearrange("p (b n) -> p b n", b=2)
        dx = scr[:, 0:2048].rearrange("p (b n) -> p b n", b=2)
        junk = scr[:, 2048:3072]
        BF = mybir.dt.bfloat16
        rank = ckv_s[:, :, 0:NE]
        over = ckv_s[:, :, NE:2 * NE]
        flags = selb[0:1, 0, 0:NT]
        steps_f = selb[0:1, 1, 0:NT]
        steps_n = qaT[0:1, 0, 0:NT].bitcast(I32)
        pair_f = qaT[0:1, 2, 0:NP]
        pair_any = qaT[0:1, 1, 0:NP].bitcast(I32)
        xs = [gcs[:, 0, :].bitcast(BF), gcs[:, 1, :].bitcast(BF), vc_s[:, 0, :].bitcast(BF)]
        xs = [v.rearrange("p (i n) -> p i n", i=TT) for v in xs]
        rest = flat2(oaT)
        picks = scr[:, 0:256].bitcast(BF).rearrange("p (b i n) -> p b i n", b=2, i=TT)
        selw = scr[:, 256:768].rearrange("p (b i n) -> p b i n", b=2, i=TT)
        esl = scr[:, 768:1024]
        hid = scr[:, 1024:1280]
        eTs = scr[:, 1280:1536].rearrange("p (j t) -> p j t", j=2)
        selT = scr[:, 1536:1792].rearrange("p (i t) -> p i t", i=TT)
        dsl, dhid = scr[:, 1792:2048], scr[:, 2048:2304]
        deT = scr[:, 2304:2560].rearrange("p (j t) -> p j t", j=2)
        xg = flat2(qbT).rearrange("p (k t) -> p k t", k=KD)
        og = flat2(kbT)

        def ocT(k):
            return (qcT, kcT)[k // 4][:, k % 4, :]

        def mT(j):
            return (qbT, kbT)[j // 4][:, j % 4, :]

        psums = [ctx.enter_context(nc.psum_tensor(f"bank{b}", [P, 512], F32)) for b in range(8)]

        S = {name: sem(name) for name in TOTAL}
        D_h, D_silu, D_hid, D_T, D_eT = (sem(n) for n in ("dense_h", "dense_silu", "dense_hid", "dense_turned",
                                                          "dense_eT"))
        slot_full = [sem(f"slot_full{n}") for n in range(NS)]
        w13_full = [sem(f"w13_full{n}") for n in range(2)]
        w2_full = [sem(f"w2_full{n}") for n in range(2)]
        bank_free = [sem(f"bank_free{n}") for n in range(NB)]
        fixed_loaded, x_loaded, pos_loaded, angles, sincos, csig, setup, out_stored = (
            sem(n) for n in ("fixed_loaded", "x_loaded", "pos_loaded", "angles", "sincos", "csig", "setup", "out_stored"))
        setup_chain = sem("setup_chain")
        waits_apart = sem("waits_apart")

        def at(l, name, n):
            return S[name], l * TOTAL[name] + n

        def full(l, unit):
            return S["bank_full"], l * NU + UNIT[unit] + 1

        def bank(unit):
            return psums[UNIT[unit] % NB]

        def freed(unit):
            return bank_free[UNIT[unit] % NB]

        def flat(b):
            return b.rearrange("p a n -> p (a n)")

        def apart(eng):
            eng.sem_inc(waits_apart, 1)

        class Chain:

            def __init__(self, eng, name):
                self.eng, self.name, self.n = eng, name, 0

            def link(self, l, ins):
                self.n += 1
                ins.then_inc(S[self.name], 1)
                self.eng.wait_ge(S[self.name], l * TOTAL[self.name] + self.n)

        def dense_steps(eng, pair, step):
            with eng.If(eng.value_load(pair_any[0:1, bass.ds(pair, 1)], min_val=0, max_val=2 * TT) > 0):
                for ex in range(2):
                    for i in range(TT):
                        at_table = (2 * pair + ex) * TT + i
                        v = eng.value_load(steps_n[0:1, bass.ds(at_table, 1)], min_val=0, max_val=DEPTH * NT)
                        with eng.If(v > 0):
                            step(v, 2 * pair + ex, ex, i)
                        eng.sem_inc(waits_apart, 1)
            eng.sem_inc(waits_apart, 1)

        def shared_steps(eng, step):
            for i in range(TT):
                v = eng.value_load(steps_n[0:1, NE * TT + i:NE * TT + i + 1], min_val=1, max_val=DEPTH * NT)
                step(v, NE, 0, i)

        block = ctx.enter_context(nc.Block())

        @block.sync
        def _(sp):
            sp.dma_start(fix[:, :], fixed).then_inc(fixed_loaded, 16)
            for i in range(TT):
                sp.dma_start(x_sb[:, i, :], x[0, i * P:(i + 1) * P, :]).then_inc(x_loaded, 16)
            sp.dma_start(c_col[:, :], c[0, :].rearrange("(p k) -> p k", k=KD)).then_inc(x_loaded, 16)

            def chunk(l, n):
                slot = n % NS
                if n < NS:
                    sp.wait_ge(S["w13_used"], l * (NP + 1) + 2)
                else:
                    sp.wait_ge(*at(l, "chunk_used", n - NS + 1))
                apart(sp)
                kind = CHUNKS[n]
                w = wring[:, slot]
                if kind[0] == "ada":
                    sp.dma_start(w, ada_w[l, :, 512 * kind[1]:512 * kind[1] + 512].rearrange("(p k) n -> p k n", k=KD))\
                      .then_inc(slot_full[slot], 32)
                elif kind[0] == "in":
                    sp.dma_start(w[:, :, 0:kind[2]],
                                 w_in[l, :, kind[1]:kind[1] + kind[2]].rearrange("(p k) n -> p k n", k=KD))\
                      .then_inc(slot_full[slot], 32)
                elif kind[0] == "oab":
                    for b, src in enumerate((w_o_a, w_o_b)):
                        sp.dma_start(w[:, 4 * b:4 * b + 4, :],
                                     src[l, :, 512 * kind[1]:512 * kind[1] + 512].rearrange("(k p) n -> p k n", p=P))\
                          .then_inc(slot_full[slot], 16)
                elif kind[0] == "oc":
                    sp.dma_start(w, w_o_c[l, :, 512 * kind[1]:512 * kind[1] + 512].rearrange("(p k) n -> p k n", k=KD))\
                      .then_inc(slot_full[slot], 32)
                else:
                    sp.dma_start(w, w_out[l, :, 512 * kind[1]:512 * kind[1] + 512].rearrange("(k p) n -> p k n", p=P))\
                      .then_inc(slot_full[slot], 32)

            def expert(slot, a1, a3, a2, inc):
                if a1 is not None:
                    sp.dma_start(w13[:, slot, 0], a1.rearrange("(p k) n -> p k n", k=KD)).then_inc(w13_full[slot // 2], inc)
                    sp.dma_start(w13[:, slot, 1], a3.rearrange("(p k) n -> p k n", k=KD)).then_inc(w13_full[slot // 2], inc)
                else:
                    sp.dma_start(w2s[:, slot], a2.rearrange("(p j) n -> p j n", j=2)).then_inc(w2_full[slot // 2], inc)

            with sp.Fori(0, depth) as l:
                for n in range(NCH):
                    chunk(l, n)
                sp.wait_ge(*full(l, ("y", 0, 0)))
                apart(sp)
                sp.wait_ge(*at(l, "chunk_used", NCH))
                apart(sp)
                q0 = l * (NP + 1)
                with sp.Fori(0, NP // 2) as r:
                    for s in range(2):
                        pair = 2 * r + s
                        sp.wait_ge(S["w13_used"], q0 + pair + 1)
                        apart(sp)
                        for ex in range(2):
                            expert(2 * s + ex, w1[l, 2 * pair + ex, :, :], w3[l, 2 * pair + ex, :, :], None, 16)
                        sp.wait_ge(S["w2_used"], q0 + pair + 1)
                        apart(sp)
                        for ex in range(2):
                            expert(2 * s + ex, None, None, w2[l, 2 * pair + ex, :, :], 16)
                sp.wait_ge(S["w13_used"], q0 + NP + 1)
                apart(sp)
                expert(0, ws1[l, :, :], ws3[l, :, :], None, 32)
                sp.wait_ge(S["w2_used"], q0 + NP + 1)
                apart(sp)
                expert(0, None, None, ws2[l, :, :], 32)
            sp.wait_ge(S["layer_done"], depth + 1)
            for i in range(TT):
                sp.dma_start(out[0, i * P:(i + 1) * P, :], x_sb[:, i, :]).then_inc(out_stored, 16)
            sp.wait_ge(out_stored, 16 * TT)

        @block.gpsimd
        def _(pool):
            chain = Chain(pool, "gpsimd_chain")
            pos_i = obT[:, 0, :].bitcast(I32)
            pool.dma_start(pos_i, positions.to_broadcast([P, SEQ])).then_inc(pos_loaded, 16)
            pool.memset(ones[:, :], 1.0)
            pool.memset(ones32[:, :], 1.0 / 32)
            pool.memset(zeros[:, :], 0.0)
            pool.memset(gate_over[:, :, NE:NEX], 1.0)
            pool.memset(steps_done[:, :], 0.0).then_inc(setup, 1)

            with pool.Fori(0, depth) as l:
                pool.wait_ge(S["layer_done"], l + 1)
                col = lambda v: v.rearrange("(p k) -> p k", k=KD)
                row = lambda v: v.rearrange("(a n) -> a n", a=1)
                pool.dma_start(gpre[:, 0, :], col(g_pre_mix[l, :])).then_inc(S["params"], 16)
                pool.dma_start(gpre[:, 1, :], col(g_pre_ffn[l, :])).then_inc(S["params"], 16)
                pool.dma_start(adabc[:, 0:2, :], ada_b[l, 0:2 * D].rearrange("(v p k) -> p v k", v=2, k=KD))\
                    .then_inc(S["params"], 16)
                pool.dma_start(adabc[:, 2:4, :], ada_b[l, 3 * D:5 * D].rearrange("(v p k) -> p v k", v=2, k=KD))\
                    .then_inc(S["params"], 16)
                pool.dma_start(gtb[0], row(ada_b[l, 2 * D:3 * D])).then_inc(S["params"], 16)
                pool.dma_start(gtb[1], row(ada_b[l, 5 * D:6 * D])).then_inc(S["params"], 16)
                pool.dma_start(gpost[:, 0, :], row(g_post_mix[l, :]).to_broadcast([P, D])).then_inc(S["params"], 16)
                pool.dma_start(gpost[:, 1, :], row(g_post_ffn[l, :]).to_broadcast([P, D])).then_inc(S["params"], 16)
                pool.dma_start(gret_c[:, :], col(g_ret[l, :])).then_inc(S["params"], 16)
                pool.dma_start(rbias[:, :], row(router_bias[l, :]).to_broadcast([P, NE])).then_inc(S["params"], 16)
                pool.dma_start(wuk[:, :, :], w_uk[l, :, :].rearrange("(b p) n -> p b n", p=P)).then_inc(S["params"], 16)
                pool.dma_start(wuv[:, :, :], w_uv[l, :, :].rearrange("(b p) n -> p b n", p=P)).then_inc(S["params"], 16)
                pool.dma_start(wrt[:, :, :], w_router[l, :, :].rearrange("(p k) n -> p k n", k=KD))\
                    .then_inc(S["params"], 16)
                with nc.allow_non_contiguous_dma(reason="two columns"):
                    pool.dma_start(gkv_c[:, :], g_kv[l, :].rearrange("(b p) -> p b", p=P)).then_inc(S["decay"], 16)
                pool.dma_start(flat(dec), decay).then_inc(S["decay"], 16)

                for n, (dst, blocks) in enumerate(((iqT, 2), (ikT, 1), (qaT[:, 0:2], 2), (qaT[:, 2:4], 2), (kT, 1),
                                                   (qcT[:, 0:2], 2), (qcT[:, 2:4], 2), (kcT[:, 0:2], 2),
                                                   (kcT[:, 2:4], 2))):
                    pool.wait_ge(*at(l, "rope_mul", n + 1))
                    to = dst[:, :] if blocks == 1 else flat(dst[:, :, :])
                    w = blocks * SEQ
                    pool.tensor_tensor(to, rp[:, n % 2, 0, 0:w], rp[:, n % 2, 1, 0:w], ALU.add)\
                        .then_inc(S["roped"], 1)

                for h in range(NH):
                    pool.wait_ge(*at(l, "zs_ready", h + 1))
                    if h >= 4:
                        pool.wait_ge(*full(l, ("ob", (h - 4) // 2)))
                    pool.tensor_tensor(aw[:, h % 4, :], zs[:, h % 2, :], cmneg, ALU.add).then_inc(S["zb_ready"], 1)

                for n in range(2 * NH):
                    w = P * (n // NH + 1)
                    pool.wait_ge(*at(l, "rinv_ready", n + 1))
                    apart(pool)
                    pool.tensor_scalar(sm[:, n % 3, 0:w], sm[:, n % 3, 0:w], rinv[:, n % 3:n % 3 + 1], None, ALU.mult)\
                        .then_inc(S["pn_ready"], 1)

                for i in range(TT):
                    pool.wait_ge(*at(l, "ocn_ready", i + 1))
                    pool.wait_ge(*at(l, "gc_ready", 4))
                    pool.tensor_tensor(rows[:, i, :], rows[:, i, :], gcs[:, i, :], ALU.mult).then_inc(S["ocg_ready"], 1)

                for j in range(KD):
                    pool.wait_ge(*at(l, "tab_ready", j + 1))
                    chain.link(l, pool.tensor_tensor(mT(j), tab[:, j % 2, 0, :], tab[:, j % 2, 1, :], ALU.add))
                    pool.wait_ge(*at(l, "tc_ready", j + 1))
                    pool.tensor_tensor(mT(j), mT(j), tc[:, j % 2, :], ALU.add).then_inc(S["mT_ready"], 1)

                for n in range(2 * TT):
                    pool.wait_ge(*at(l, "dx_ready", n + 1))
                    i = n % TT
                    pool.tensor_tensor(x_sb[:, i, :], x_sb[:, i, :], dx[:, i, :], ALU.add).then_inc(S["x_ready"], 1)
            assert chain.n == TOTAL["gpsimd_chain"], chain.n

        @block.scalar
        def _(act):
            chain = Chain(act, "scalar_chain")
            act.wait_ge(angles, 1)
            act.activation(sinT[:, :], sinT[:, :], ACT.Sin)
            act.activation(cosT[:, :], cosT[:, :], ACT.Sin).then_inc(sincos, 1)
            act.wait_ge(x_loaded, 48)
            act.activation(c_col[:, :], c_col[:, :], ACT.Silu).then_inc(csig, 1)

            def rsqrt(l, n, w):
                act.wait_ge(*at(l, "ms_ready", n + 1))
                chain.link(l, act.activation(rs0[:, 0:w], ms[:, 0:w], ACT.Ln))
                act.activation(rs0[:, 0:w], rs0[:, 0:w], ACT.Exp, scale=-0.5).then_inc(S["rsq_raw"], 1)

            def normed_rows(l, n):
                act.wait_ge(*at(l, "rms_ready", n + 1))
                for i in range(TT):
                    act.activation(rows[:, i, :], x_sb[:, i, :], ACT.Copy, scale=rs[:, i:i + 1])\
                       .then_inc(S["xn_ready"], 1)

            def copy_out(l, unit, dst, src, name, func=ACT.Copy, scale=1.0):
                act.wait_ge(*full(l, unit))
                act.activation(dst, src, func, scale=scale).then_inc(S[name], 1)

            with act.Fori(0, depth) as l:
                for n in range(12):
                    act.wait_ge(*full(l, ("ada", n)))
                    chain.link(l, act.activation(adaS[:, n % 4, :], bank(("ada", n))[:, :], ACT.Copy))
                    act.sem_inc(S["ada_copied"], 1)
                    act.sem_inc(freed(("ada", n)), 1)
                rsqrt(l, 0, TT)
                normed_rows(l, 0)

                def take(unit, dst, src, name, func=ACT.Copy, scale=1.0):
                    act.wait_ge(*full(l, unit))
                    chain.link(l, act.activation(dst, src, func, scale=scale))
                    act.sem_inc(S[name], 1)
                    act.sem_inc(freed(unit), 1)

                two = lambda b: b[:, :].rearrange("p (a n) -> p a n", a=2)
                take(("ckv",), ckv_s[:, :, :], two(bank(("ckv",))), "ckv_copied")
                take(("iw",), iw_s[:, :, :], bank(("iw",))[:, 0:2 * IDXH].rearrange("p (i h) -> p i h", i=TT), "iw_ready")
                rsqrt(l, 1, TT)
                n = 0
                for i in range(TT):
                    w = P * (i + 1)
                    for h in range(IDXH):
                        if n >= 4:
                            act.wait_ge(*at(l, "lg_used", n - 3))
                        take(("lg", i, h), lr[:, n % 4, 0:w], bank(("lg", i, h))[:, 0:w], "relu_ready",
                             ACT.Relu, HD ** -0.5 * IDXH ** -0.5)
                        n += 1
                for name, dst in (("qb", qbT), ("kb", kbT)):
                    for m in range(2):
                        take((name, m), flat(dst[:, 2 * m:2 * m + 2, :]), bank((name, m))[:, :], "qkb_ready")
                for i in range(TT):
                    take(("vb", i), vb_s[:, i, :], bank(("vb", i))[:, :], "vb_ready")
                act.wait_ge(*at(l, "roped", 9))
                for n in range(NH + 2):
                    if n < NH:
                        z, e = zs[:, n % 2, :], ln[:, n % 2, :]
                        if n >= 2:
                            act.wait_ge(*full(l, ("cum", n - 2)))
                            act.wait_ge(*at(l, "zb_ready", n - 1))
                        take(("z", n), z, bank(("z", n))[:, 0:TRI], "zs_ready", ACT.Copy, HD ** -0.5)
                        chain.link(l, act.activation(e, z, ACT.Abs))
                        chain.link(l, act.activation(e, e, ACT.Exp, scale=-1.0))
                        act.activation(e, e, ACT.Ln, bias=1.0).then_inc(S["ln_ready"], 1)
                    if 1 <= n < NH + 1:
                        act.wait_ge(*at(l, "w_ready", n))
                        act.activation(aw[:, (n - 1) % 4, :], aw[:, (n - 1) % 4, :], ACT.Exp).then_inc(S["a_ready"], 1)
                    if n >= 3 and n % 2 == 1:
                        m = (n - 3) // 2
                        take(("ob", m), obT[:, m, :], bank(("ob", m))[:, 0:SEQ], "ob_ready")
                    if n < 4:
                        take(("vc", n), vc_s[:, n % 2, 512 * (n // 2):512 * (n // 2) + 512], bank(("vc", n))[:, :],
                             "vc_ready")
                    elif n < 8:
                        m = n - 4
                        take(("gc", m), gcs[:, m % 2, 512 * (m // 2):512 * (m // 2) + 512], bank(("gc", m))[:, :],
                             "gc_ready", ACT.Silu)
                for n in range(2 * NH + 3):
                    if n < 2 * NH:
                        w = P * (n // NH + 1)
                        act.wait_ge(*at(l, "sm_ready", n + 1))
                        act.activation(sm[:, n % 3, 0:w], sm[:, n % 3, 0:w], ACT.Exp, bias=nmx[:, n % 3:n % 3 + 1],
                                       accum_out=rsum[:, n % 3:n % 3 + 1]).then_inc(S["p_ready"], 1)
                    if 2 <= n < 2 * NH + 2:
                        m = n - 2
                        w = P * (m // NH + 1)
                        take(("pT", m), pTs[:, m % 4, 0:w], bank(("pT", m))[:, 0:w], "pTs_ready")
                    if n >= 4 and n % 2 == 0:
                        m = (n - 4) // 2
                        i, hb = m // PAIRS, m % PAIRS
                        take(("oa", m), oaT[:, hb, i * P:(i + 1) * P], bank(("oa", m))[:, 0:P], "oa_ready")
                    if n < 12:
                        take(("gate", n), flat(gT[:, 2 * n:2 * n + 2, :]), bank(("gate", n))[:, :], "gate_ready",
                             ACT.Sigmoid)
                for h in range(NH):
                    take(("oc", h), rows[:, :, h * CV:(h + 1) * CV],
                         bank(("oc", h))[:, 0:2 * CV].rearrange("p (i n) -> p i n", i=TT), "osb_ready")
                rsqrt(l, 2, 2 * NH)
                for m in range(4):
                    act.wait_ge(*full(l, ("ocT", m)))
                    for kk in range(2):
                        k = 2 * m + kk
                        chain.link(l, act.activation(ocT(k), bank(("ocT", m))[:, kk * SEQ:(kk + 1) * SEQ], ACT.Copy,
                                                     scale=gret_c[:, k:k + 1]))
                    act.sem_inc(S["ocT_ready"], 1)
                    act.sem_inc(freed(("ocT", m)), 1)
                for hf in range(2):
                    for i in range(TT):
                        take(("y", hf, i), rows[:, i, hf * 512:hf * 512 + 512], bank(("y", hf, i))[:, :], "y_ready")
                rsqrt(l, 3, TT)
                rsqrt(l, 4, TT)
                normed_rows(l, 1)
                take(("rt",), rsc[:, :, :], bank(("rt",))[:, 0:TT * NE].rearrange("p (i e) -> p i e", i=TT),
                     "scores_ready", ACT.Sigmoid)

                act.wait_ge(*at(l, "table_ready", 1))
                q0 = l * NP

                def gathered(q):
                    act.wait_ge(S["xg_full"], q + 1)
                    for k in range(4, KD):
                        ins = act.activation(xg[:, k, :], psums[1][:, (k - 4) * P:(k - 3) * P], ACT.Identity,
                                             scale=modc[:, 3, k:k + 1], bias=modc[:, 2, k:k + 1])
                    ins.then_inc(S["xg1_ready"], 1)

                def silu(q):
                    act.wait_ge(S["h_full"], q + 1)
                    act.activation(esl, psums[2][:, 0:ED], ACT.Silu).then_inc(S["silu_ready"], 1)

                def dense(v, e, ex, i):
                    act.wait_ge(D_h, v)
                    act.activation(dsl, psums[3][:, 0:ED], ACT.Silu).then_inc(D_silu, 1)
                    act.wait_ge(D_T, v)
                    act.activation(flat(deT), psums[3][:, 0:ED], ACT.Copy).then_inc(D_eT, 1)

                def pair_step(pair, ahead):
                    q = q0 + pair
                    if ahead:
                        gathered(q + 1)
                    act.wait_ge(S["turned"], q + 1)
                    act.activation(flat(eTs), psums[3][:, 0:ED], ACT.Copy).then_inc(S["eT_ready"], 1)
                    act.wait_ge(S["o_full"], q + 1)
                    act.activation(og[:, 512:D], psums[1][:, :], ACT.Copy).then_inc(S["o1_ready"], 1)
                    if ahead:
                        silu(q + 1)
                        dense_steps(act, pair + 1, dense)

                gathered(q0)
                silu(q0)
                dense_steps(act, 0, dense)
                with act.Fori(0, NP // 2 - 1) as r:
                    pair_step(2 * r, True)
                    pair_step(2 * r + 1, True)
                pair_step(NP - 2, True)
                pair_step(NP - 1, False)
                shared_steps(act, dense)
                act.wait_ge(*at(l, "yacc_ready", 2))
                for i in range(TT):
                    for hf in range(2):
                        act.activation(rows[:, i, hf * 512:hf * 512 + 512], psums[4 + 2 * i + hf][:, :], ACT.Copy)\
                           .then_inc(S["y2_ready"], 1)
                rsqrt(l, 5, TT)
            assert chain.n == TOTAL["scalar_chain"], chain.n

        @block.vector
        def _(dve):
            chain = Chain(dve, "vector_chain")
            for b in range(NB):
                dve.sem_inc(bank_free[b], 1)
            dve.sem_inc(S["layer_done"], 1)
            dve.sem_inc(S["w13_used"], 2)
            dve.sem_inc(S["w2_used"], 2)

            steps = [0]

            def once(ins):
                steps[0] += 1
                ins.then_inc(setup_chain, 1)
                dve.wait_ge(setup_chain, steps[0])

            dve.wait_ge(fixed_loaded, 16)
            dve.wait_ge(pos_loaded, 16)
            pos_f, ang, turns = (obT[:, n, :] for n in (1, 2, 3))
            once(dve.tensor_copy(pos_f, obT[:, 0, :].bitcast(I32)))
            once(dve.tensor_scalar(ang, pos_f, invf, None, ALU.mult))
            near = 1.5 * 2 ** 23
            c1 = 6.28125
            c2 = float(np.float32(2 * np.pi - c1))
            c2 = float(np.frombuffer((np.frombuffer(np.float32(c2).tobytes(), np.uint32) & 0xFFFFF000).tobytes(),
                                     np.float32)[0])
            c3 = float(np.float32(2 * np.pi - c1 - c2))
            for dst, quarter in ((sinT, 0.0), (cosT, 0.25)):
                once(dve.tensor_scalar(turns, ang, 1 / (2 * np.pi), quarter, ALU.mult, ALU.add))
                once(dve.tensor_scalar(turns, turns, near, near, ALU.add, ALU.subtract))
                once(dve.scalar_tensor_tensor(out=dst[:, :], in0=turns, scalar=-c1, in1=ang, op0=ALU.mult, op1=ALU.add))
                once(dve.scalar_tensor_tensor(out=dst[:, :], in0=turns, scalar=-c2, in1=dst[:, :], op0=ALU.mult,
                                              op1=ALU.add))
                once(dve.scalar_tensor_tensor(out=dst[:, :], in0=turns, scalar=-c3, in1=dst[:, :], op0=ALU.mult,
                                              op1=ALU.add))
                if quarter:
                    once(dve.tensor_scalar(dst[:, :], dst[:, :], np.pi / 2, None, ALU.add))
                pi = float(np.nextafter(np.float32(np.pi), np.float32(0)))
                once(dve.tensor_scalar(dst[:, :], dst[:, :], -pi, pi, ALU.max, ALU.min))
            dve.sem_inc(angles, 1)
            dve.wait_ge(setup, 1)
            dve.wait_ge(csig, 1)
            for k in range(KD):
                once(dve.tensor_scalar(c_rep[:, k, :], ones[:, 0:32], c_col[:, k:k + 1], None, ALU.mult))
            dve.wait_ge(sincos, 1)
            once(dve.tensor_scalar(sinT[:, :], sinT[:, :], rsign, None, ALU.mult))
            dve.sem_inc(setup, 1)

            with dve.Fori(0, depth) as l:
                link = lambda ins: chain.link(l, ins)

                def refine(n, w):
                    dve.wait_ge(*at(l, "rsq_raw", n + 1))
                    link(dve.tensor_tensor(rt1[:, 0:w], ms[:, 0:w], rs0[:, 0:w], ALU.mult))
                    link(dve.tensor_tensor(rt1[:, 0:w], rt1[:, 0:w], rs0[:, 0:w], ALU.mult))
                    link(dve.tensor_scalar(rt1[:, 0:w], rt1[:, 0:w], -0.5, 1.5, ALU.mult, ALU.add))
                    link(dve.tensor_tensor(rs[:, 0:w], rs0[:, 0:w], rt1[:, 0:w], ALU.mult))

                def mean_square(src, w, to):
                    link(dve.tensor_tensor_reduce(junk[:, 0:w], src, src, 1.0, 0.0, ALU.mult, ALU.add,
                                                  part[:, to:to + 1]))

                def to_ms(w):
                    link(dve.tensor_scalar(ms[:, 0:TT], part[:, 0:TT], 1.0 / w, EPS, ALU.mult, ALU.add))
                    dve.sem_inc(S["ms_ready"], 1)

                def prenorm(n, root, units):
                    for i in range(TT):
                        mean_square(x_sb[:, i, :], D, i)
                    to_ms(D)
                    refine(root, TT)
                    dve.sem_inc(S["rms_ready"], 1)
                    for m in range(4):
                        unit = (units, m)
                        dve.wait_ge(*full(l, unit))
                        for kk in range(2):
                            k = 2 * m + kk
                            link(dve.tensor_scalar(hT[:, k, :], bank(unit)[:, kk * SEQ:(kk + 1) * SEQ],
                                                   modc[:, 2 * n + 1, k:k + 1], modc[:, 2 * n, k:k + 1],
                                                   ALU.mult, ALU.add))
                        dve.sem_inc(S["hT_ready"], 1)
                        dve.sem_inc(freed(unit), 1)

                def rope(n, unit, blocks):
                    b = bank(unit)
                    dve.wait_ge(*full(l, unit))
                    if n >= 2:
                        dve.wait_ge(*at(l, "roped", n - 1))
                    for q in range(4):
                        o = 32 * (q ^ 1)
                        for a in range(blocks):
                            dve.tensor_tensor(rp[32 * q:32 * q + 32, n % 2, 0, a * SEQ:(a + 1) * SEQ],
                                              b[o:o + 32, a * SEQ:(a + 1) * SEQ], sinT[32 * q:32 * q + 32, :],
                                              ALU.mult)
                    for a in range(blocks):
                        ins = dve.tensor_tensor(rp[:, n % 2, 1, a * SEQ:(a + 1) * SEQ], b[:, a * SEQ:(a + 1) * SEQ],
                                                cosT[:, :], ALU.mult)
                    link(ins)
                    dve.sem_inc(S["rope_mul"], 1)
                    if unit != ("kv",):
                        dve.sem_inc(freed(unit), 1)

                dve.wait_ge(*at(l, "params", 13 * 16))
                for n in (0, 2, 4, 5, 6, 8, 10, 11):
                    if n in (4, 5, 10, 11):
                        g, hf = n // 6, n % 2
                        dve.wait_ge(*full(l, ("gt", n)))
                        link(dve.tensor_tensor(gtg[:, g, hf * 512:hf * 512 + 512], bank(("gt", n))[:, :],
                                               gpost[:, g, hf * 512:hf * 512 + 512], ALU.mult))
                        dve.sem_inc(freed(("gt", n)), 1)
                    else:
                        v = {0: 0, 2: 1, 6: 2, 8: 3}[n]
                        dve.wait_ge(*full(l, ("mod", n)))
                        link(dve.tensor_tensor(modc[:, v, :], bank(("mod", n))[:, 0:KD], adabc[:, v, :], ALU.add))
                        dve.sem_inc(freed(("mod", n)), 1)
                        if v % 2:
                            link(dve.scalar_tensor_tensor(out=modc[:, v, :], in0=modc[:, v, :], scalar=1.0,
                                                          in1=gpre[:, v // 2, :], op0=ALU.add, op1=ALU.mult))
                dve.wait_ge(x_loaded, 48)
                prenorm(0, 0, "xT")

                dve.wait_ge(*at(l, "ckv_copied", 1))
                for i in range(TT):
                    mean_square(ckv_s[:, i, :], KVL, i)
                to_ms(KVL)
                refine(1, TT)
                for i in range(TT):
                    link(dve.tensor_scalar(ckv_s[:, i, :], ckv_s[:, i, :], rs[:, i:i + 1], None, ALU.mult))
                dve.sem_inc(S["ckv_scaled"], 1)
                rope(0, ("iq",), 2)
                rope(1, ("ik",), 1)
                rope(2, ("qa", 0), 2)
                rope(3, ("qa", 1), 2)
                dve.wait_ge(*at(l, "decay", 32))
                dve.wait_ge(*full(l, ("ckvT",)))
                for b in range(2):
                    link(dve.tensor_scalar(ckvT[:, b, :], bank(("ckvT",))[:, b * SEQ:(b + 1) * SEQ], gkv_c[:, b:b + 1],
                                           None, ALU.mult))
                dve.sem_inc(S["ckvT_ready"], 1)
                dve.sem_inc(freed(("ckvT",)), 1)
                rope(4, ("kv",), 1)
                link(dve.tensor_copy(vA[:, :, :], bank(("kv",))[:, SEQ:SEQ + TT * HD].rearrange("p (i n) -> p i n", i=TT)))
                dve.sem_inc(S["vA_ready"], 1)
                dve.sem_inc(freed(("kv",)), 1)

                dve.wait_ge(*at(l, "iw_ready", 1))
                n = 0
                for i in range(TT):
                    w = P * (i + 1)
                    score = selb[:, i, 0:w]
                    for h in range(IDXH):
                        dve.wait_ge(*at(l, "relu_ready", n + 1))
                        link(dve.scalar_tensor_tensor(out=score, in0=lr[:, n % 4, 0:w],
                                                      scalar=iw_s[:, i, h:h + 1],
                                                      in1=adm[:, i, 0:w] if h == 0 else score,
                                                      op0=ALU.mult, op1=ALU.add))
                        dve.sem_inc(S["lg_used"], 1)
                        n += 1
                    for _ in range(TOPK // 8):
                        apart(dve)
                        link(dve.max(top8[:, :], score))
                        apart(dve)
                        link(dve.match_replace(score, top8[:, :], score, GONE))
                    link(dve.tensor_scalar(score, score, GONE_T, -1.0, ALU.is_le, ALU.add))
                    link(dve.tensor_scalar(score, score, BIG, None, ALU.mult))
                    dve.sem_inc(S["sel_ready"], 1)
                for n, (name, m) in enumerate((("qc", 0), ("qc", 1), ("kc", 0), ("kc", 1))):
                    rope(5 + n, (name, m), 2)

                for n in range(NH + 1):
                    if n < NH:
                        dve.wait_ge(*at(l, "ln_ready", n + 1))
                        z, e = zs[:, n % 2, :], ln[:, n % 2, :]
                        link(dve.scalar_tensor_tensor(out=e, in0=z, scalar=0.0, in1=e, op0=ALU.max, op1=ALU.add))
                        dve.tensor_tensor(e, e, cm01, ALU.mult).then_inc(S["sp_ready"], 1)
                    if n >= 1:
                        h = n - 1
                        dve.wait_ge(*full(l, ("cum", h)))
                        dve.wait_ge(*at(l, "zb_ready", h + 1))
                        link(dve.scalar_tensor_tensor(out=aw[:, h % 4, :], in0=bank(("cum", h))[:, 0:TRI], scalar=-1.0,
                                                      in1=aw[:, h % 4, :], op0=ALU.mult, op1=ALU.add))
                        dve.sem_inc(S["w_ready"], 1)
                        dve.sem_inc(freed(("cum", h)), 1)

                dve.wait_ge(*full(l, ("ob", PAIRS - 1)))
                for n in range(2 * NH + 1):
                    if n < 2 * NH:
                        i = n // NH
                        w = P * (i + 1)
                        dve.wait_ge(*full(l, ("sc", n)))
                        if n >= 3:
                            dve.wait_ge(*full(l, ("pT", n - 3)))
                        link(dve.scalar_tensor_tensor(out=sm[:, n % 3, 0:w], in0=bank(("sc", n))[:, 0:w],
                                                      scalar=HD ** -0.5, in1=selb[:, i, 0:w], op0=ALU.mult,
                                                      op1=ALU.add))
                        dve.sem_inc(freed(("sc", n)), 1)
                        dve.tensor_reduce(nmx[:, n % 3:n % 3 + 1], sm[:, n % 3, 0:w], AX, ALU.max, negate=True)\
                           .then_inc(S["sm_ready"], 1)
                    if n >= 1:
                        m = (n - 1) % 3
                        dve.wait_ge(*at(l, "p_ready", n))
                        dve.reciprocal(rinv[:, m:m + 1], rsum[:, m:m + 1]).then_inc(S["rinv_ready"], 1)

                dve.wait_ge(*full(l, ("oa", 2 * PAIRS - 1)))
                for n in range(NH + 1):
                    if n < NH:
                        dve.wait_ge(*full(l, ("ret", n)))
                        link(dve.tensor_tensor(rw[:, n % 2, :], bank(("ret", n))[:, 0:TRI], dec[:, n, :], ALU.mult))
                        dve.sem_inc(S["rw_ready"], 1)
                        dve.sem_inc(freed(("ret", n)), 1)
                    if n >= 1:
                        h = n - 1
                        dve.wait_ge(*at(l, "osb_ready", n))
                        for i in range(TT):
                            link(dve.bn_stats(bst[:, i * NH + h, :], rows[:, i, h * CV:(h + 1) * CV]))
                for m in range(TT * NH):
                    apart(dve)
                    link(dve.bn_aggr(mv[:, m, :], bst[:, m, :]))
                link(dve.tensor_scalar(ms[:, 0:TT * NH], mv[:, :, 1], EPS, None, ALU.add))
                dve.sem_inc(S["ms_ready"], 1)
                refine(2, TT * NH)
                for i in range(TT):
                    for h in range(NH):
                        m = i * NH + h
                        link(dve.tensor_scalar(rows[:, i, h * CV:(h + 1) * CV], rows[:, i, h * CV:(h + 1) * CV],
                                               mv[:, m, 0:1], rs[:, m:m + 1], ALU.subtract, ALU.mult))
                    dve.sem_inc(S["ocn_ready"], 1)

                dve.wait_ge(*at(l, "gate_ready", 12))
                for j in range(KD):
                    if j >= 2:
                        dve.wait_ge(*at(l, "mT_ready", j - 1))
                    dve.wait_ge(*full(l, ("yab", j)))
                    link(dve.tensor_tensor(tab[:, j % 2], bank(("yab", j))[:, :].rearrange("p (a n) -> p a n", a=2),
                                           gT[:, j:j + 9:8, :], ALU.mult))
                    dve.sem_inc(S["tab_ready"], 1)
                    dve.sem_inc(freed(("yab", j)), 1)
                    dve.wait_ge(*full(l, ("yc", j)))
                    link(dve.tensor_tensor(tc[:, j % 2, :], bank(("yc", j))[:, 0:SEQ], gT[:, 16 + j, :], ALU.mult))
                    dve.sem_inc(S["tc_ready"], 1)
                    dve.sem_inc(freed(("yc", j)), 1)

                def postnorm(n, root, name):
                    dve.wait_ge(*at(l, name, 4))
                    for i in range(TT):
                        mean_square(rows[:, i, :], D, i)
                    to_ms(D)
                    refine(root, TT)
                    for i in range(TT):
                        dve.scalar_tensor_tensor(out=dx[:, i, :], in0=rows[:, i, :], scalar=rs[:, i:i + 1],
                                                 in1=gtg[:, n, :], op0=ALU.mult, op1=ALU.mult)\
                           .then_inc(S["dx_ready"], 1)
                    dve.wait_ge(*at(l, "x_ready", TT * (n + 1)))

                postnorm(0, 3, "y_ready")
                prenorm(1, 4, "hT")

                dve.wait_ge(*at(l, "scores_ready", 1))
                for i in range(TT):
                    sel = rsel[:, i, :]
                    link(dve.tensor_tensor(sel, rsc[:, i, :], rbias[:, :], ALU.add))
                    for g in range(NG):
                        apart(dve)
                        link(dve.max(g8[:, g, :], rsel[:, i, g * EG:(g + 1) * EG]))
                    link(dve.tensor_tensor(gsc[:, :], g8[:, :, 0], g8[:, :, 1], ALU.add))
                    apart(dve)
                    link(dve.max(top8[:, :], gsc[:, :]))
                    link(dve.memset(top8[:, TOPG:8], 2 * GONE_T / 3))
                    apart(dve)
                    link(dve.match_replace(gsc[:, :], top8[:, :], gsc[:, :], GONE))
                    link(dve.tensor_scalar(gsc[:, :], gsc[:, :], GONE_T, -1.0, ALU.is_le, ALU.add))
                    link(dve.tensor_scalar(gsc[:, :], gsc[:, :], BIG, None, ALU.mult))
                    link(dve.tensor_tensor(sel.rearrange("p (g e) -> p g e", g=NG),
                                           sel.rearrange("p (g e) -> p g e", g=NG),
                                           gsc[:, :].unsqueeze(2).to_broadcast([P, NG, EG]), ALU.add))
                    apart(dve)
                    link(dve.max(top8[:, :], sel))
                    apart(dve)
                    link(dve.match_replace(sel, top8[:, :], sel, GONE))
                    link(dve.tensor_scalar(sel, sel, GONE_T, None, ALU.is_le))
                    link(dve.tensor_tensor_reduce(rwk[:, i, :], sel, rsc[:, i, :], 1.0, 0.0, ALU.mult, ALU.add,
                                                  part[:, i:i + 1]))
                    link(dve.reciprocal(part[:, 2 + i:3 + i], part[:, i:i + 1]))
                    link(dve.tensor_scalar(gate[:, i, :], rwk[:, i, :], part[:, 2 + i:3 + i], ROUTED_SCALE,
                                           ALU.mult, ALU.mult))
                dve.sem_inc(S["mask_ready"], 1)

                for i in range(TT):
                    left = rest[:, 0:D]
                    link(dve.tensor_copy(xs[0][:, i, :], rows[:, i, :]))
                    link(dve.tensor_tensor(left, rows[:, i, :], xs[0][:, i, :], ALU.subtract))
                    link(dve.tensor_copy(xs[1][:, i, :], left))
                    link(dve.tensor_tensor(left, left, xs[1][:, i, :], ALU.subtract))
                    link(dve.tensor_copy(xs[2][:, i, :], left))
                    dve.sem_inc(S["split_ready"], 1)

                dve.wait_ge(*full(l, ("rank",)))
                b = bank(("rank",))[:, 0:TT * NE].rearrange("p (i e) -> p i e", i=TT)
                link(dve.tensor_scalar(over[:, :, :], b, float(SLOTS), None, ALU.is_ge))
                link(dve.tensor_tensor(over, over, rsel[:, :, :], ALU.mult))
                dve.sem_inc(S["over_ready"], 1)
                link(dve.scalar_tensor_tensor(out=rank[:, :, :], in0=b, scalar=UNPICKED, in1=rsel[:, :, :], op0=ALU.add,
                                              op1=ALU.mult))
                dve.sem_inc(freed(("rank",)), 1)
                link(dve.tensor_scalar(rank[:, :, :], rank[:, :, :], UNPICKED, None, ALU.subtract))
                link(dve.tensor_tensor(gate_over[:, :, 0:NE], gate[:, :, :], over[:, :, :], ALU.mult))

                dve.wait_ge(*full(l, ("over",)))
                fl = flags[:, 0:NE * TT]
                link(dve.memset(flags[:, NE * TT:], 1.0))
                link(dve.tensor_scalar(fl.rearrange("p (e i) -> p i e", i=TT),
                                       bank(("over",))[0:1, 0:TT * NE].rearrange("p (i e) -> p i e", i=TT),
                                       1.0, None, ALU.min))
                dve.sem_inc(freed(("over",)), 1)
                link(dve.tensor_reduce(pair_f, fl.rearrange("p (n f) -> p n f", f=2 * TT), AX, ALU.add))
                link(dve.tensor_copy(pair_any, pair_f))
                link(dve.tensor_tensor_scan(steps_f[:, :], flags[:, :], flags[:, :], steps_done[:, :], ALU.add,
                                            ALU.max))
                link(dve.tensor_tensor(steps_n[:, :], steps_f[:, :], flags[:, :], ALU.mult))
                link(dve.tensor_copy(steps_done[:, :], steps_f[:, NT - 1:NT]))
                dve.sem_inc(S["table_ready"], 1)

                q0 = l * NP

                def build_selection(pair, s):
                    shape = [P, TT, 2, SLOTS]
                    hot = picks[:, s].rearrange("p i (x n) -> p i x n", x=2)
                    r = rank[:, :, bass.ds(2 * pair, 2)].unsqueeze(3).to_broadcast(shape)
                    g = gate[:, :, bass.ds(2 * pair, 2)].unsqueeze(3).to_broadcast(shape)
                    numbers = slot_no.unsqueeze(1).unsqueeze(1).to_broadcast(shape)
                    dve.tensor_tensor(hot, numbers, r, ALU.is_equal).then_inc(S["hot_built"], 1)
                    dve.wait_ge(S["hot_built"], q0 + pair + 1)
                    dve.tensor_tensor(selw[:, s].rearrange("p i (x n) -> p i x n", x=2), hot, g, ALU.mult)\
                       .then_inc(S["sel_built"], 1)

                def gathered(q):
                    dve.wait_ge(S["xg_full"], q + 1)
                    for k in range(4):
                        ins = dve.tensor_scalar(xg[:, k, :], psums[0][:, k * P:(k + 1) * P], modc[:, 3, k:k + 1],
                                                modc[:, 2, k:k + 1], ALU.mult, ALU.add)
                    ins.then_inc(S["xg0_ready"], 1)

                def hidden(q):
                    dve.wait_ge(S["silu_ready"], q + 1)
                    dve.tensor_tensor(hid, esl, psums[2][:, ED:2 * ED], ALU.mult).then_inc(S["hid_ready"], 1)

                def dense(v, e, ex, i):
                    dve.wait_ge(D_silu, v)
                    dve.scalar_tensor_tensor(out=dhid, in0=dsl, scalar=gate_over[:, i, bass.ds(e, 1)],
                                             in1=psums[3][:, ED:2 * ED], op0=ALU.mult, op1=ALU.mult)\
                       .then_inc(D_hid, 1)

                def pair_step(pair, s, ahead, build):
                    q = q0 + pair
                    if ahead:
                        gathered(q + 1)
                    dve.wait_ge(S["turned"], q + 1)
                    dve.tensor_copy(flat(selT), psums[2][:, 0:ED]).then_inc(S["selT_ready"], 1)
                    if build:
                        build_selection(pair + 2, s)
                    dve.wait_ge(S["o_full"], q + 1)
                    dve.tensor_copy(og[:, 0:512], psums[0][:, :]).then_inc(S["o0_ready"], 1)
                    if ahead:
                        hidden(q + 1)
                        dense_steps(dve, pair + 1, dense)

                build_selection(0, 0)
                build_selection(1, 1)
                gathered(q0)
                hidden(q0)
                dense_steps(dve, 0, dense)
                with dve.Fori(0, NP // 2 - 1) as r:
                    pair_step(2 * r, 0, True, True)
                    pair_step(2 * r + 1, 1, True, True)
                pair_step(NP - 2, 0, True, False)
                pair_step(NP - 1, 1, False, False)
                shared_steps(dve, dense)
                postnorm(1, 5, "y2_ready")
                dve.sem_inc(S["layer_done"], 1)
            assert chain.n == TOTAL["vector_chain"], chain.n

        @block.tensor
        def _(pe):
            mm = pe.matmul
            pe.wait_ge(setup, 2)
            pe.wait_ge(fixed_loaded, 16)

            with pe.Fori(0, depth) as l:
                order = [0]
                used = [0]

                def take(*unit):
                    u = order[0]
                    assert UNITS[u] == unit, (UNITS[u], unit)
                    order[0] += 1
                    pe.wait_ge(bank_free[u % NB], l * USES[u % NB] + u // NB + 1)
                    return psums[u % NB]

                def chunk_in(n):
                    pe.wait_ge(slot_full[n % NS], l * (NCH // NS * 32) + 32 * (n // NS + 1))
                    return wring[:, n % NS]

                def chunk_out(ins):
                    used[0] += 1
                    pe.sem_inc(S["chunk_used"], 1)

                def ada(n):
                    b = take("ada", n)
                    w = chunk_in(n)
                    for k in range(KD):
                        j = k % 4
                        ins = mm(b[32 * j:32 * j + 32, :], c_rep[:, k, :], w[:, k, :], start=(k < 4), stop=(k >= 4),
                                 tile_position=(0, 32 * j))
                    ins.then_inc(S["bank_full"], 1)
                    pe.wait_ge(S["bank_full"], l * NU + order[0])
                    pe.sem_inc(S["chunk_used"], 1)

                def mod_columns(n):
                    b = take("mod", n)
                    for hf in range(2):
                        pe.wait_ge(*at(l, "ada_copied", n + hf + 1))
                        for k in range(KD):
                            ins = mm(b[64 * hf:64 * hf + 64, k:k + 1], adaS[:, (n + hf) % 4, k:512:KD], ones32[:, 0:1],
                                     start=True, stop=True)
                    ins.then_inc(S["bank_full"], 1)

                def gate_rows(n):
                    b = take("gt", n)
                    pe.wait_ge(*at(l, "ada_copied", n + 1))
                    pe.wait_ge(*at(l, "params", 13 * 16))
                    mm(b[:, :], ones32[:, :], adaS[:, n % 4, :], start=True, stop=False)
                    mm(b[:, :], ones[0:1, :], gtb[n // 6][:, 512 * (n % 2):512 * (n % 2) + 512], start=False, stop=True)\
                        .then_inc(S["bank_full"], 1)

                for g in range(7):
                    if g < 6:
                        ada(2 * g)
                        ada(2 * g + 1)
                    if g >= 1:
                        n = 2 * (g - 1)
                        if n in (4, 10):
                            gate_rows(n)
                            gate_rows(n + 1)
                        else:
                            mod_columns(n)

                def transposes(unit, i_ready):
                    for m in range(4):
                        b = take(unit, m)
                        if m == 0:
                            for name, count in i_ready:
                                pe.wait_ge(*at(l, name, count))
                        for kk in range(2):
                            for i in range(TT):
                                ins = pe.transpose(b[:, kk * SEQ + i * P:kk * SEQ + (i + 1) * P],
                                                   rows[:, i, 2 * m + kk:D:KD], ident)
                        ins.then_inc(S["bank_full"], 1)

                transposes("xT", [("xn_ready", 2)])
                pe.wait_ge(*at(l, "hT_ready", 4))

                def project_T(unit, w, cols, blocks, at_col=0):
                    b = take(*unit)
                    for a in range(blocks):
                        for k in range(KD):
                            ins = mm(b[:, at_col + a * SEQ:at_col + (a + 1) * SEQ], w[:, k, cols + a * P:cols + (a + 1) * P],
                                     hT[:, k, :], start=(k == 0), stop=(k == KD - 1))
                    ins.then_inc(S["bank_full"], 1)

                def project(b, at_col, w, cols, width, i):
                    for k in range(KD):
                        ins = mm(b[:, at_col:at_col + width], hT[:, k, i * P:(i + 1) * P], w[:, k, cols:cols + width],
                                 start=(k == 0), stop=(k == KD - 1))
                    return ins

                def chunk_done():
                    pe.wait_ge(S["bank_full"], l * NU + order[0])
                    pe.sem_inc(S["chunk_used"], 1)

                c = 12
                w = chunk_in(c)
                b = take("ckv")
                for i in range(TT):
                    ins = project(b, i * KVL, w, 0, KVL, i)
                ins.then_inc(S["bank_full"], 1)
                chunk_done()
                c += 1
                w = chunk_in(c)
                project_T(("iq",), w, 0, 2)
                b = take("ik")
                for hf in range(2):
                    for k in range(KD):
                        ins = mm(b[64 * hf:64 * hf + 64, 0:SEQ], w[:, k, 256:320], hT[:, k, :], start=(k == 0),
                                 stop=(k == KD - 1))
                ins.then_inc(S["bank_full"], 1)
                b = take("iw")
                for i in range(TT):
                    ins = project(b, i * IDXH, w, 320, IDXH, i)
                ins.then_inc(S["bank_full"], 1)
                chunk_done()
                c += 1
                w = chunk_in(c)
                project_T(("qa", 0), w, 0, 2)
                project_T(("qa", 1), w, 256, 2)
                chunk_done()
                c += 1
                b = take("ckvT")
                pe.wait_ge(*at(l, "ckv_scaled", 1))
                for a in range(2):
                    for i in range(TT):
                        ins = pe.transpose(b[:, a * SEQ + i * P:a * SEQ + (i + 1) * P], ckv_s[:, i, a * P:(a + 1) * P],
                                           ident)
                ins.then_inc(S["bank_full"], 1)
                b = take("kv")
                pe.wait_ge(*at(l, "ckvT_ready", 1))
                for hf in range(2):
                    for a in range(2):
                        mm(b[64 * hf:64 * hf + 64, 0:SEQ], wuk[:, a, :], ckvT[:, a, :], start=(a == 0), stop=(a == 1))
                for i in range(TT):
                    for a in range(2):
                        ins = mm(b[:, SEQ + i * HD:SEQ + (i + 1) * HD], ckvT[:, a, i * P:(i + 1) * P], wuv[:, a, :],
                                 start=(a == 0), stop=(a == 1))
                ins.then_inc(S["bank_full"], 1)
                pe.wait_ge(*at(l, "roped", 2))
                for i in range(TT):
                    for h in range(IDXH):
                        b = take("lg", i, h)
                        r = slice(64 * (h % 2), 64 * (h % 2) + 64)
                        mm(b[:, 0:P * (i + 1)], iqT[r, h // 2, i * P:(i + 1) * P], ikT[r, 0:P * (i + 1)], start=True,
                           stop=True).then_inc(S["bank_full"], 1)
                for name in ("qb", "kb"):
                    w = chunk_in(c)
                    project_T((name, 0), w, 0, 2)
                    project_T((name, 1), w, 256, 2)
                    chunk_done()
                    c += 1
                w = chunk_in(c)
                for i in range(TT):
                    b = take("vb", i)
                    project(b, 0, w, 0, 512, i).then_inc(S["bank_full"], 1)
                chunk_done()
                c += 1
                for name in ("qc", "kc"):
                    w = chunk_in(c)
                    project_T((name, 0), w, 0, 2)
                    project_T((name, 1), w, 256, 2)
                    chunk_done()
                    c += 1

                def head_rows(h):
                    return slice(64 * (h % 2), 64 * (h % 2) + 64)

                def key_query(b, kk, qq, h):
                    r, hb = head_rows(h), h // 2
                    mm(b[:, 0:SEQ], kk[r, hb, 0:P], qq[r, hb, :], start=True, stop=True)
                    return mm(b[:, SEQ:TRI], kk[r, hb, P:SEQ], qq[r, hb, P:SEQ], start=True, stop=True)

                pe.wait_ge(*at(l, "qkb_ready", 4))
                for n in range(NH + 2):
                    if n < NH:
                        b = take("z", n)
                        key_query(b, kbT, qbT, n).then_inc(S["bank_full"], 1)
                    if 1 <= n < NH + 1:
                        h = n - 1
                        b = take("cum", h)
                        pe.wait_ge(*at(l, "sp_ready", h + 1))
                        e = ln[:, h % 2, :]
                        mm(b[:, 0:SEQ], later, e[:, 0:SEQ], start=True, stop=False)
                        mm(b[:, P:SEQ], ones[:, :], e[:, SEQ:TRI], start=False, stop=True)
                        mm(b[:, SEQ:TRI], later, e[:, SEQ:TRI], start=True, stop=True).then_inc(S["bank_full"], 1)
                    if n >= 3 and n % 2 == 1:
                        m = (n - 3) // 2
                        b = take("ob", m)
                        if m == 0:
                            pe.wait_ge(*at(l, "vb_ready", 2))
                        for h in (2 * m, 2 * m + 1):
                            pe.wait_ge(*at(l, "a_ready", h + 1))
                            a = aw[:, h % 4, :]
                            r = head_rows(h)
                            mm(b[r, 0:SEQ], vb_s[:, 0, h * HD:(h + 1) * HD], a[:, 0:SEQ], start=True, stop=False)
                            ins = mm(b[r, P:SEQ], vb_s[:, 1, h * HD:(h + 1) * HD], a[:, SEQ:TRI], start=False, stop=True)
                        ins.then_inc(S["bank_full"], 1)
                    if n < 4:
                        if n % 2 == 0:
                            w = chunk_in(c)
                        b = take("vc", n)
                        project(b, 0, w, 0, 512, n % 2).then_inc(S["bank_full"], 1)
                    elif n < 8:
                        if n % 2 == 0:
                            w = chunk_in(c)
                        b = take("gc", n - 4)
                        project(b, 0, w, 0, 512, n % 2).then_inc(S["bank_full"], 1)
                    if n < 8 and n % 2:
                        chunk_done()
                        c += 1

                for n in range(2 * NH + 3):
                    if n < 2 * NH:
                        i, h = n // NH, n % NH
                        b = take("sc", n)
                        if n == 0:
                            pe.wait_ge(*at(l, "roped", 5))
                        r = head_rows(h)
                        mm(b[:, 0:P * (i + 1)], qaT[r, h // 2, i * P:(i + 1) * P], kT[r, 0:P * (i + 1)], start=True,
                           stop=True).then_inc(S["bank_full"], 1)
                    if 2 <= n < 2 * NH + 2:
                        m = n - 2
                        b = take("pT", m)
                        pe.wait_ge(*at(l, "pn_ready", m + 1))
                        for a in range(m // NH + 1):
                            ins = pe.transpose(b[:, a * P:(a + 1) * P], sm[:, m % 3, a * P:(a + 1) * P], ident)
                        ins.then_inc(S["bank_full"], 1)
                    if n >= 4 and n % 2 == 0:
                        o = (n - 4) // 2
                        i = o // PAIRS
                        b = take("oa", o)
                        if o == 0:
                            pe.wait_ge(*at(l, "vA_ready", 1))
                        for m in (2 * o, 2 * o + 1):
                            pe.wait_ge(*at(l, "pTs_ready", m + 1))
                            for a in range(i + 1):
                                ins = mm(b[head_rows(m), 0:P], vA[:, a, :], pTs[:, m % 4, a * P:(a + 1) * P],
                                         start=(a == 0), stop=(a == i))
                        ins.then_inc(S["bank_full"], 1)
                    if n < 12:
                        if n % 2 == 0:
                            w = chunk_in(c)
                        project_T(("gate", n), w, 256 * (n % 2), 2)
                        if n % 2:
                            chunk_done()
                            c += 1

                pe.wait_ge(*at(l, "roped", 9))
                pe.wait_ge(*at(l, "vc_ready", 4))
                for n in range(NH + 1):
                    if n < NH:
                        b = take("ret", n)
                        key_query(b, kcT, qcT, n).then_inc(S["bank_full"], 1)
                    if n >= 1:
                        h = n - 1
                        b = take("oc", h)
                        pe.wait_ge(*at(l, "rw_ready", h + 1))
                        s = rw[:, h % 2, :]
                        v0, v1 = (vc_s[:, i, h * CV:(h + 1) * CV] for i in range(TT))
                        mm(b[:, 0:CV], s[:, 0:P], v0, start=True, stop=True)
                        mm(b[:, CV:2 * CV], s[:, P:SEQ], v0, start=True, stop=False)
                        mm(b[:, CV:2 * CV], s[:, SEQ:TRI], v1, start=False, stop=True).then_inc(S["bank_full"], 1)
                transposes("ocT", [("ocg_ready", 2)])
                pe.wait_ge(*at(l, "ocT_ready", 4))
                pe.wait_ge(*at(l, "oa_ready", 8))
                pe.wait_ge(*at(l, "ob_ready", 4))

                for j in range(KD):
                    if j % 4 == 0:
                        wab, wc = chunk_in(c), chunk_in(c + 1)
                    cols = slice(P * (j % 4), P * (j % 4) + P)
                    b = take("yab", j)
                    for a, src in enumerate((oaT, obT)):
                        for k in range(4):
                            ins = mm(b[:, a * SEQ:(a + 1) * SEQ], wab[:, 4 * a + k, cols], src[:, k, :], start=(k == 0),
                                     stop=(k == 3))
                    ins.then_inc(S["bank_full"], 1)
                    b = take("yc", j)
                    for k in range(KD):
                        ins = mm(b[:, 0:SEQ], wc[:, k, cols], ocT(k), start=(k == 0), stop=(k == KD - 1))
                    ins.then_inc(S["bank_full"], 1)
                    if j % 4 == 3:
                        chunk_done()
                        chunk_done()
                        c += 2
                pe.wait_ge(*at(l, "mT_ready", 8))
                for hf in range(2):
                    w = chunk_in(c)
                    for i in range(TT):
                        b = take("y", hf, i)
                        for j in range(KD):
                            ins = mm(b[:, :], mT(j)[:, i * P:(i + 1) * P], w[:, j, :], start=(j == 0), stop=(j == KD - 1))
                        ins.then_inc(S["bank_full"], 1)
                    chunk_done()
                    c += 1
                assert c == NCH
                transposes("hT", [("xn_ready", 4)])
                pe.wait_ge(*at(l, "hT_ready", 8))
                b = take("rt")
                for i in range(TT):
                    for k in range(KD):
                        ins = mm(b[:, i * NE:(i + 1) * NE], hT[:, k, i * P:(i + 1) * P], wrt[:, k, :], start=(k == 0),
                                 stop=(k == KD - 1))
                ins.then_inc(S["bank_full"], 1)
                b = take("rank")
                pe.wait_ge(*at(l, "mask_ready", 1))
                mm(b[:, 0:NE], earlier, rsel[:, 0, :], start=True, stop=True)
                mm(b[:, NE:2 * NE], ones[:, :], rsel[:, 0, :], start=True, stop=False)
                mm(b[:, NE:2 * NE], earlier, rsel[:, 1, :], start=False, stop=True).then_inc(S["bank_full"], 1)
                b = take("over")
                pe.wait_ge(*at(l, "over_ready", 1))
                mm(b[0:1, 0:TT * NE].rearrange("p (i e) -> p i e", i=TT), ones[:, 0:1], over, start=True, stop=True)\
                    .then_inc(S["bank_full"], 1)
                assert order[0] == NU

                for b in range(NB):
                    pe.wait_ge(bank_free[b], l * USES[b] + USES[b] + 1)
                q0 = l * NP
                u0 = l * (NP + 1)
                halves = [slice(0, SLOTS), slice(SLOTS, P)]

                def w13_in(s, turn):
                    pe.wait_ge(w13_full[s], (l * (NP // 2 + (s == 0)) + turn + 1) * 64)

                def w2_in(s, turn):
                    pe.wait_ge(w2_full[s], (l * (NP // 2 + (s == 0)) + turn + 1) * 32)

                def gather(q, s):
                    pe.wait_ge(S["sel_built"], q + 1)
                    for k in range(KD):
                        for n, part3 in enumerate(xs):
                            for i in range(TT):
                                ins = mm(psums[k // 4][:, (k % 4) * P:(k % 4 + 1) * P], part3[:, i, k:D:KD], picks[:, s, i, :],
                                         start=(n == 0 and i == 0), stop=(n == 2 and i == TT - 1))
                    ins.then_inc(S["xg_full"], 1)

                def up(q, s):
                    pe.wait_ge(S["xg0_ready"], q + 1)
                    for k in range(KD):
                        if k == 4:
                            pe.wait_ge(S["xg1_ready"], q + 1)
                        for ex in range(2):
                            ins = mm(psums[2][halves[ex], :].rearrange("p (j n) -> p j n", j=2), xg[:, k, halves[ex]],
                                     w13[:, 2 * s + ex, :, k, :], start=(k == 0), stop=(k == KD - 1))
                    ins.then_inc(S["h_full"], 1)

                def turn(q, s):
                    pe.wait_ge(S["hid_ready"], q + 1)
                    for j in range(2):
                        pe.transpose(psums[3][:, j * P:(j + 1) * P], hid[:, j:ED:2], ident)
                    for i in range(TT):
                        ins = pe.transpose(psums[2][:, i * P:(i + 1) * P], selw[:, s, i, :], ident)
                    ins.then_inc(S["turned"], 1)

                def down(q, s, ahead):
                    pe.wait_ge(S["eT_ready"], q + 1)
                    for hf in range(2):
                        if ahead:
                            pe.wait_ge(S[f"xg{hf}_ready"], q + 2)
                        for j in range(2):
                            for ex in range(2):
                                ins = mm(psums[hf][halves[ex], :], eTs[:, j, halves[ex]],
                                         w2s[:, 2 * s + ex, j, hf * 512:hf * 512 + 512], start=(j == 0), stop=(j == 1))
                    ins.then_inc(S["o_full"], 1)

                def scatter(q):
                    pe.wait_ge(S["selT_ready"], q + 1)
                    pe.wait_ge(S["o0_ready"], q + 1)
                    pe.wait_ge(S["o1_ready"], q + 1)
                    for hf in range(2):
                        for i in range(TT):
                            mm(psums[4 + 2 * i + hf][:, :], selT[:, i, :], og[:, hf * 512:hf * 512 + 512], start=False,
                               stop=False, skip_group_check=True)

                def dense_in(s):
                    def step(v, e, ex, i, last=False):
                        for k in range(KD):
                            ins = mm(psums[3][:, :].rearrange("p (j n) -> p j n", j=2), hT[:, k, i * P:(i + 1) * P],
                                     w13[:, 2 * s + ex, :, k, :], start=(k == 0), stop=(k == KD - 1))
                        ins.then_inc(D_h, 1)
                        pe.wait_ge(D_hid, v)
                        for j in range(2):
                            ins = pe.transpose(psums[3][:, j * P:(j + 1) * P], dhid[:, j:ED:2], ident)
                        ins.then_inc(D_T, 1)
                        pe.wait_ge(D_eT, v)
                        for hf in range(2):
                            for j in range(2):
                                ins = mm(psums[4 + 2 * i + hf][:, :], deT[:, j, :],
                                         w2s[:, 2 * s + ex, j, hf * 512:hf * 512 + 512], start=False,
                                         stop=(last and j == 1), skip_group_check=True)
                        return ins
                    return step

                def dense(pair, s, turn_no):
                    w2_in(s, turn_no)
                    apart(pe)
                    dense_steps(pe, pair, dense_in(s))

                def pair_step(pair, s, turn_no, ahead):
                    q = q0 + pair
                    t = 1 - s
                    next_turn = turn_no + s
                    if ahead:
                        gather(q + 1, t)
                    turn(q, s)
                    down(q, s, ahead)
                    pe.wait_ge(S["o_full"], q + 1)
                    pe.sem_inc(S["w2_used"], 1)
                    pe.wait_ge(S["selT_ready"], q + 1)
                    if ahead:
                        w13_in(t, next_turn)
                        up(q + 1, t)
                        dense(pair + 1, t, next_turn)
                        pe.wait_ge(S["h_full"], q + 2)
                        pe.sem_inc(S["w13_used"], 1)
                    scatter(q)

                for n in range(4):
                    mm(psums[4 + n][:, :], zeros[0:1, 0:P], ones32[0:1, 0:1].to_broadcast([1, 512]), start=True,
                       stop=False, skip_group_check=True)
                pe.wait_ge(*at(l, "split_ready", 2))
                pe.wait_ge(*at(l, "table_ready", 1))
                gather(q0, 0)
                w13_in(0, 0)
                up(q0, 0)
                dense(0, 0, 0)
                pe.wait_ge(S["h_full"], q0 + 1)
                pe.sem_inc(S["w13_used"], 1)
                with pe.Fori(0, NP // 2 - 1) as r:
                    pair_step(2 * r, 0, r, True)
                    pair_step(2 * r + 1, 1, r, True)
                pair_step(NP - 2, 0, NP // 2 - 1, True)
                pair_step(NP - 1, 1, NP // 2 - 1, False)
                w13_in(0, NP // 2)
                w2_in(0, NP // 2)
                apart(pe)
                step = dense_in(0)

                def last_step(v, e, ex, i):
                    step(v, e, ex, i, True).then_inc(S["yacc_ready"], 1)

                shared_steps(pe, last_step)
                pe.wait_ge(*at(l, "yacc_ready", 2))
                pe.sem_inc(S["w13_used"], 1)
                pe.sem_inc(S["w2_used"], 1)


_INS = ["x", "c", "positions", "ada_w", "ada_b", "g_pre_mix", "g_post_mix", "g_pre_ffn", "g_post_ffn", "w_in", "g_kv",
        "w_uk", "w_uv", "g_ret", "w_o_a", "w_o_b", "w_o_c", "w_out", "w_router", "router_bias", "w1", "w3", "w2",
        "ws1", "ws3", "ws2"]


def kernel(**inputs):
    import concourse.bacc as _bacc
    from concourse.bass_utils import run_bass_kernel_spmd as _run

    nc = _bacc.Bacc("TRN2", target_bir_lowering=False, num_devices=1)
    arrays = {name: np.ascontiguousarray(inputs[name]) for name in _INS}
    arrays["fixed"], arrays["decay"] = mixer_constants()
    args = {name: nc.dram_tensor(f"in_{name}", a.shape, mybir.dt.from_np(a.dtype), kind="ExternalInput").ap()
            for name, a in arrays.items()}
    args["out"] = nc.dram_tensor("out_0", (1, SEQ, D), F32, kind="ExternalOutput").ap()
    build(nc, **args)
    r = _run(nc, [{f"in_{name}": a for name, a in arrays.items()}], core_ids=[0])
    return r.results[0]["out_0"]
```

```python
from contextlib import ExitStack

import concourse.bass as bass
import numpy as np
from concourse import mybir

F32 = mybir.dt.float32
I32 = mybir.dt.int32
ALU = mybir.AluOpType
ACT = mybir.ActivationFunctionType
AX = mybir.AxisListType.X

P = 128
D = 1024
SEQ = 256
DEPTH = 2
TT = SEQ // P
KD = D // P
EPS = 1e-6
HD = 64
NH = 8
KVL = 256
IDXH = 4
TOPK = 64
CHUNK = 64
CV = 128
NE = 64
NG = 8
EG = NE // NG
TOPG = 4
ED = 256
ROUTED_SCALE = 2.5
BIG = 1e30
GONE = -3e38
GONE_T = -2e38
TRI = SEQ + P

IN = dict(qa=0, ckv=512, iq=768, ik=1024, iw=1088, qb=1092, kb=1604, vb=2116, qc=2628, kc=3140, vc=3652,
          gc=4676, gates=5700)

NS = 3
ADA_LATER = 4
CHUNKS = ([("ada", n) for n in range(ADA_LATER)]
          + [("in", IN["ckv"], 256), ("in", IN["iq"], 324), ("in", IN["qa"], 512), ("in", IN["qb"], 512),
             ("in", IN["kb"], 512), ("in", IN["vb"], 512), ("in", IN["qc"], 512), ("in", IN["kc"], 512),
             ("in", IN["vc"], 512), ("in", IN["vc"] + 512, 512), ("in", IN["gc"], 512), ("in", IN["gc"] + 512, 512)]
          + [("in", IN["gates"] + 512 * n, 512) for n in range(6)]
          + [("ada", 4), ("ada", 5), ("oab", 0)] + [("ada", n) for n in range(6, 10)]
          + [("oc", 0), ("oab", 1), ("oc", 1), ("out", 0), ("out", 1)]
          + [("ada", n) for n in range(10, 12)])
NCH = len(CHUNKS)
assert NCH % NS == 0

NB = 8
PAIRS = NH // 2


def plan_units():
    u = []
    u += [("ada", 0), ("ada", 1), ("ada", 2), ("mod", 0), ("ada", 3)]
    u += [("xT", m) for m in range(4)]
    u += [("mod", 2)]
    u += [("ckv",), ("iq",), ("ik",), ("iw",), ("qa", 0), ("qa", 1), ("ckvT",), ("kv",)]
    u += [("lg", i, h) for i in range(TT) for h in range(IDXH)]
    u += [("qb", 0), ("qb", 1), ("kb", 0), ("kb", 1), ("vb", 0), ("vb", 1)]
    u += [("qc", 0), ("qc", 1), ("kc", 0), ("kc", 1)]
    for n in range(NH + 2):
        if n < NH:
            u += [("z", n)]
        if 1 <= n < NH + 1:
            u += [("cum", n - 1)]
        if n >= 3 and n % 2 == 1:
            u += [("ob", (n - 3) // 2)]
        if n < 4:
            u += [("vc", n)]
        elif n < 8:
            u += [("gc", n - 4)]
    for n in range(2 * NH + 3):
        if n < 2 * NH:
            u += [("sc", n)]
        if 2 <= n < 2 * NH + 2:
            u += [("pT", n - 2)]
        if n >= 4 and n % 2 == 0:
            u += [("oa", (n - 4) // 2)]
        if n < 12:
            u += [("gate", n)]
        elif n in (14, 16):
            u += [("ada", n // 2 - 3)]
    for n in range(NH + 1):
        if n < NH:
            u += [("ret", n)]
        if n >= 1:
            u += [("oc", n - 1)]
    u += [("yab", j) for j in range(4)]
    u += [("gt", 4), ("gt", 5)]
    for n in (6, 8):
        u += [("ada", n), ("ada", n + 1), ("mod", n)]
    u += [("ocT", m) for m in range(4)]
    u += [("yc", j) for j in range(4)] + [("yab", j) for j in range(4, 8)] + [("yc", j) for j in range(4, 8)]
    u += [("y", i, h) for i in range(TT) for h in range(2)]
    u += [("ada", 10), ("ada", 11), ("gt", 10), ("gt", 11)]
    u += [("hT", m) for m in range(4)]
    u += [("rt",)]
    return u


UNITS = plan_units()
UNIT = {name: n for n, name in enumerate(UNITS)}
NU = len(UNITS)
USES = [len(range(b, NU, NB)) for b in range(NB)]
NW = 4
SLOTS = P // 2
NP = NE // 2
NT = NE * TT
UNPICKED = 1000.0

TOTAL = dict(
    bank_full=NU, chunk_used=len(CHUNKS), layer_done=1, params=16 * 9, gate_params=16 * 5, ffn_params=16, gtg_ready=1, decay=32,
    ada_copied=12, squared=14, ms_ready=11, rsq_raw=11, rms_ready=4, xn_ready=4, hT_ready=8, x_ready=4,
    ckv_copied=1, ckv_scaled=1, ckvT_ready=1, vA_ready=1, rope_mul=9, roped=9, iw_ready=1, relu_ready=8, lg_used=8,
    sel_ready=2, qkb_ready=4, vb_ready=2, vc_ready=4, gc_ready=4, gate_ready=12,
    zs_ready=8, ln_ready=8, zb_ready=8, sp_ready=8, w_ready=8, a_ready=8, ob_ready=4,
    sm_ready=16, p_ready=16, rinv_ready=16, pn_ready=16, pTs_ready=16, oa_ready=8,
    rw_ready=8, osb_ready=8, ocn_ready=1, ocg_ready=2, ocT_ready=4,
    tab_ready=8, tc_ready=8, mT_begun=8, mT_ready=8,
    scores_ready=1, mask_ready=1, rank_full=1, over_ready=1, over_full=1, table_ready=1, split_ready=2,
    sh_h=TT, sh_silu=TT, sh_hid=TT, sh_turned=TT, sh_eT=TT, sh_done=1,
    hot_built=NP, sel_built=NP, xg_full=NP, xg0_ready=NP, xg1_ready=NP, h_full=NP, silu_ready=NP, hid_ready=NP, turned=NP,
    eT_ready=NP, selT_ready=NP, o_full=NP, o0_ready=NP, o1_ready=NP,
    yacc_ready=1, split=2 * TT, left=2 * TT,
    vector_chain=228, scalar_chain=131, gpsimd_chain=4,
)


def mixer_constants():
    half = HD // 2
    inv = np.float32(10000.0) ** (-np.arange(half, dtype=np.float32) / np.float32(half))
    p = np.arange(P)
    col = np.zeros((P, 4), np.float32)
    col[:, 0] = inv.astype(np.float32)[p % half]
    col[:, 1] = np.where(p % HD < half, -1.0, 1.0)
    ident = np.eye(P, dtype=np.float32)
    later = (p[:, None] >= p[None, :]).astype(np.float32)
    t = np.arange(SEQ)
    key0, key1 = p[:, None], p[:, None] + P
    causal = np.concatenate([key0 < t[None, :], key1 < t[None, P:]], 1)
    earlier = (p[:, None] < p[None, :]).astype(np.float32)
    slots = np.broadcast_to(np.arange(SLOTS, dtype=np.float32), (P, SLOTS))
    causal_neg = np.where(causal, 0.0, -BIG)
    adm = np.zeros((P, TT, SEQ), np.float32)
    for i in range(TT):
        adm[:, i, :] = np.where(t[None, :] // CHUNK <= (p[:, None] + i * P) // CHUNK, 0.0, -BIG)
    dec = np.zeros((P, NH, TRI), np.float64)
    for h in range(NH):
        lg = np.log(1.0 - 2.0 ** (-5.0 - h))
        for keys, q, c0 in ((p, t, 0), (p + P, t[P:], SEQ)):
            k, a = keys[:, None], q[None, :]
            inner = np.exp(lg * np.abs(k - a))
            cross = np.exp(lg * ((a % CHUNK + 1) + CHUNK * (a // CHUNK - k // CHUNK - 1) + (CHUNK - 1 - k % CHUNK)))
            w = np.where(k // CHUNK == a // CHUNK, inner, np.where(k // CHUNK < a // CHUNK, cross, 0.0))
            dec[:, h, c0:c0 + len(q)] = w * HD ** -0.5
    fixed = np.concatenate([ident, later, col, causal, causal_neg, adm.reshape(P, -1), earlier, slots], 1).astype(np.float32)
    return np.ascontiguousarray(fixed), np.ascontiguousarray(dec.reshape(P, -1).astype(np.float32))


def build(nc, x, c, positions, ada_w, ada_b, g_pre_mix, g_post_mix, g_pre_ffn, g_post_ffn, w_in, g_kv, w_uk, w_uv,
          g_ret, w_o_a, w_o_b, w_o_c, w_out, w_router, router_bias, w1, w3, w2, ws1, ws3, ws2, fixed, decay, out,
          depth=DEPTH, dbg=None):
    ctx = ExitStack()
    with ctx:
        def sb(name, shape, dt=F32):
            return ctx.enter_context(nc.sbuf_tensor(name, shape, dt))

        def sem(name):
            return ctx.enter_context(nc.semaphore(name))

        M = sb("M", [P, 24576])
        wring = M[:, 0:NS * 4096].rearrange("p (s k n) -> p s k n", s=NS, k=KD)
        gT = M[:, 12288:18432].rearrange("p (b t) -> p b t", b=24)
        dec = M[:, 18432:21504].rearrange("p (h t) -> p h t", h=NH)
        qcT = M[:, 21504:22528].rearrange("p (b t) -> p b t", b=4)
        kcT = M[:, 22528:23552].rearrange("p (b t) -> p b t", b=4)
        vb_s = M[:, 23552:24576].rearrange("p (i n) -> p i n", i=TT)
        w13 = M[:, 0:NW * 4096].rearrange("p (s j k n) -> p s j k n", s=NW, j=2, k=KD)
        w2s = M[:, 16384:24576].rearrange("p (s j n) -> p s j n", s=NW, j=2)
        x_sb = sb("x_sb", [P, TT, D])
        hT = sb("hT", [P, KD, SEQ])
        rows = sb("rows", [P, TT, D])
        fix = sb("fix", [P, 260 + 2 * TRI + TT * SEQ + P + SLOTS])
        ident, later = fix[:, 0:128], fix[:, 128:256]
        invf, rsign = fix[:, 256:257], fix[:, 257:258]
        cm01, cmneg = fix[:, 260:260 + TRI], fix[:, 260 + TRI:260 + 2 * TRI]
        earlier = fix[:, 260 + 2 * TRI + TT * SEQ:][:, 0:P]
        slot_no = fix[:, 260 + 2 * TRI + TT * SEQ + P:]
        adm = fix[:, 260 + 2 * TRI:260 + 2 * TRI + TT * SEQ].rearrange("p (i t) -> p i t", i=TT)
        ones = sb("ones", [P, P])
        exponent = sb("exponent", [P, 16])
        ones32 = sb("ones32", [P, P])
        cosT = sb("cosT", [P, SEQ])
        sinT = sb("sinT", [P, SEQ])
        c_col = sb("c_col", [P, KD])
        c_rep = sb("c_rep", [P, KD, 32])
        gtg = sb("gtg", [P, 2, D])
        modc = sb("modc", [P, 4, KD])
        gpre = sb("gpre", [P, 2, KD])
        adabc = sb("adabc", [P, 4, KD])
        gkv_c = sb("gkv_c", [P, 2])
        gret_c = sb("gret_c", [P, KD])
        rbias = sb("rbias", [P, NE])
        wuk = sb("wuk", [P, 2, HD])
        wuv = sb("wuv", [P, 2, HD])
        wrt = sb("wrt", [P, KD, NE])
        ssq = sb("ssq", [P, TT, 2])
        ms, rs0, rs, rt1 = (sb(f"norm_{n}", [P, 16]) for n in ("ms", "raw", "r", "t"))
        part = sb("part", [P, 4])
        qbT = sb("qbT", [P, 4, SEQ])
        kbT = sb("kbT", [P, 4, SEQ])
        qaT = sb("qaT", [P, 4, SEQ])
        vc_s = sb("vc_s", [P, TT, D])
        gcs = sb("gcs", [P, TT, D])
        oaT = sb("oaT", [P, 4, SEQ])
        obT = sb("obT", [P, 4, SEQ])
        iqT = sb("iqT", [P, 2, SEQ])
        ikT = sb("ikT", [P, SEQ])
        kT = sb("kT", [P, SEQ])
        vA = sb("vA", [P, TT, HD])
        iw_s = sb("iw_s", [P, TT, IDXH])
        ckv_s = sb("ckv_s", [P, TT, KVL])
        ckvT = sb("ckvT", [P, 2, SEQ])
        selb = sb("selb", [P, TT, SEQ])
        top8 = sb("top8", [P, 8])
        nmx = sb("nmx", [P, 3])
        rsum = sb("rsum", [P, 3])
        rinv = sb("rinv", [P, 3])
        bst = sb("bst", [P, 2 * NH, 6])
        mv = sb("mv", [P, 2 * NH, 2])
        scr = sb("scr", [P, 3072])
        rsc = sb("rsc", [P, TT, NE])
        rsel = sb("rsel", [P, TT, NE])
        rwk = sb("rwk", [P, TT, NE])
        gsc = sb("gsc", [P, TT, NG])
        g8 = sb("g8", [P, TT, NG, 8])
        t8 = sb("t8", [P, TT, 8])
        gate = sb("gate", [P, TT, NE])
        gate_over = sb("gate_over", [P, TT, NE])
        steps_done = sb("steps_done", [1, 1])
        def flat2(b):
            return b[:, :, :].rearrange("p a n -> p (a n)")

        gpost = flat2(qaT)
        gtb = {n: flat2(b)[0:1, :] for n, b in ((4, iqT), (5, ckv_s), (10, selb), (11, ckvT))}
        rp = scr[:, 0:2048].rearrange("p (b a n) -> p b a n", b=2, a=2)
        lr = scr[:, 2048:3072].rearrange("p (b t) -> p b t", b=4)
        zs = scr[:, 0:768].rearrange("p (b n) -> p b n", b=2)
        ln = scr[:, 768:1536].rearrange("p (b n) -> p b n", b=2)
        aw = scr[:, 1536:3072].rearrange("p (b n) -> p b n", b=4)
        sm = scr[:, 0:768].rearrange("p (b n) -> p b n", b=3)
        pTs = scr[:, 768:1792].rearrange("p (b n) -> p b n", b=4)
        rw = scr[:, 0:768].rearrange("p (b n) -> p b n", b=2)
        tab = scr[:, 0:1024].rearrange("p (b a n) -> p b a n", b=2, a=2)
        tc = scr[:, 1024:1536].rearrange("p (b n) -> p b n", b=2)
        dx = scr[:, 0:2048].rearrange("p (b n) -> p b n", b=2)
        junk = scr[:, 2048:3072]
        modulation = [vc_s[:, i, 512 * a:512 * a + 512] for i in range(TT) for a in range(2)]
        modulation += [scr[:, 2048:2560], scr[:, 2560:3072]]
        adaS = [modulation[n] if n < 4 else modulation[4 + n % 2] if n < 10 else modulation[n - 10] for n in range(12)]
        BF = mybir.dt.bfloat16
        rank = ckv_s[:, :, 0:NE]
        over = ckv_s[:, :, NE:2 * NE]
        flags = selb[0:1, 0, 0:NT]
        steps_f = selb[0:1, 1, 0:NT]
        steps_n = qaT[0:1, 0, 0:NT].bitcast(I32)
        pair_f = qaT[0:1, 2, 0:NP]
        pair_any = qaT[0:1, 1, 0:NP].bitcast(I32)
        xs = [gcs[:, 0, :].bitcast(BF), gcs[:, 1, :].bitcast(BF), vc_s[:, 0, :].bitcast(BF)]
        xs = [v.rearrange("p (i n) -> p i n", i=TT) for v in xs]
        rest = [flat2(b) for b in (oaT, obT)]
        picks = scr[:, 0:256].bitcast(BF).rearrange("p (b i n) -> p b i n", b=2, i=TT)
        selw = scr[:, 256:768].rearrange("p (b i n) -> p b i n", b=2, i=TT)
        esl = scr[:, 768:1024]
        hid = scr[:, 1024:1280]
        eTs = scr[:, 1280:1536].rearrange("p (j t) -> p j t", j=2)
        selT = scr[:, 1536:2048].rearrange("p (b i t) -> p b i t", b=2, i=TT)
        dsl, dhid = scr[:, 2048:2304], scr[:, 2304:2560]
        deT = scr[:, 2560:2816].rearrange("p (j t) -> p j t", j=2)
        xg = flat2(qbT).rearrange("p (k t) -> p k t", k=KD)
        og = flat2(kbT)

        def ocT(k):
            return (qcT, kcT)[k // 4][:, k % 4, :]

        def mT(j):
            return (qbT, kbT)[j // 4][:, j % 4, :]

        psums = [ctx.enter_context(nc.psum_tensor(f"bank{b}", [P, 512], F32)) for b in range(8)]

        S = {name: sem(name) for name in TOTAL}
        D_h, D_silu, D_hid, D_T, D_eT = (sem(n) for n in ("dense_h", "dense_silu", "dense_hid", "dense_turned",
                                                          "dense_eT"))
        slot_full = [sem(f"slot_full{n}") for n in range(NS)]
        w13_full = [sem(f"w13_full{n}") for n in range(2)]
        w2_full = [sem(f"w2_full{n}") for n in range(2)]
        shared_in = sem("shared_in")
        bank_free = [sem(f"bank_free{n}") for n in range(NB)]
        c_loaded = sem("c_loaded")
        fixed_loaded, x_loaded, pos_loaded, angles, sincos, csig, setup, out_stored = (
            sem(n) for n in ("fixed_loaded", "x_loaded", "pos_loaded", "angles", "sincos", "csig", "setup", "out_stored"))
        setup_chain = sem("setup_chain")
        waits_apart = sem("waits_apart")

        def at(l, name, n):
            return S[name], l * TOTAL[name] + n

        def full(l, unit):
            return S["bank_full"], l * NU + UNIT[unit] + 1

        def bank(unit):
            return psums[UNIT[unit] % NB]

        def freed(unit):
            return bank_free[UNIT[unit] % NB]

        def flat(b):
            return b.rearrange("p a n -> p (a n)")

        def apart(eng):
            eng.sem_inc(waits_apart, 1)

        class Chain:

            def __init__(self, eng, name):
                self.eng, self.name, self.n = eng, name, 0

            def link(self, l, ins):
                self.n += 1
                ins.then_inc(S[self.name], 1)
                self.eng.wait_ge(S[self.name], l * TOTAL[self.name] + self.n)

        def dense_steps(eng, pair, step):
            with eng.If(eng.value_load(pair_any[0:1, bass.ds(pair, 1)], min_val=0, max_val=2 * TT) > 0):
                for ex in range(2):
                    for i in range(TT):
                        at_table = (2 * pair + ex) * TT + i
                        v = eng.value_load(steps_n[0:1, bass.ds(at_table, 1)], min_val=0, max_val=DEPTH * NT)
                        with eng.If(v > 0):
                            step(v, 2 * pair + ex, ex, i)
                        eng.sem_inc(waits_apart, 1)
            eng.sem_inc(waits_apart, 1)

        block = ctx.enter_context(nc.Block())

        @block.sync
        def _(sp):
            sp.dma_start(c_col[:, :], c[0, :].rearrange("(p k) -> p k", k=KD)).then_inc(c_loaded, 16)

            def chunk(l, n):
                slot = n % NS
                if n < NS - 1:
                    sp.wait_ge(S["xg_full"], l * NP + 1)
                elif n < NS:
                    sp.wait_ge(S["o_full"], l * NP + 1)
                else:
                    sp.wait_ge(*at(l, "chunk_used", n - NS + 1))
                apart(sp)
                kind = CHUNKS[n]
                w = wring[:, slot]
                if kind[0] == "ada":
                    sp.dma_start(w, ada_w[l, :, 512 * kind[1]:512 * kind[1] + 512].rearrange("(p k) n -> p k n", k=KD))\
                      .then_inc(slot_full[slot], 32)
                elif kind[0] == "in":
                    sp.dma_start(w[:, :, 0:kind[2]],
                                 w_in[l, :, kind[1]:kind[1] + kind[2]].rearrange("(p k) n -> p k n", k=KD))\
                      .then_inc(slot_full[slot], 32)
                elif kind[0] == "oab":
                    for b, src in enumerate((w_o_a, w_o_b)):
                        sp.dma_start(w[:, 4 * b:4 * b + 4, :],
                                     src[l, :, 512 * kind[1]:512 * kind[1] + 512].rearrange("(k p) n -> p k n", p=P))\
                          .then_inc(slot_full[slot], 16)
                elif kind[0] == "oc":
                    sp.dma_start(w, w_o_c[l, :, 512 * kind[1]:512 * kind[1] + 512].rearrange("(p k) n -> p k n", k=KD))\
                      .then_inc(slot_full[slot], 32)
                else:
                    sp.dma_start(w, w_out[l, :, 512 * kind[1]:512 * kind[1] + 512].rearrange("(k p) n -> p k n", p=P))\
                      .then_inc(slot_full[slot], 32)

            def up_in(slot, a1, a3, loaded):
                sp.dma_start(w13[:, slot, 0], a1.rearrange("(p k) n -> p k n", k=KD)).then_inc(loaded, 16)
                sp.dma_start(w13[:, slot, 1], a3.rearrange("(p k) n -> p k n", k=KD)).then_inc(loaded, 16)

            def down_in(slot, a2, loaded):
                sp.dma_start(w2s[:, slot], a2.rearrange("(p j) n -> p j n", j=2)).then_inc(loaded, 16)

            with sp.Fori(0, depth) as l:
                for n in range(NCH):
                    chunk(l, n)
                sp.wait_ge(*full(l, ("y", 0, 0)))
                apart(sp)
                up_in(3, ws1[l, :, :], ws3[l, :, :], shared_in)
                down_in(3, ws2[l, :, :], shared_in)
                sp.wait_ge(*at(l, "chunk_used", NCH - 2))
                apart(sp)
                up_in(0, w1[l, 0, :, :], w3[l, 0, :, :], w13_full[0])
                down_in(0, w2[l, 0, :, :], w2_full[0])
                down_in(1, w2[l, 1, :, :], w2_full[0])
                sp.wait_ge(*at(l, "chunk_used", NCH - 1))
                apart(sp)
                up_in(1, w1[l, 1, :, :], w3[l, 1, :, :], w13_full[0])
                sp.wait_ge(*at(l, "chunk_used", NCH))
                apart(sp)
                up_in(2, w1[l, 2, :, :], w3[l, 2, :, :], w13_full[1])
                down_in(2, w2[l, 2, :, :], w2_full[1])
                sp.wait_ge(*at(l, "sh_done", 1))
                apart(sp)
                up_in(3, w1[l, 3, :, :], w3[l, 3, :, :], w13_full[1])
                down_in(3, w2[l, 3, :, :], w2_full[1])
                with sp.Fori(1, NP // 2) as r:
                    for s in range(2):
                        pair = 2 * r + s
                        sp.wait_ge(S["xg_full"], l * NP + pair + 1)
                        apart(sp)
                        for ex in range(2):
                            up_in(2 * s + ex, w1[l, 2 * pair + ex, :, :], w3[l, 2 * pair + ex, :, :], w13_full[s])
                        sp.wait_ge(S["o_full"], l * NP + pair)
                        apart(sp)
                        for ex in range(2):
                            down_in(2 * s + ex, w2[l, 2 * pair + ex, :, :], w2_full[s])
            sp.wait_ge(S["layer_done"], depth + 1)
            for i in range(TT):
                sp.dma_start(out[0, i * P:(i + 1) * P, :], x_sb[:, i, :]).then_inc(out_stored, 16)
            sp.wait_ge(out_stored, 16 * TT)

        @block.gpsimd
        def _(pool):
            chain = Chain(pool, "gpsimd_chain")
            pos_i = obT[:, 0, :].bitcast(I32)
            pool.dma_start(pos_i, positions.to_broadcast([P, SEQ])).then_inc(pos_loaded, 16)
            pool.memset(ones[:, :], 1.0)
            pool.memset(ones32[:, :], 1.0 / 32)
            pool.memset(exponent[:, :], -0.5)
            pool.memset(steps_done[:, :], 0.0).then_inc(setup, 1)

            with pool.Fori(0, depth) as l:
                powers = [0]

                def power(c0, c1):
                    powers[0] += 1
                    pool.wait_ge(*at(l, "ms_ready", powers[0]))
                    apart(pool)
                    pool.tensor_tensor(rs0[:, c0:c1], ms[:, c0:c1], exponent[:, c0:c1], ALU.pow)\
                        .then_inc(S["rsq_raw"], 1)

                pool.wait_ge(S["layer_done"], l + 1)
                col = lambda v: v.rearrange("(p k) -> p k", k=KD)
                row = lambda v: v.rearrange("(a n) -> a n", a=1)
                pool.dma_start(gpre[:, 0, :], col(g_pre_mix[l, :])).then_inc(S["params"], 16)
                pool.dma_start(gpre[:, 1, :], col(g_pre_ffn[l, :])).then_inc(S["params"], 16)
                pool.dma_start(adabc[:, 0:2, :], ada_b[l, 0:2 * D].rearrange("(v p k) -> p v k", v=2, k=KD))\
                    .then_inc(S["params"], 16)
                pool.dma_start(adabc[:, 2:4, :], ada_b[l, 3 * D:5 * D].rearrange("(v p k) -> p v k", v=2, k=KD))\
                    .then_inc(S["params"], 16)
                pool.dma_start(gret_c[:, :], col(g_ret[l, :])).then_inc(S["params"], 16)
                pool.dma_start(rbias[:, :], row(router_bias[l, :]).to_broadcast([P, NE])).then_inc(S["params"], 16)
                pool.dma_start(wuk[:, :, :], w_uk[l, :, :].rearrange("(b p) n -> p b n", p=P)).then_inc(S["params"], 16)
                pool.dma_start(wuv[:, :, :], w_uv[l, :, :].rearrange("(b p) n -> p b n", p=P)).then_inc(S["params"], 16)
                pool.dma_start(wrt[:, :, :], w_router[l, :, :].rearrange("(p k) n -> p k n", k=KD))\
                    .then_inc(S["params"], 16)
                with nc.allow_non_contiguous_dma(reason="two columns"):
                    pool.dma_start(gkv_c[:, :], g_kv[l, :].rearrange("(b p) -> p b", p=P)).then_inc(S["decay"], 16)
                pool.dma_start(flat(dec), decay).then_inc(S["decay"], 16)

                for n in range(2 * TT):
                    power(n % TT, n % TT + 1)
                for n, (dst, blocks) in enumerate(((iqT, 2), (ikT, 1), (qaT[:, 0:2], 2), (qaT[:, 2:4], 2), (kT, 1),
                                                   (qcT[:, 0:2], 2), (qcT[:, 2:4], 2), (kcT[:, 0:2], 2),
                                                   (kcT[:, 2:4], 2))):
                    pool.wait_ge(*at(l, "rope_mul", n + 1))
                    to = dst[:, :] if blocks == 1 else flat(dst[:, :, :])
                    w = blocks * SEQ
                    pool.tensor_tensor(to, rp[:, n % 2, 0, 0:w], rp[:, n % 2, 1, 0:w], ALU.add)\
                        .then_inc(S["roped"], 1)

                for h in range(NH):
                    pool.wait_ge(*at(l, "zs_ready", h + 1))
                    if h >= 4:
                        pool.wait_ge(*full(l, ("ob", (h - 4) // 2)))
                    pool.tensor_tensor(aw[:, h % 4, :], zs[:, h % 2, :], cmneg, ALU.add).then_inc(S["zb_ready"], 1)

                for n in range(2 * NH):
                    w = P * (n // NH + 1)
                    pool.wait_ge(*at(l, "rinv_ready", n + 1))
                    apart(pool)
                    pool.tensor_scalar(sm[:, n % 3, 0:w], sm[:, n % 3, 0:w], rinv[:, n % 3:n % 3 + 1], None, ALU.mult)\
                        .then_inc(S["pn_ready"], 1)

                pool.wait_ge(*full(l, ("oa", 2 * PAIRS - 1)))
                pool.wait_ge(*at(l, "sm_ready", 2 * NH))
                for n in (4, 5, 10, 11):
                    pool.dma_start(gtb[n], row(ada_b[l, 512 * n:512 * n + 512])).then_inc(S["gate_params"], 16)
                pool.dma_start(gpost, row(g_post_mix[l, :]).to_broadcast([P, D])).then_inc(S["gate_params"], 16)

                power(0, TT * NH)
                pool.wait_ge(*at(l, "ocn_ready", 1))
                pool.wait_ge(*at(l, "gc_ready", 4))
                pool.tensor_tensor(rows[:, 0, :], rows[:, 0, :], gcs[:, 0, :], ALU.mult).then_inc(S["ocg_ready"], 1)

                for j0 in (0, 4):
                    for j in range(j0, j0 + 4):
                        pool.wait_ge(*at(l, "tab_ready", j + 1))
                        pool.tensor_tensor(mT(j), tab[:, j % 2, 0, :], tab[:, j % 2, 1, :], ALU.add)\
                            .then_inc(S["mT_begun"], 1)
                    for j in range(j0, j0 + 4):
                        pool.wait_ge(*at(l, "tc_ready", j + 1))
                        pool.wait_ge(*at(l, "mT_begun", j + 1))
                        pool.tensor_tensor(mT(j), mT(j), tc[:, j % 2, :], ALU.add).then_inc(S["mT_ready"], 1)

                pool.wait_ge(*at(l, "gtg_ready", 1))
                apart(pool)
                pool.dma_start(gpost, row(g_post_ffn[l, :]).to_broadcast([P, D])).then_inc(S["ffn_params"], 16)

                for i in range(TT):
                    for _ in range(2):
                        power(i, i + 1)

                for n in range(2):
                    for i in range(TT):
                        pool.wait_ge(*at(l, "split", n * TT + i + 1))
                        chain.link(l, pool.tensor_tensor(rest[i], rest[i] if n else rows[:, i, :], xs[n][:, i, :],
                                                         ALU.subtract))
                        pool.sem_inc(S["left"], 1)
                power(0, 1)
                power(1, 2)
            assert chain.n == TOTAL["gpsimd_chain"], chain.n

        @block.scalar
        def _(act):
            chain = Chain(act, "scalar_chain")
            act.dma_start(fix[:, :], fixed).then_inc(fixed_loaded, 16)
            for i in range(TT):
                act.dma_start(x_sb[:, i, :], x[0, i * P:(i + 1) * P, :]).then_inc(x_loaded, 16)
            act.wait_ge(c_loaded, 16)
            act.activation(c_col[:, :], c_col[:, :], ACT.Silu).then_inc(csig, 1)
            act.wait_ge(angles, 1)
            act.activation(sinT[:, :], sinT[:, :], ACT.Sin)
            act.activation(cosT[:, :], cosT[:, :], ACT.Sin).then_inc(sincos, 1)

            def squares(l, src, half, i):
                w = src.shape[-1]
                chain.link(l, act.activation(junk[:, 0:w], src, ACT.Square, accum_out=ssq[:, i, half:half + 1]))
                act.sem_inc(S["squared"], 1)

            def normed_rows(l, n, i):
                act.wait_ge(*at(l, "rms_ready", TT * n + i + 1))
                act.activation(rows[:, i, :], x_sb[:, i, :], ACT.Copy, scale=rs[:, i:i + 1]).then_inc(S["xn_ready"], 1)

            def ada_rows(l, n):
                act.wait_ge(*full(l, ("ada", n)))
                chain.link(l, act.activation(adaS[n], bank(("ada", n))[:, :], ACT.Copy))
                act.sem_inc(S["ada_copied"], 1)
                act.sem_inc(freed(("ada", n)), 1)

            with act.Fori(0, depth) as l:
                for i in range(TT):
                    act.wait_ge(*at(l, "x_ready", i + 1))
                    squares(l, x_sb[:, i, :], 0, i)
                    ada_rows(l, i)
                for i in range(TT):
                    normed_rows(l, 0, i)
                    ada_rows(l, 2 + i)

                def take(unit, dst, src, name, func=ACT.Copy, scale=1.0):
                    act.wait_ge(*full(l, unit))
                    chain.link(l, act.activation(dst, src, func, scale=scale))
                    act.sem_inc(S[name], 1)
                    act.sem_inc(freed(unit), 1)

                two = lambda b: b[:, :].rearrange("p (a n) -> p a n", a=2)
                act.wait_ge(*full(l, ("ckv",)))
                for i in range(TT):
                    squares(l, bank(("ckv",))[:, i * KVL:(i + 1) * KVL], 0, i)
                take(("ckv",), ckv_s[:, :, :], two(bank(("ckv",))), "ckv_copied")
                take(("iw",), iw_s[:, :, :], bank(("iw",))[:, 0:2 * IDXH].rearrange("p (i h) -> p i h", i=TT), "iw_ready")
                n = 0
                for i in range(TT):
                    w = P * (i + 1)
                    for h in range(IDXH):
                        if n >= 4:
                            act.wait_ge(*at(l, "lg_used", n - 3))
                        take(("lg", i, h), lr[:, n % 4, 0:w], bank(("lg", i, h))[:, 0:w], "relu_ready",
                             ACT.Relu, HD ** -0.5 * IDXH ** -0.5)
                        n += 1
                for name, dst in (("qb", qbT), ("kb", kbT)):
                    for m in range(2):
                        take((name, m), flat(dst[:, 2 * m:2 * m + 2, :]), bank((name, m))[:, :], "qkb_ready")
                for i in range(TT):
                    take(("vb", i), vb_s[:, i, :], bank(("vb", i))[:, :], "vb_ready")
                act.wait_ge(*at(l, "roped", 9))
                for n in range(NH + 2):
                    if n < NH:
                        z, e = zs[:, n % 2, :], ln[:, n % 2, :]
                        if n >= 2:
                            act.wait_ge(*full(l, ("cum", n - 2)))
                            act.wait_ge(*at(l, "zb_ready", n - 1))
                        take(("z", n), z, bank(("z", n))[:, 0:TRI], "zs_ready", ACT.Copy, HD ** -0.5)
                        chain.link(l, act.activation(e, z, ACT.Abs))
                        chain.link(l, act.activation(e, e, ACT.Exp, scale=-1.0))
                        act.activation(e, e, ACT.Ln, bias=1.0).then_inc(S["ln_ready"], 1)
                    if 1 <= n < NH + 1:
                        act.wait_ge(*at(l, "w_ready", n))
                        act.activation(aw[:, (n - 1) % 4, :], aw[:, (n - 1) % 4, :], ACT.Exp).then_inc(S["a_ready"], 1)
                    if n >= 3 and n % 2 == 1:
                        m = (n - 3) // 2
                        take(("ob", m), obT[:, m, :], bank(("ob", m))[:, 0:SEQ], "ob_ready")
                    if n < 4:
                        take(("vc", n), vc_s[:, n % 2, 512 * (n // 2):512 * (n // 2) + 512], bank(("vc", n))[:, :],
                             "vc_ready")
                    elif n < 8:
                        m = n - 4
                        take(("gc", m), gcs[:, m % 2, 512 * (m // 2):512 * (m // 2) + 512], bank(("gc", m))[:, :],
                             "gc_ready", ACT.Silu)
                for n in range(2 * NH + 3):
                    if n < 2 * NH:
                        w = P * (n // NH + 1)
                        act.wait_ge(*at(l, "sm_ready", n + 1))
                        act.activation(sm[:, n % 3, 0:w], sm[:, n % 3, 0:w], ACT.Exp, bias=nmx[:, n % 3:n % 3 + 1],
                                       accum_out=rsum[:, n % 3:n % 3 + 1]).then_inc(S["p_ready"], 1)
                    if 2 <= n < 2 * NH + 2:
                        m = n - 2
                        w = P * (m // NH + 1)
                        take(("pT", m), pTs[:, m % 4, 0:w], bank(("pT", m))[:, 0:w], "pTs_ready")
                    if n >= 4 and n % 2 == 0:
                        m = (n - 4) // 2
                        i, hb = m // PAIRS, m % PAIRS
                        take(("oa", m), oaT[:, hb, i * P:(i + 1) * P], bank(("oa", m))[:, 0:P], "oa_ready")
                    if n < 12:
                        take(("gate", n), flat(gT[:, 2 * n:2 * n + 2, :]), bank(("gate", n))[:, :], "gate_ready",
                             ACT.Sigmoid)
                    elif n in (14, 16):
                        ada_rows(l, n // 2 - 3)
                for h in range(NH):
                    take(("oc", h), rows[:, :, h * CV:(h + 1) * CV],
                         bank(("oc", h))[:, 0:2 * CV].rearrange("p (i n) -> p i n", i=TT), "osb_ready")
                for n in range(6, 10):
                    ada_rows(l, n)
                for m in range(4):
                    act.wait_ge(*full(l, ("ocT", m)))
                    for kk in range(2):
                        k = 2 * m + kk
                        chain.link(l, act.activation(ocT(k), bank(("ocT", m))[:, kk * SEQ:(kk + 1) * SEQ], ACT.Copy,
                                                     scale=gret_c[:, k:k + 1]))
                    act.sem_inc(S["ocT_ready"], 1)
                    act.sem_inc(freed(("ocT", m)), 1)
                for i in range(TT):
                    for hf in range(2):
                        act.wait_ge(*full(l, ("y", i, hf)))
                        squares(l, bank(("y", i, hf))[:, :], hf, i)
                    act.wait_ge(*at(l, "x_ready", TT + i + 1))
                    squares(l, x_sb[:, i, :], 0, i)
                for i in range(TT):
                    normed_rows(l, 1, i)
                    ada_rows(l, 10 + i)
                take(("rt",), rsc[:, :, :], bank(("rt",))[:, 0:TT * NE].rearrange("p (i e) -> p i e", i=TT),
                     "scores_ready", ACT.Sigmoid)

                def split(n, i):
                    if n:
                        act.wait_ge(*at(l, "left", (n - 1) * TT + i + 1))
                    act.activation(xs[n][:, i, :], rest[i] if n else rows[:, i, :], ACT.Copy)\
                       .then_inc(S["split" if n < 2 else "split_ready"], 1)

                split(0, 0)
                split(0, 1)
                for i in range(TT):
                    act.wait_ge(*at(l, "sh_h", i + 1))
                    act.activation(dsl, psums[3][:, 0:ED], ACT.Silu).then_inc(S["sh_silu"], 1)
                    act.wait_ge(*at(l, "sh_turned", i + 1))
                    act.activation(flat(deT), psums[3][:, 0:ED], ACT.Copy).then_inc(S["sh_eT"], 1)
                    split(1, i)
                split(2, 0)
                split(2, 1)

                act.wait_ge(*at(l, "table_ready", 1))
                q0 = l * NP

                def gathered(q):
                    act.wait_ge(S["xg_full"], q + 2)
                    for k in range(4, KD):
                        ins = act.activation(xg[:, k, :], psums[1][:, (k - 4) * P:(k - 3) * P], ACT.Identity,
                                             scale=modc[:, 3, k:k + 1], bias=modc[:, 2, k:k + 1])
                    ins.then_inc(S["xg1_ready"], 1)

                def silu(q):
                    act.wait_ge(S["h_full"], q + 1)
                    act.activation(esl, psums[2][:, 0:ED], ACT.Silu).then_inc(S["silu_ready"], 1)

                def dense(v, e, ex, i):
                    act.wait_ge(D_h, v)
                    act.activation(dsl, psums[3][:, 0:ED], ACT.Silu).then_inc(D_silu, 1)
                    act.wait_ge(D_T, v)
                    act.activation(flat(deT), psums[3][:, 0:ED], ACT.Copy).then_inc(D_eT, 1)

                def pair_step(pair, ahead):
                    q = q0 + pair
                    if ahead:
                        gathered(q + 1)
                    act.wait_ge(S["turned"], q + 1)
                    act.activation(flat(eTs), psums[3][:, 0:ED], ACT.Copy).then_inc(S["eT_ready"], 1)
                    act.wait_ge(S["o_full"], q + 2)
                    act.activation(og[:, 512:D], psums[1][:, :], ACT.Copy).then_inc(S["o1_ready"], 1)
                    if ahead:
                        silu(q + 1)
                        dense_steps(act, pair + 1, dense)

                gathered(q0)
                silu(q0)
                dense_steps(act, 0, dense)
                with act.Fori(0, NP // 2 - 1) as r:
                    pair_step(2 * r, True)
                    pair_step(2 * r + 1, True)
                pair_step(NP - 2, True)
                pair_step(NP - 1, False)
                act.wait_ge(S["yacc_ready"], l + 2)
                for i in range(TT):
                    for hf in range(2):
                        squares(l, psums[4 + 2 * i + hf][:, :], hf, i)
            assert chain.n == TOTAL["scalar_chain"], chain.n

        @block.vector
        def _(dve):
            chain = Chain(dve, "vector_chain")
            for b in range(NB):
                dve.sem_inc(bank_free[b], 1)
            dve.sem_inc(S["layer_done"], 1)
            dve.sem_inc(S["xg_full"], 1)
            dve.sem_inc(S["o_full"], 1)
            dve.sem_inc(S["yacc_ready"], 1)

            steps = [0]

            def once(ins):
                steps[0] += 1
                ins.then_inc(setup_chain, 1)
                dve.wait_ge(setup_chain, steps[0])

            dve.wait_ge(setup, 1)
            dve.wait_ge(csig, 1)
            for k in range(KD):
                once(dve.tensor_scalar(c_rep[:, k, :], ones[:, 0:32], c_col[:, k:k + 1], None, ALU.mult))
            dve.sem_inc(setup, 1)
            dve.wait_ge(fixed_loaded, 16)
            dve.wait_ge(pos_loaded, 16)
            pos_f, ang, turns = (obT[:, n, :] for n in (1, 2, 3))
            once(dve.tensor_copy(pos_f, obT[:, 0, :].bitcast(I32)))
            once(dve.tensor_scalar(ang, pos_f, invf, None, ALU.mult))
            near = 1.5 * 2 ** 23
            c1 = 6.28125
            c2 = float(np.float32(2 * np.pi - c1))
            c2 = float(np.frombuffer((np.frombuffer(np.float32(c2).tobytes(), np.uint32) & 0xFFFFF000).tobytes(),
                                     np.float32)[0])
            c3 = float(np.float32(2 * np.pi - c1 - c2))
            for dst, quarter in ((sinT, 0.0), (cosT, 0.25)):
                once(dve.tensor_scalar(turns, ang, 1 / (2 * np.pi), quarter, ALU.mult, ALU.add))
                once(dve.tensor_scalar(turns, turns, near, near, ALU.add, ALU.subtract))
                once(dve.scalar_tensor_tensor(out=dst[:, :], in0=turns, scalar=-c1, in1=ang, op0=ALU.mult, op1=ALU.add))
                once(dve.scalar_tensor_tensor(out=dst[:, :], in0=turns, scalar=-c2, in1=dst[:, :], op0=ALU.mult,
                                              op1=ALU.add))
                once(dve.scalar_tensor_tensor(out=dst[:, :], in0=turns, scalar=-c3, in1=dst[:, :], op0=ALU.mult,
                                              op1=ALU.add))
                if quarter:
                    once(dve.tensor_scalar(dst[:, :], dst[:, :], np.pi / 2, None, ALU.add))
                pi = float(np.nextafter(np.float32(np.pi), np.float32(0)))
                once(dve.tensor_scalar(dst[:, :], dst[:, :], -pi, pi, ALU.max, ALU.min))
            dve.sem_inc(angles, 1)
            dve.wait_ge(sincos, 1)
            once(dve.tensor_scalar(sinT[:, :], sinT[:, :], rsign, None, ALU.mult))

            dve.wait_ge(x_loaded, 32)
            dve.sem_inc(S["x_ready"], TT)

            with dve.Fori(0, depth) as l:
                link = lambda ins: chain.link(l, ins)

                roots = [0]

                def root(c0, c1):
                    m, r0, t, r = (b[:, c0:c1] for b in (ms, rs0, rt1, rs))
                    dve.sem_inc(S["ms_ready"], 1)
                    roots[0] += 1
                    dve.wait_ge(*at(l, "rsq_raw", roots[0]))
                    link(dve.tensor_tensor(t, m, r0, ALU.mult))
                    link(dve.scalar_tensor_tensor(out=t, in0=t, scalar=-0.5, in1=r0, op0=ALU.mult, op1=ALU.mult))
                    link(dve.scalar_tensor_tensor(out=r, in0=t, scalar=1.5, in1=r0, op0=ALU.add, op1=ALU.mult))

                def row_root(i, count, w, halves):
                    dve.wait_ge(*at(l, "squared", count))
                    if halves:
                        link(dve.tensor_tensor(ssq[:, i, 0:1], ssq[:, i, 0:1], ssq[:, i, 1:2], ALU.add))
                    link(dve.tensor_scalar(ms[:, i:i + 1], ssq[:, i, 0:1], 1.0 / w, EPS, ALU.mult, ALU.add))
                    root(i, i + 1)

                def prenorm_root(i, count):
                    row_root(i, count, D, False)
                    dve.sem_inc(S["rms_ready"], 1)

                def modulated(n, units):
                    for m in range(4):
                        unit = (units, m)
                        dve.wait_ge(*full(l, unit))
                        for kk in range(2):
                            k = 2 * m + kk
                            ins = dve.tensor_scalar(hT[:, k, :], bank(unit)[:, kk * SEQ:(kk + 1) * SEQ],
                                                    modc[:, 2 * n + 1, k:k + 1], modc[:, 2 * n, k:k + 1],
                                                    ALU.mult, ALU.add)
                        link(ins)
                        dve.sem_inc(S["hT_ready"], 1)
                        dve.sem_inc(freed(unit), 1)

                def postnorm(n, i, count, banks, frees):
                    row_root(i, count, D, True)
                    for hf in range(2):
                        half = slice(hf * 512, hf * 512 + 512)
                        link(dve.scalar_tensor_tensor(out=dx[:, i, half], in0=banks[hf][:, :], scalar=rs[:, i:i + 1],
                                                      in1=gtg[:, n, half], op0=ALU.mult, op1=ALU.mult))
                        if frees:
                            dve.sem_inc(frees[hf], 1)
                    link(dve.tensor_tensor(x_sb[:, i, :], x_sb[:, i, :], dx[:, i, :], ALU.add))
                    dve.sem_inc(S["x_ready"], 1)

                def mod_in(n):
                    v = {0: 0, 2: 1, 6: 2, 8: 3}[n]
                    dve.wait_ge(*full(l, ("mod", n)))
                    link(dve.tensor_tensor(modc[:, v, :], bank(("mod", n))[:, 0:KD], adabc[:, v, :], ALU.add))
                    dve.sem_inc(freed(("mod", n)), 1)
                    if v % 2:
                        link(dve.scalar_tensor_tensor(out=modc[:, v, :], in0=modc[:, v, :], scalar=1.0,
                                                      in1=gpre[:, v // 2, :], op0=ALU.add, op1=ALU.mult))

                def gate_in(n):
                    g, half = n // 6, slice(512 * (n % 2), 512 * (n % 2) + 512)
                    dve.wait_ge(*full(l, ("gt", n)))
                    link(dve.tensor_tensor(gtg[:, g, half], bank(("gt", n))[:, :], gpost[:, half], ALU.mult))
                    dve.sem_inc(freed(("gt", n)), 1)

                def rope(n, unit, blocks):
                    b = bank(unit)
                    dve.wait_ge(*full(l, unit))
                    if n >= 2:
                        dve.wait_ge(*at(l, "roped", n - 1))
                    for q in range(4):
                        o = 32 * (q ^ 1)
                        for a in range(blocks):
                            dve.tensor_tensor(rp[32 * q:32 * q + 32, n % 2, 0, a * SEQ:(a + 1) * SEQ],
                                              b[o:o + 32, a * SEQ:(a + 1) * SEQ], sinT[32 * q:32 * q + 32, :],
                                              ALU.mult)
                    for a in range(blocks):
                        ins = dve.tensor_tensor(rp[:, n % 2, 1, a * SEQ:(a + 1) * SEQ], b[:, a * SEQ:(a + 1) * SEQ],
                                                cosT[:, :], ALU.mult)
                    link(ins)
                    dve.sem_inc(S["rope_mul"], 1)
                    if unit != ("kv",):
                        dve.sem_inc(freed(unit), 1)

                for i in range(TT):
                    prenorm_root(i, i + 1)
                dve.wait_ge(*at(l, "params", 9 * 16))
                mod_in(0)
                mod_in(2)
                modulated(0, "xT")

                dve.wait_ge(*at(l, "ckv_copied", 1))
                for i in range(TT):
                    row_root(i, TT + i + 1, KVL, False)
                for i in range(TT):
                    ins = dve.tensor_scalar(ckv_s[:, i, :], ckv_s[:, i, :], rs[:, i:i + 1], None, ALU.mult)
                link(ins)
                dve.sem_inc(S["ckv_scaled"], 1)
                rope(0, ("iq",), 2)
                rope(1, ("ik",), 1)
                rope(2, ("qa", 0), 2)
                rope(3, ("qa", 1), 2)
                dve.wait_ge(*at(l, "decay", 32))
                dve.wait_ge(*full(l, ("ckvT",)))
                for b in range(2):
                    link(dve.tensor_scalar(ckvT[:, b, :], bank(("ckvT",))[:, b * SEQ:(b + 1) * SEQ], gkv_c[:, b:b + 1],
                                           None, ALU.mult))
                dve.sem_inc(S["ckvT_ready"], 1)
                dve.sem_inc(freed(("ckvT",)), 1)
                rope(4, ("kv",), 1)
                link(dve.tensor_copy(vA[:, :, :], bank(("kv",))[:, SEQ:SEQ + TT * HD].rearrange("p (i n) -> p i n", i=TT)))
                dve.sem_inc(S["vA_ready"], 1)
                dve.sem_inc(freed(("kv",)), 1)

                dve.wait_ge(*at(l, "iw_ready", 1))
                n = 0
                for i in range(TT):
                    w = P * (i + 1)
                    score = selb[:, i, 0:w]
                    for h in range(IDXH):
                        dve.wait_ge(*at(l, "relu_ready", n + 1))
                        link(dve.scalar_tensor_tensor(out=score, in0=lr[:, n % 4, 0:w],
                                                      scalar=iw_s[:, i, h:h + 1],
                                                      in1=adm[:, i, 0:w] if h == 0 else score,
                                                      op0=ALU.mult, op1=ALU.add))
                        dve.sem_inc(S["lg_used"], 1)
                        n += 1
                    for _ in range(TOPK // 8):
                        apart(dve)
                        link(dve.max(top8[:, :], score))
                        apart(dve)
                        link(dve.match_replace(score, top8[:, :], score, GONE))
                    link(dve.tensor_scalar(score, score, GONE_T, -1.0, ALU.is_le, ALU.add))
                    link(dve.tensor_scalar(score, score, BIG, None, ALU.mult))
                    dve.sem_inc(S["sel_ready"], 1)
                for n, (name, m) in enumerate((("qc", 0), ("qc", 1), ("kc", 0), ("kc", 1))):
                    rope(5 + n, (name, m), 2)

                for n in range(NH + 1):
                    if n < NH:
                        dve.wait_ge(*at(l, "ln_ready", n + 1))
                        z, e = zs[:, n % 2, :], ln[:, n % 2, :]
                        link(dve.scalar_tensor_tensor(out=e, in0=z, scalar=0.0, in1=e, op0=ALU.max, op1=ALU.add))
                        dve.tensor_tensor(e, e, cm01, ALU.mult).then_inc(S["sp_ready"], 1)
                    if n >= 1:
                        h = n - 1
                        dve.wait_ge(*full(l, ("cum", h)))
                        dve.wait_ge(*at(l, "zb_ready", h + 1))
                        link(dve.scalar_tensor_tensor(out=aw[:, h % 4, :], in0=bank(("cum", h))[:, 0:TRI], scalar=-1.0,
                                                      in1=aw[:, h % 4, :], op0=ALU.mult, op1=ALU.add))
                        dve.sem_inc(S["w_ready"], 1)
                        dve.sem_inc(freed(("cum", h)), 1)

                dve.wait_ge(*full(l, ("ob", PAIRS - 1)))
                for n in range(2 * NH + 1):
                    if n < 2 * NH:
                        i = n // NH
                        w = P * (i + 1)
                        dve.wait_ge(*full(l, ("sc", n)))
                        if n >= 3:
                            dve.wait_ge(*full(l, ("pT", n - 3)))
                        link(dve.scalar_tensor_tensor(out=sm[:, n % 3, 0:w], in0=bank(("sc", n))[:, 0:w],
                                                      scalar=HD ** -0.5, in1=selb[:, i, 0:w], op0=ALU.mult,
                                                      op1=ALU.add))
                        dve.sem_inc(freed(("sc", n)), 1)
                        dve.tensor_reduce(nmx[:, n % 3:n % 3 + 1], sm[:, n % 3, 0:w], AX, ALU.max, negate=True)\
                           .then_inc(S["sm_ready"], 1)
                    if n >= 1:
                        m = (n - 1) % 3
                        dve.wait_ge(*at(l, "p_ready", n))
                        dve.reciprocal(rinv[:, m:m + 1], rsum[:, m:m + 1]).then_inc(S["rinv_ready"], 1)

                dve.wait_ge(*full(l, ("oa", 2 * PAIRS - 1)))
                for n in range(NH + 1):
                    if n < NH:
                        dve.wait_ge(*full(l, ("ret", n)))
                        link(dve.tensor_tensor(rw[:, n % 2, :], bank(("ret", n))[:, 0:TRI], dec[:, n, :], ALU.mult))
                        dve.sem_inc(S["rw_ready"], 1)
                        dve.sem_inc(freed(("ret", n)), 1)
                    if n >= 1:
                        h = n - 1
                        dve.wait_ge(*at(l, "osb_ready", n))
                        for i in range(TT):
                            ins = dve.bn_stats(bst[:, i * NH + h, :], rows[:, i, h * CV:(h + 1) * CV])
                        link(ins)
                        apart(dve)
                        for i in range(TT):
                            ins = dve.bn_aggr(mv[:, i * NH + h, :], bst[:, i * NH + h, :])
                link(ins)
                link(dve.tensor_scalar(ms[:, 0:TT * NH], mv[:, :, 1], EPS, None, ALU.add))
                root(0, TT * NH)
                for i in range(TT):
                    for h in range(NH):
                        m = i * NH + h
                        ins = dve.tensor_scalar(rows[:, i, h * CV:(h + 1) * CV], rows[:, i, h * CV:(h + 1) * CV],
                                                mv[:, m, 0:1], rs[:, m:m + 1], ALU.subtract, ALU.mult)
                    link(ins)
                    if i == 0:
                        dve.sem_inc(S["ocn_ready"], 1)
                dve.wait_ge(*at(l, "gc_ready", 4))
                dve.tensor_tensor(rows[:, 1, :], rows[:, 1, :], gcs[:, 1, :], ALU.mult).then_inc(S["ocg_ready"], 1)

                dve.wait_ge(*at(l, "gate_ready", 12))

                def gated_ab(j):
                    if j >= 2:
                        dve.wait_ge(*at(l, "mT_begun", j - 1))
                    dve.wait_ge(*full(l, ("yab", j)))
                    link(dve.tensor_tensor(tab[:, j % 2], bank(("yab", j))[:, :].rearrange("p (a n) -> p a n", a=2),
                                           gT[:, j:j + 9:8, :], ALU.mult))
                    dve.sem_inc(S["tab_ready"], 1)
                    dve.sem_inc(freed(("yab", j)), 1)

                def gated_c(j):
                    if j >= 2:
                        dve.wait_ge(*at(l, "mT_ready", j - 1))
                    dve.wait_ge(*full(l, ("yc", j)))
                    link(dve.tensor_tensor(tc[:, j % 2, :], bank(("yc", j))[:, 0:SEQ], gT[:, 16 + j, :], ALU.mult))
                    dve.sem_inc(S["tc_ready"], 1)
                    dve.sem_inc(freed(("yc", j)), 1)

                for j in range(4):
                    gated_ab(j)
                dve.wait_ge(*at(l, "gate_params", 5 * 16))
                gate_in(4)
                gate_in(5)
                dve.sem_inc(S["gtg_ready"], 1)
                mod_in(6)
                mod_in(8)
                for j in range(4):
                    gated_c(j)
                for j in range(4, KD):
                    gated_ab(j)
                for j in range(4, KD):
                    gated_c(j)

                for i in range(TT):
                    postnorm(0, i, 6 + 3 * i, [bank(("y", i, hf)) for hf in range(2)],
                             [freed(("y", i, hf)) for hf in range(2)])
                    prenorm_root(i, 7 + 3 * i)
                modulated(1, "hT")
                dve.wait_ge(*at(l, "ffn_params", 16))
                gate_in(10)
                gate_in(11)

                def shared_hidden(i):
                    dve.wait_ge(*at(l, "sh_silu", i + 1))
                    dve.tensor_tensor(dhid, dsl, psums[3][:, ED:2 * ED], ALU.mult).then_inc(S["sh_hid"], 1)

                dve.wait_ge(*at(l, "scores_ready", 1))
                groups = lambda v: v.rearrange("p i (g e) -> p i g e", g=NG)
                link(dve.tensor_tensor(rsel[:, :, :], rsc[:, :, :], rbias[:, :].unsqueeze(1).to_broadcast([P, TT, NE]),
                                       ALU.add))
                apart(dve)
                for i in range(TT):
                    for g in range(NG):
                        ins = dve.max(g8[:, i, g, :], rsel[:, i, g * EG:(g + 1) * EG])
                link(ins)
                link(dve.tensor_tensor(gsc[:, :, :], g8[:, :, :, 0], g8[:, :, :, 1], ALU.add))
                apart(dve)
                for i in range(TT):
                    ins = dve.max(t8[:, i, :], gsc[:, i, :])
                link(ins)
                link(dve.memset(t8[:, :, TOPG:8], 2 * GONE_T / 3))
                apart(dve)
                for i in range(TT):
                    ins = dve.match_replace(gsc[:, i, :], t8[:, i, :], gsc[:, i, :], GONE)
                link(ins)
                link(dve.tensor_scalar(gsc[:, :, :], gsc[:, :, :], GONE_T, -1.0, ALU.is_le, ALU.add))
                link(dve.tensor_scalar(gsc[:, :, :], gsc[:, :, :], BIG, None, ALU.mult))
                link(dve.tensor_tensor(groups(rsel[:, :, :]), groups(rsel[:, :, :]),
                                       gsc[:, :, :].unsqueeze(3).to_broadcast([P, TT, NG, EG]), ALU.add))
                shared_hidden(0)
                apart(dve)
                for i in range(TT):
                    ins = dve.max(t8[:, i, :], rsel[:, i, :])
                link(ins)
                apart(dve)
                for i in range(TT):
                    ins = dve.match_replace(rsel[:, i, :], t8[:, i, :], rsel[:, i, :], GONE)
                link(ins)
                link(dve.tensor_scalar(rsel[:, :, :], rsel[:, :, :], GONE_T, None, ALU.is_le))
                dve.sem_inc(S["mask_ready"], 1)
                for i in range(TT):
                    ins = dve.tensor_tensor_reduce(rwk[:, i, :], rsel[:, i, :], rsc[:, i, :], 1.0, 0.0, ALU.mult,
                                                   ALU.add, part[:, i:i + 1])
                link(ins)
                link(dve.reciprocal(part[:, 2:2 + TT], part[:, 0:TT]))
                for i in range(TT):
                    ins = dve.tensor_scalar(gate[:, i, :], rwk[:, i, :], part[:, 2 + i:3 + i], ROUTED_SCALE,
                                            ALU.mult, ALU.mult)
                link(ins)
                shared_hidden(1)

                dve.wait_ge(*at(l, "rank_full", 1))
                b = psums[0][:, 0:TT * NE].rearrange("p (i e) -> p i e", i=TT)
                link(dve.tensor_scalar(over[:, :, :], b, float(SLOTS), None, ALU.is_ge))
                link(dve.tensor_tensor(over, over, rsel[:, :, :], ALU.mult))
                dve.sem_inc(S["over_ready"], 1)
                link(dve.scalar_tensor_tensor(out=rank[:, :, :], in0=b, scalar=UNPICKED, in1=rsel[:, :, :], op0=ALU.add,
                                              op1=ALU.mult))
                link(dve.tensor_scalar(rank[:, :, :], rank[:, :, :], UNPICKED, None, ALU.subtract))
                link(dve.tensor_tensor(gate_over[:, :, 0:NE], gate[:, :, :], over[:, :, :], ALU.mult))

                dve.wait_ge(*at(l, "over_full", 1))
                fl = flags
                link(dve.tensor_scalar(fl.rearrange("p (e i) -> p i e", i=TT),
                                       psums[1][0:1, 0:TT * NE].rearrange("p (i e) -> p i e", i=TT),
                                       1.0, None, ALU.min))
                link(dve.tensor_reduce(pair_f, fl.rearrange("p (n f) -> p n f", f=2 * TT), AX, ALU.add))
                link(dve.tensor_copy(pair_any, pair_f))
                link(dve.tensor_tensor_scan(steps_f[:, :], flags[:, :], flags[:, :], steps_done[:, :], ALU.add,
                                            ALU.max))
                link(dve.tensor_tensor(steps_n[:, :], steps_f[:, :], flags[:, :], ALU.mult))
                link(dve.tensor_copy(steps_done[:, :], steps_f[:, NT - 1:NT]))
                dve.sem_inc(S["table_ready"], 1)

                q0 = l * NP

                def build_selection(pair, s):
                    shape = [P, TT, 2, SLOTS]
                    hot = picks[:, s].rearrange("p i (x n) -> p i x n", x=2)
                    r = rank[:, :, bass.ds(2 * pair, 2)].unsqueeze(3).to_broadcast(shape)
                    g = gate[:, :, bass.ds(2 * pair, 2)].unsqueeze(3).to_broadcast(shape)
                    numbers = slot_no.unsqueeze(1).unsqueeze(1).to_broadcast(shape)
                    dve.tensor_tensor(hot, numbers, r, ALU.is_equal).then_inc(S["hot_built"], 1)
                    dve.wait_ge(S["hot_built"], q0 + pair + 1)
                    dve.tensor_tensor(selw[:, s].rearrange("p i (x n) -> p i x n", x=2), hot, g, ALU.mult)\
                       .then_inc(S["sel_built"], 1)

                def gathered(q):
                    dve.wait_ge(S["xg_full"], q + 2)
                    for k in range(4):
                        ins = dve.tensor_scalar(xg[:, k, :], psums[0][:, k * P:(k + 1) * P], modc[:, 3, k:k + 1],
                                                modc[:, 2, k:k + 1], ALU.mult, ALU.add)
                    ins.then_inc(S["xg0_ready"], 1)

                def hidden(q):
                    dve.wait_ge(S["silu_ready"], q + 1)
                    dve.tensor_tensor(hid, esl, psums[2][:, ED:2 * ED], ALU.mult).then_inc(S["hid_ready"], 1)

                def dense(v, e, ex, i):
                    dve.wait_ge(D_silu, v)
                    dve.scalar_tensor_tensor(out=dhid, in0=dsl, scalar=gate_over[:, i, bass.ds(e, 1)],
                                             in1=psums[3][:, ED:2 * ED], op0=ALU.mult, op1=ALU.mult)\
                       .then_inc(D_hid, 1)

                def pair_step(pair, s, ahead, build):
                    q = q0 + pair
                    if ahead:
                        gathered(q + 1)
                    dve.wait_ge(S["turned"], q + 1)
                    dve.tensor_copy(flat(selT[:, s]), psums[2][:, 0:ED]).then_inc(S["selT_ready"], 1)
                    if build:
                        build_selection(pair + 2, s)
                    dve.wait_ge(S["o_full"], q + 2)
                    dve.tensor_copy(og[:, 0:512], psums[0][:, :]).then_inc(S["o0_ready"], 1)
                    if ahead:
                        hidden(q + 1)
                        dense_steps(dve, pair + 1, dense)

                build_selection(0, 0)
                build_selection(1, 1)
                gathered(q0)
                hidden(q0)
                dense_steps(dve, 0, dense)
                with dve.Fori(0, NP // 2 - 1) as r:
                    pair_step(2 * r, 0, True, True)
                    pair_step(2 * r + 1, 1, True, True)
                pair_step(NP - 2, 0, True, False)
                pair_step(NP - 1, 1, False, False)
                for i in range(TT):
                    postnorm(1, i, 12 + 2 * i, [psums[4 + 2 * i + hf] for hf in range(2)], None)
                dve.sem_inc(S["layer_done"], 1)
            assert chain.n == TOTAL["vector_chain"], chain.n

        @block.tensor
        def _(pe):
            mm = pe.matmul
            pe.wait_ge(setup, 2)
            pe.wait_ge(fixed_loaded, 16)

            with pe.Fori(0, depth) as l:
                order = [0]
                used = [0]

                def take(*unit):
                    u = order[0]
                    assert UNITS[u] == unit, (UNITS[u], unit)
                    order[0] += 1
                    pe.wait_ge(bank_free[u % NB], l * USES[u % NB] + u // NB + 1)
                    return psums[u % NB]

                def chunk_in(n):
                    pe.wait_ge(slot_full[n % NS], l * (NCH // NS * 32) + 32 * (n // NS + 1))
                    return wring[:, n % NS]

                def chunk_out(ins):
                    used[0] += 1
                    pe.sem_inc(S["chunk_used"], 1)

                def ada(n, c):
                    b = take("ada", n)
                    w = chunk_in(c)
                    for k in range(KD):
                        j = k % 4
                        ins = mm(b[32 * j:32 * j + 32, :], c_rep[:, k, :], w[:, k, :], start=(k < 4), stop=(k >= 4),
                                 tile_position=(0, 32 * j))
                    ins.then_inc(S["bank_full"], 1)
                    pe.wait_ge(S["bank_full"], l * NU + order[0])
                    pe.sem_inc(S["chunk_used"], 1)

                def mod_columns(n):
                    b = take("mod", n)
                    for hf in range(2):
                        pe.wait_ge(*at(l, "ada_copied", n + hf + 1))
                        for k in range(KD):
                            ins = mm(b[64 * hf:64 * hf + 64, k:k + 1], adaS[n + hf][:, k:512:KD], ones32[:, 0:1],
                                     start=True, stop=True)
                    ins.then_inc(S["bank_full"], 1)

                def gate_rows(n):
                    b = take("gt", n)
                    pe.wait_ge(*at(l, "ada_copied", n + 1))
                    pe.wait_ge(*at(l, "gate_params", 5 * 16))
                    mm(b[:, :], ones32[:, :], adaS[n], start=True, stop=False)
                    mm(b[:, :], ones[0:1, :], gtb[n], start=False, stop=True)\
                        .then_inc(S["bank_full"], 1)

                for n in range(3):
                    ada(n, n)
                mod_columns(0)
                pe.wait_ge(S["layer_done"], l + 1)
                ada(3, 3)

                def transposes(unit, i_ready):
                    for m in range(4):
                        b = take(unit, m)
                        if m == 0:
                            for name, count in i_ready:
                                pe.wait_ge(*at(l, name, count))
                        for kk in range(2):
                            for i in range(TT):
                                ins = pe.transpose(b[:, kk * SEQ + i * P:kk * SEQ + (i + 1) * P],
                                                   rows[:, i, 2 * m + kk:D:KD], ident)
                        ins.then_inc(S["bank_full"], 1)

                transposes("xT", [("xn_ready", 2)])
                mod_columns(2)
                pe.wait_ge(*at(l, "hT_ready", 4))

                def project_T(unit, w, cols, blocks, at_col=0):
                    b = take(*unit)
                    for a in range(blocks):
                        for k in range(KD):
                            ins = mm(b[:, at_col + a * SEQ:at_col + (a + 1) * SEQ], w[:, k, cols + a * P:cols + (a + 1) * P],
                                     hT[:, k, :], start=(k == 0), stop=(k == KD - 1))
                    ins.then_inc(S["bank_full"], 1)

                def project(b, at_col, w, cols, width, i):
                    for k in range(KD):
                        ins = mm(b[:, at_col:at_col + width], hT[:, k, i * P:(i + 1) * P], w[:, k, cols:cols + width],
                                 start=(k == 0), stop=(k == KD - 1))
                    return ins

                def chunk_done():
                    pe.wait_ge(S["bank_full"], l * NU + order[0])
                    pe.sem_inc(S["chunk_used"], 1)

                c = ADA_LATER
                w = chunk_in(c)
                b = take("ckv")
                for i in range(TT):
                    ins = project(b, i * KVL, w, 0, KVL, i)
                ins.then_inc(S["bank_full"], 1)
                chunk_done()
                c += 1
                w = chunk_in(c)
                project_T(("iq",), w, 0, 2)
                b = take("ik")
                for k in range(KD):
                    for hf in range(2):
                        ins = mm(b[64 * hf:64 * hf + 64, 0:SEQ], w[:, k, 256:320], hT[:, k, :], start=(k == 0),
                                 stop=(k == KD - 1))
                ins.then_inc(S["bank_full"], 1)
                b = take("iw")
                for i in range(TT):
                    ins = project(b, i * IDXH, w, 320, IDXH, i)
                ins.then_inc(S["bank_full"], 1)
                chunk_done()
                c += 1
                w = chunk_in(c)
                project_T(("qa", 0), w, 0, 2)
                project_T(("qa", 1), w, 256, 2)
                chunk_done()
                c += 1
                b = take("ckvT")
                pe.wait_ge(*at(l, "ckv_scaled", 1))
                for a in range(2):
                    for i in range(TT):
                        ins = pe.transpose(b[:, a * SEQ + i * P:a * SEQ + (i + 1) * P], ckv_s[:, i, a * P:(a + 1) * P],
                                           ident)
                ins.then_inc(S["bank_full"], 1)
                b = take("kv")
                pe.wait_ge(*at(l, "ckvT_ready", 1))
                for a in range(2):
                    for hf in range(2):
                        mm(b[64 * hf:64 * hf + 64, 0:SEQ], wuk[:, a, :], ckvT[:, a, :], start=(a == 0), stop=(a == 1))
                for i in range(TT):
                    for a in range(2):
                        ins = mm(b[:, SEQ + i * HD:SEQ + (i + 1) * HD], ckvT[:, a, i * P:(i + 1) * P], wuv[:, a, :],
                                 start=(a == 0), stop=(a == 1))
                ins.then_inc(S["bank_full"], 1)
                pe.wait_ge(*at(l, "roped", 2))
                for i in range(TT):
                    for h in range(IDXH):
                        b = take("lg", i, h)
                        r = slice(64 * (h % 2), 64 * (h % 2) + 64)
                        mm(b[:, 0:P * (i + 1)], iqT[r, h // 2, i * P:(i + 1) * P], ikT[r, 0:P * (i + 1)], start=True,
                           stop=True).then_inc(S["bank_full"], 1)
                for name in ("qb", "kb"):
                    w = chunk_in(c)
                    project_T((name, 0), w, 0, 2)
                    project_T((name, 1), w, 256, 2)
                    chunk_done()
                    c += 1
                w = chunk_in(c)
                for i in range(TT):
                    b = take("vb", i)
                    project(b, 0, w, 0, 512, i).then_inc(S["bank_full"], 1)
                chunk_done()
                c += 1
                for name in ("qc", "kc"):
                    w = chunk_in(c)
                    project_T((name, 0), w, 0, 2)
                    project_T((name, 1), w, 256, 2)
                    chunk_done()
                    c += 1

                def head_rows(h):
                    return slice(64 * (h % 2), 64 * (h % 2) + 64)

                def key_query(b, kk, qq, h):
                    r, hb = head_rows(h), h // 2
                    mm(b[:, 0:SEQ], kk[r, hb, 0:P], qq[r, hb, :], start=True, stop=True)
                    return mm(b[:, SEQ:TRI], kk[r, hb, P:SEQ], qq[r, hb, P:SEQ], start=True, stop=True)

                pe.wait_ge(*at(l, "qkb_ready", 4))
                for n in range(NH + 2):
                    if n < NH:
                        b = take("z", n)
                        key_query(b, kbT, qbT, n).then_inc(S["bank_full"], 1)
                    if 1 <= n < NH + 1:
                        h = n - 1
                        b = take("cum", h)
                        pe.wait_ge(*at(l, "sp_ready", h + 1))
                        e = ln[:, h % 2, :]
                        mm(b[:, 0:SEQ], later, e[:, 0:SEQ], start=True, stop=False)
                        mm(b[:, P:SEQ], ones[:, :], e[:, SEQ:TRI], start=False, stop=True)
                        mm(b[:, SEQ:TRI], later, e[:, SEQ:TRI], start=True, stop=True).then_inc(S["bank_full"], 1)
                    if n >= 3 and n % 2 == 1:
                        m = (n - 3) // 2
                        b = take("ob", m)
                        if m == 0:
                            pe.wait_ge(*at(l, "vb_ready", 2))
                        for h in (2 * m, 2 * m + 1):
                            pe.wait_ge(*at(l, "a_ready", h + 1))
                            a = aw[:, h % 4, :]
                            r = head_rows(h)
                            mm(b[r, 0:SEQ], vb_s[:, 0, h * HD:(h + 1) * HD], a[:, 0:SEQ], start=True, stop=False)
                            ins = mm(b[r, P:SEQ], vb_s[:, 1, h * HD:(h + 1) * HD], a[:, SEQ:TRI], start=False, stop=True)
                        ins.then_inc(S["bank_full"], 1)
                    if n < 4:
                        if n % 2 == 0:
                            w = chunk_in(c)
                        b = take("vc", n)
                        project(b, 0, w, 0, 512, n % 2).then_inc(S["bank_full"], 1)
                    elif n < 8:
                        if n % 2 == 0:
                            w = chunk_in(c)
                        b = take("gc", n - 4)
                        project(b, 0, w, 0, 512, n % 2).then_inc(S["bank_full"], 1)
                    if n < 8 and n % 2:
                        chunk_done()
                        c += 1

                for n in range(2 * NH + 3):
                    if n < 2 * NH:
                        i, h = n // NH, n % NH
                        b = take("sc", n)
                        if n == 0:
                            pe.wait_ge(*at(l, "roped", 5))
                        r = head_rows(h)
                        mm(b[:, 0:P * (i + 1)], qaT[r, h // 2, i * P:(i + 1) * P], kT[r, 0:P * (i + 1)], start=True,
                           stop=True).then_inc(S["bank_full"], 1)
                    if 2 <= n < 2 * NH + 2:
                        m = n - 2
                        b = take("pT", m)
                        pe.wait_ge(*at(l, "pn_ready", m + 1))
                        for a in range(m // NH + 1):
                            ins = pe.transpose(b[:, a * P:(a + 1) * P], sm[:, m % 3, a * P:(a + 1) * P], ident)
                        ins.then_inc(S["bank_full"], 1)
                    if n >= 4 and n % 2 == 0:
                        o = (n - 4) // 2
                        i = o // PAIRS
                        b = take("oa", o)
                        if o == 0:
                            pe.wait_ge(*at(l, "vA_ready", 1))
                        for m in (2 * o, 2 * o + 1):
                            pe.wait_ge(*at(l, "pTs_ready", m + 1))
                            for a in range(i + 1):
                                ins = mm(b[head_rows(m), 0:P], vA[:, a, :], pTs[:, m % 4, a * P:(a + 1) * P],
                                         start=(a == 0), stop=(a == i))
                        ins.then_inc(S["bank_full"], 1)
                    if n < 12:
                        if n % 2 == 0:
                            w = chunk_in(c)
                        project_T(("gate", n), w, 256 * (n % 2), 2)
                        if n % 2:
                            chunk_done()
                            c += 1
                    elif n in (14, 16):
                        ada(n // 2 - 3, c)
                        c += 1

                pe.wait_ge(*at(l, "roped", 9))
                pe.wait_ge(*at(l, "vc_ready", 4))
                for n in range(NH + 1):
                    if n < NH:
                        b = take("ret", n)
                        key_query(b, kcT, qcT, n).then_inc(S["bank_full"], 1)
                    if n >= 1:
                        h = n - 1
                        b = take("oc", h)
                        pe.wait_ge(*at(l, "rw_ready", h + 1))
                        s = rw[:, h % 2, :]
                        v0, v1 = (vc_s[:, i, h * CV:(h + 1) * CV] for i in range(TT))
                        mm(b[:, 0:CV], s[:, 0:P], v0, start=True, stop=True)
                        mm(b[:, CV:2 * CV], s[:, P:SEQ], v0, start=True, stop=False)
                        mm(b[:, CV:2 * CV], s[:, SEQ:TRI], v1, start=False, stop=True).then_inc(S["bank_full"], 1)
                pe.wait_ge(*at(l, "oa_ready", 8))
                pe.wait_ge(*at(l, "ob_ready", 4))

                def out_ab(j0):
                    w = chunk_in(c)
                    for j in range(j0, j0 + 4):
                        cols = slice(P * (j % 4), P * (j % 4) + P)
                        b = take("yab", j)
                        for a, src in enumerate((oaT, obT)):
                            for k in range(4):
                                ins = mm(b[:, a * SEQ:(a + 1) * SEQ], w[:, 4 * a + k, cols], src[:, k, :],
                                         start=(k == 0), stop=(k == 3))
                        ins.then_inc(S["bank_full"], 1)
                    chunk_done()

                def out_c(j0):
                    w = chunk_in(c)
                    for j in range(j0, j0 + 4):
                        cols = slice(P * (j % 4), P * (j % 4) + P)
                        b = take("yc", j)
                        for k in range(KD):
                            ins = mm(b[:, 0:SEQ], w[:, k, cols], ocT(k), start=(k == 0), stop=(k == KD - 1))
                        ins.then_inc(S["bank_full"], 1)
                    chunk_done()

                out_ab(0)
                c += 1
                gate_rows(4)
                gate_rows(5)
                for n in (6, 8):
                    ada(n, c)
                    ada(n + 1, c + 1)
                    c += 2
                    mod_columns(n)
                transposes("ocT", [("ocg_ready", 2)])
                pe.wait_ge(*at(l, "ocT_ready", 4))
                out_c(0)
                c += 1
                out_ab(4)
                c += 1
                out_c(4)
                c += 1
                pe.wait_ge(*at(l, "mT_ready", 8))
                for i in range(TT):
                    for hf in range(2):
                        w = chunk_in(c + hf)
                        b = take("y", i, hf)
                        for j in range(KD):
                            ins = mm(b[:, :], mT(j)[:, i * P:(i + 1) * P], w[:, j, :], start=(j == 0), stop=(j == KD - 1))
                        ins.then_inc(S["bank_full"], 1)
                        if i == TT - 1:
                            chunk_done()
                ada(10, c + 2)
                ada(11, c + 3)
                c += 4
                gate_rows(10)
                gate_rows(11)
                assert c == NCH
                transposes("hT", [("xn_ready", 4)])
                pe.wait_ge(*at(l, "hT_ready", 8))
                b = take("rt")
                for i in range(TT):
                    for k in range(KD):
                        ins = mm(b[:, i * NE:(i + 1) * NE], hT[:, k, i * P:(i + 1) * P], wrt[:, k, :], start=(k == 0),
                                 stop=(k == KD - 1))
                ins.then_inc(S["bank_full"], 1)
                assert order[0] == NU

                for b in range(NB):
                    pe.wait_ge(bank_free[b], l * USES[b] + USES[b] + 1)
                pe.wait_ge(shared_in, (l + 1) * 48)
                for i in range(TT):
                    for k in range(KD):
                        ins = mm(psums[3][:, :].rearrange("p (j n) -> p j n", j=2), hT[:, k, i * P:(i + 1) * P],
                                 w13[:, 3, :, k, :], start=(k == 0), stop=(k == KD - 1))
                    ins.then_inc(S["sh_h"], 1)
                    pe.wait_ge(*at(l, "sh_hid", i + 1))
                    for j in range(2):
                        ins = pe.transpose(psums[3][:, j * P:(j + 1) * P], dhid[:, j:ED:2], ident)
                    ins.then_inc(S["sh_turned"], 1)
                    pe.wait_ge(*at(l, "sh_eT", i + 1))
                    for hf in range(2):
                        for j in range(2):
                            ins = mm(psums[4 + 2 * i + hf][:, :], deT[:, j, :], w2s[:, 3, j, hf * 512:hf * 512 + 512],
                                     start=(j == 0), stop=False, skip_group_check=True)
                ins.then_inc(S["sh_done"], 1)

                b = psums[0]
                pe.wait_ge(*at(l, "mask_ready", 1))
                mm(b[:, 0:NE], earlier, rsel[:, 0, :], start=True, stop=True)
                mm(b[:, NE:2 * NE], ones[:, :], rsel[:, 0, :], start=True, stop=False)
                mm(b[:, NE:2 * NE], earlier, rsel[:, 1, :], start=False, stop=True).then_inc(S["rank_full"], 1)
                pe.wait_ge(*at(l, "over_ready", 1))
                mm(psums[1][0:1, 0:TT * NE].rearrange("p (i e) -> p i e", i=TT), ones[:, 0:1], over, start=True,
                   stop=True).then_inc(S["over_full"], 1)

                q0 = l * NP
                halves = [slice(0, SLOTS), slice(SLOTS, P)]

                def w13_in(s, turn):
                    pe.wait_ge(w13_full[s], (l * (NP // 2) + turn + 1) * 64)

                def w2_in(s, turn):
                    pe.wait_ge(w2_full[s], (l * (NP // 2) + turn + 1) * 32)

                def gather(q, s, after):
                    pe.wait_ge(S["sel_built"], q + 1)
                    for k in range(KD):
                        if k % 4 == 0 and after:
                            pe.wait_ge(S[f"o{k // 4}_ready"], q - 1)
                        for n, part3 in enumerate(xs):
                            for i in range(TT):
                                ins = mm(psums[k // 4][:, (k % 4) * P:(k % 4 + 1) * P], part3[:, i, k:D:KD], picks[:, s, i, :],
                                         start=(n == 0 and i == 0), stop=(n == 2 and i == TT - 1))
                    ins.then_inc(S["xg_full"], 1)

                def up(q, s):
                    pe.wait_ge(S["xg0_ready"], q + 1)
                    for k in range(KD):
                        if k == 4:
                            pe.wait_ge(S["xg1_ready"], q + 1)
                        for ex in range(2):
                            ins = mm(psums[2][halves[ex], :].rearrange("p (j n) -> p j n", j=2), xg[:, k, halves[ex]],
                                     w13[:, 2 * s + ex, :, k, :], start=(k == 0), stop=(k == KD - 1))
                    ins.then_inc(S["h_full"], 1)

                def turn(q, s):
                    pe.wait_ge(S["hid_ready"], q + 1)
                    for j in range(2):
                        pe.transpose(psums[3][:, j * P:(j + 1) * P], hid[:, j:ED:2], ident)
                    for i in range(TT):
                        ins = pe.transpose(psums[2][:, i * P:(i + 1) * P], selw[:, s, i, :], ident)
                    ins.then_inc(S["turned"], 1)

                def down(q, s, turn, ahead):
                    w2_in(s, turn)
                    pe.wait_ge(S["eT_ready"], q + 1)
                    for hf in range(2):
                        if ahead:
                            pe.wait_ge(S[f"xg{hf}_ready"], q + 2)
                        for j in range(2):
                            for ex in range(2):
                                ins = mm(psums[hf][halves[ex], :], eTs[:, j, halves[ex]],
                                         w2s[:, 2 * s + ex, j, hf * 512:hf * 512 + 512], start=(j == 0), stop=(j == 1))
                    ins.then_inc(S["o_full"], 1)

                def scatter(q, s, last=False):
                    pe.wait_ge(S["selT_ready"], q + 1)
                    for hf in range(2):
                        pe.wait_ge(S[f"o{hf}_ready"], q + 1)
                        for i in range(TT):
                            ins = mm(psums[4 + 2 * i + hf][:, :], selT[:, s, i, :], og[:, hf * 512:hf * 512 + 512],
                                     start=False, stop=last, skip_group_check=True)
                    return ins

                def dense_in(s, turn):
                    def step(v, e, ex, i):
                        for k in range(KD):
                            ins = mm(psums[3][:, :].rearrange("p (j n) -> p j n", j=2), hT[:, k, i * P:(i + 1) * P],
                                     w13[:, 2 * s + ex, :, k, :], start=(k == 0), stop=(k == KD - 1))
                        ins.then_inc(D_h, 1)
                        pe.wait_ge(D_hid, v)
                        for j in range(2):
                            ins = pe.transpose(psums[3][:, j * P:(j + 1) * P], dhid[:, j:ED:2], ident)
                        ins.then_inc(D_T, 1)
                        w2_in(s, turn)
                        pe.wait_ge(D_eT, v)
                        for hf in range(2):
                            for j in range(2):
                                ins = mm(psums[4 + 2 * i + hf][:, :], deT[:, j, :],
                                         w2s[:, 2 * s + ex, j, hf * 512:hf * 512 + 512], start=False,
                                         stop=False, skip_group_check=True)
                    return step

                def ahead_of(pair, s, turn):
                    w13_in(s, turn)
                    up(q0 + pair, s)
                    apart(pe)
                    dense_steps(pe, pair, dense_in(s, turn))

                def pair_step(pair, s, turn_no, first=False, ahead=True):
                    q = q0 + pair
                    t = 1 - s
                    if ahead:
                        gather(q + 1, t, not first)
                    turn(q, s)
                    if not first:
                        scatter(q - 1, t)
                    down(q, s, turn_no, ahead)
                    if ahead:
                        pe.wait_ge(S["selT_ready"], q + 1)
                        ahead_of(pair + 1, t, turn_no + s)

                pe.wait_ge(*at(l, "split_ready", 2))
                pe.wait_ge(*at(l, "table_ready", 1))
                gather(q0, 0, False)
                ahead_of(0, 0, 0)
                pair_step(0, 0, 0, first=True)
                with pe.Fori(0, NP // 2 - 1) as r:
                    pair_step(2 * r + 1, 1, r)
                    pair_step(2 * r + 2, 0, r + 1)
                pair_step(NP - 1, 1, NP // 2 - 1, ahead=False)
                scatter(q0 + NP - 1, 1, last=True).then_inc(S["yacc_ready"], 1)


_INS = ["x", "c", "positions", "ada_w", "ada_b", "g_pre_mix", "g_post_mix", "g_pre_ffn", "g_post_ffn", "w_in", "g_kv",
        "w_uk", "w_uv", "g_ret", "w_o_a", "w_o_b", "w_o_c", "w_out", "w_router", "router_bias", "w1", "w3", "w2",
        "ws1", "ws3", "ws2"]


def kernel(**inputs):
    import concourse.bacc as _bacc
    from concourse.bass_utils import run_bass_kernel_spmd as _run

    nc = _bacc.Bacc("TRN2", target_bir_lowering=False, num_devices=1)
    arrays = {name: np.ascontiguousarray(inputs[name]) for name in _INS}
    arrays["fixed"], arrays["decay"] = mixer_constants()
    args = {name: nc.dram_tensor(f"in_{name}", a.shape, mybir.dt.from_np(a.dtype), kind="ExternalInput").ap()
            for name, a in arrays.items()}
    args["out"] = nc.dram_tensor("out_0", (1, SEQ, D), F32, kind="ExternalOutput").ap()
    build(nc, **args)
    r = _run(nc, [{f"in_{name}": a for name, a in arrays.items()}], core_ids=[0])
    return r.results[0]["out_0"]
```
